# Optimizing a Trainium2 kernel written in Bass

```python
import math
import jax, jax.numpy as jnp
from jax import lax
import numpy as np

D_MODEL = 1024
BATCH = 1
SEQ = 1024
DEPTH = 1
DEC_BATCH = 8
DEC_SEQ = 8
PAST_LEN = 1024
PAGE_SIZE = 128

D_MIX = D_MODEL
H_DIFF = 4
QK_HEAD_DIM = D_MIX // 16
V_HEAD_DIM = 2 * QK_HEAD_DIM
DIFF_WIDTH = H_DIFF * V_HEAD_DIM
A_GROUPS = 4
A_WIDTH = D_MIX - DIFF_WIDTH
A_GROUP_DIM = A_WIDTH // A_GROUPS
CHUNK = 128
Q_COLS = H_DIFF * 2 * QK_HEAD_DIM
K_COLS = Q_COLS
V_COLS = DIFF_WIDTH
IN_COLS = Q_COLS + K_COLS + V_COLS + 2 * A_WIDTH
D_FF = 11 * D_MODEL // 4
CONV_W = 3
REL_BUCKETS = 32
REL_MAX_EXACT = REL_BUCKETS // 2
REL_MAX_DIST = 128
Q_BLOCK = 128
NORM_EPS = 1e-6
SUBLN_EPS = 1e-5
NEG_INF = -1e30

kernel_name = "hymba_diffattn_chunkmlp_convffn_step"

def rmsnorm(x, g, eps=NORM_EPS):
    xf = x.astype(jnp.float32)
    y = xf * lax.rsqrt(jnp.mean(xf * xf, axis=-1, keepdims=True) + eps)
    return (y * g.astype(jnp.float32)).astype(x.dtype)

def layernorm(x, g, b, eps=NORM_EPS):
    xf = x.astype(jnp.float32)
    xc = xf - jnp.mean(xf, axis=-1, keepdims=True)
    y = xc * lax.rsqrt(jnp.mean(xc * xc, axis=-1, keepdims=True) + eps)
    return (y * g.astype(jnp.float32) + b.astype(jnp.float32)).astype(x.dtype)

def t5_bucket(dist):
    n = jnp.maximum(dist, 0)
    nf = jnp.maximum(n, 1).astype(jnp.float32)
    large = REL_MAX_EXACT + (jnp.log(nf / REL_MAX_EXACT) / math.log(REL_MAX_DIST / REL_MAX_EXACT)
                             * (REL_BUCKETS - REL_MAX_EXACT)).astype(jnp.int32)
    large = jnp.minimum(large, REL_BUCKETS - 1)
    return jnp.where(n < REL_MAX_EXACT, n, large)

def lambda_init(layer):
    return 0.8 - 0.6 * math.exp(-0.3 * layer)

def diff_lambda(lq1, lk1, lq2, lk2, lam_init):
    f = jnp.float32
    return (jnp.exp(jnp.sum(lq1.astype(f) * lk1.astype(f)))
            - jnp.exp(jnp.sum(lq2.astype(f) * lk2.astype(f))) + lam_init)

def project(xn, w_in):
    lead = xn.shape[:-1]
    z = xn @ w_in
    q, k, v, a = jnp.split(z, [Q_COLS, Q_COLS + K_COLS, Q_COLS + K_COLS + V_COLS], axis=-1)
    q = q.reshape(*lead, H_DIFF, 2, QK_HEAD_DIM)
    k = k.reshape(*lead, H_DIFF, 2 * QK_HEAD_DIM)
    v = v.reshape(*lead, H_DIFF, V_HEAD_DIM)
    u_a, v_a = jnp.split(jax.nn.gelu(a), 2, axis=-1)
    return q, k, v, u_a, v_a

def diff_attn_core(q, k, v, qpos, kpos, rel_bias, lam):
    B, Tk = k.shape[:2]
    k2 = k.reshape(B, Tk, H_DIFF, 2, QK_HEAD_DIM)
    s = jnp.einsum('bqhmd,bkhmd->bhmqk', q, k2).astype(jnp.float32) * (QK_HEAD_DIM ** -0.5)
    dist = qpos[:, None] - kpos[None, :]
    bias = jnp.transpose(rel_bias.astype(jnp.float32)[t5_bucket(dist)], (2, 0, 1))
    s = jnp.where(dist >= 0, s + bias[None, :, None], NEG_INF)
    p = jax.nn.softmax(s, axis=-1)
    a = p[:, :, 0] - lam * p[:, :, 1]
    return jnp.einsum('bhqk,bkhd->bqhd', a.astype(v.dtype), v)

def diff_attn_prompt(q, k, v, rel_bias, lam):
    B, S = q.shape[:2]
    nblk = S // Q_BLOCK
    qb = jnp.moveaxis(q.reshape(B, nblk, Q_BLOCK, H_DIFF, 2, QK_HEAD_DIM), 1, 0)
    kpos = jnp.arange(S)

    def one_block(args):
        q_blk, bi = args
        qpos = bi * Q_BLOCK + jnp.arange(Q_BLOCK)
        return diff_attn_core(q_blk, k, v, qpos, kpos, rel_bias, lam)

    out = lax.map(one_block, (qb, jnp.arange(nblk)))
    return jnp.moveaxis(out, 0, 1).reshape(B, S, H_DIFF, V_HEAD_DIM)

def diff_head_out(o, subln_gain, lam_init):
    B, L = o.shape[:2]
    o = rmsnorm(o, subln_gain, SUBLN_EPS) * (1.0 - lam_init)
    return o.reshape(B, L, DIFF_WIDTH)

def spatial_gate(u_a, v_a, ln_g, ln_b, w_s, b_s, t_len):
    B, L = v_a.shape[:2]
    vn = layernorm(v_a, ln_g, ln_b)
    vr = vn.reshape(B, L // t_len, t_len, A_GROUPS, A_GROUP_DIM)
    w = jnp.tril(w_s[:, :t_len, :t_len])
    s = jnp.einsum('gts,bnsgc->bntgc', w, vr) + b_s[:, :t_len].T[None, None, :, :, None]
    return u_a * s.reshape(B, L, A_WIDTH), vn

def conv_ffn(xn, buf, w_up, conv_w, conv_b, w_down):
    L = xn.shape[1]
    h = xn @ w_up
    hp = jnp.concatenate([buf.astype(h.dtype), h], axis=1)
    c = conv_b
    for j in range(CONV_W):
        c = c + conv_w[j] * hp[:, j:j + L]
    g, u = jnp.split(c, 2, axis=-1)
    return (jax.nn.silu(g) * u) @ w_down, hp[:, L:]

def setup_inputs(seed: int = 0) -> dict:
    key = jax.random.key(seed)
    ks = jax.random.split(key, 32)
    f = jnp.float32
    n_pages = PAST_LEN // PAGE_SIZE
    n_pool = (DEC_BATCH * n_pages * 5) // 4

    def nrm(k, shape, scale=1.0):
        return jax.random.normal(k, shape, f) * scale

    def gain(k, shape):
        return 1.0 + 0.05 * jax.random.normal(k, shape, f)

    page_table = jax.random.permutation(ks[5], n_pool)[:DEC_BATCH * n_pages]
    page_table = page_table.reshape(DEC_BATCH, n_pages).astype(jnp.int32)
    return {
        "x_prompt": nrm(ks[0], (BATCH, SEQ, D_MODEL)),
        "x_sample": nrm(ks[1], (DEC_BATCH, DEC_SEQ, D_MODEL)),
        "cache_k": nrm(ks[2], (DEPTH, n_pool, PAGE_SIZE, H_DIFF, 2 * QK_HEAD_DIM)),
        "cache_v": nrm(ks[3], (DEPTH, n_pool, PAGE_SIZE, H_DIFF, V_HEAD_DIM)),
        "state_conv": nrm(ks[4], (DEPTH, DEC_BATCH, CONV_W - 1, 2 * D_FF)),
        "page_table": page_table,
        "rel_bias": nrm(ks[6], (REL_BUCKETS, H_DIFF), 0.5),
        "norm_mix_pre": gain(ks[7], (DEPTH, D_MODEL)),
        "norm_mix_post": gain(ks[8], (DEPTH, D_MODEL)),
        "norm_ffn_pre": gain(ks[9], (DEPTH, D_MODEL)),
        "norm_ffn_post": gain(ks[10], (DEPTH, D_MODEL)),
        "w_in": nrm(ks[11], (DEPTH, D_MODEL, IN_COLS), D_MODEL ** -0.5),
        "lambda_q1": nrm(ks[12], (DEPTH, QK_HEAD_DIM), 0.1),
        "lambda_k1": nrm(ks[13], (DEPTH, QK_HEAD_DIM), 0.1),
        "lambda_q2": nrm(ks[14], (DEPTH, QK_HEAD_DIM), 0.1),
        "lambda_k2": nrm(ks[15], (DEPTH, QK_HEAD_DIM), 0.1),
        "subln_gain": gain(ks[16], (DEPTH, V_HEAD_DIM)),
        "sgu_ln_gain": gain(ks[17], (DEPTH, A_WIDTH)),
        "sgu_ln_bias": nrm(ks[18], (DEPTH, A_WIDTH), 0.02),
        "w_spatial": nrm(ks[19], (DEPTH, A_GROUPS, CHUNK, CHUNK), CHUNK ** -0.5),
        "b_spatial": 1.0 + nrm(ks[20], (DEPTH, A_GROUPS, CHUNK), 0.02),
        "w_out": nrm(ks[21], (DEPTH, D_MIX, D_MODEL), D_MIX ** -0.5),
        "w_up": nrm(ks[22], (DEPTH, D_MODEL, 2 * D_FF), D_MODEL ** -0.5),
        "conv_w": nrm(ks[23], (DEPTH, CONV_W, 2 * D_FF), CONV_W ** -0.5),
        "conv_b": nrm(ks[24], (DEPTH, 2 * D_FF), 0.02),
        "w_down": nrm(ks[25], (DEPTH, D_FF, D_MODEL), D_FF ** -0.5),
    }

def reference(x_prompt, x_sample, cache_k, cache_v, state_conv, page_table, rel_bias,
              norm_mix_pre, norm_mix_post, norm_ffn_pre, norm_ffn_post, w_in,
              lambda_q1, lambda_k1, lambda_q2, lambda_k2, subln_gain, sgu_ln_gain, sgu_ln_bias,
              w_spatial, b_spatial, w_out, w_up, conv_w, conv_b, w_down):
    n_pages = page_table.shape[1]
    past_len = n_pages * PAGE_SIZE
    dec_batch, dec_seq = x_sample.shape[:2]

    def layer(x, l, attend, conv_buf, t_len):
        lam_init = lambda_init(l)
        lam = diff_lambda(lambda_q1[l], lambda_k1[l], lambda_q2[l], lambda_k2[l], lam_init)
        xn = rmsnorm(x, norm_mix_pre[l])
        q, k, v, u_a, v_a = project(xn, w_in[l])
        o_b = diff_head_out(attend(q, k, v, lam), subln_gain[l], lam_init)
        o_a, vn = spatial_gate(u_a, v_a, sgu_ln_gain[l], sgu_ln_bias[l], w_spatial[l], b_spatial[l], t_len)
        mix = jnp.concatenate([o_b, o_a], axis=-1) @ w_out[l]
        x = x + rmsnorm(mix, norm_mix_post[l])
        f, new_buf = conv_ffn(rmsnorm(x, norm_ffn_pre[l]), conv_buf, w_up[l], conv_w[l], conv_b[l], w_down[l])
        x = x + rmsnorm(f, norm_ffn_post[l])
        return x, k, v, new_buf, vn

    def prompt_attend(q, k, v, lam):
        return diff_attn_prompt(q, k, v, rel_bias, lam)

    def sample_attend(l):
        def attend(q, k, v, lam):
            pk = cache_k[l][page_table].reshape(dec_batch, past_len, H_DIFF, 2 * QK_HEAD_DIM)
            pv = cache_v[l][page_table].reshape(dec_batch, past_len, H_DIFF, V_HEAD_DIM)
            k_all = jnp.concatenate([pk.astype(k.dtype), k], axis=1)
            v_all = jnp.concatenate([pv.astype(v.dtype), v], axis=1)
            qpos = past_len + jnp.arange(dec_seq)
            kpos = jnp.arange(past_len + dec_seq)
            return diff_attn_core(q, k_all, v_all, qpos, kpos, rel_bias, lam)
        return attend

    zero_buf = jnp.zeros((x_prompt.shape[0], CONV_W - 1, 2 * D_FF), x_prompt.dtype)
    y_p, y_s = x_prompt, x_sample
    kp, vp, cp, ksm, vsm, csm, svs = [], [], [], [], [], [], []
    for l in range(DEPTH):
        y_p, k_l, v_l, c_l, _ = layer(y_p, l, prompt_attend, zero_buf, CHUNK)
        kp.append(k_l); vp.append(v_l); cp.append(c_l)
        y_s, k_l, v_l, c_l, vn_l = layer(y_s, l, sample_attend(l), state_conv[l], dec_seq)
        ksm.append(k_l); vsm.append(v_l); csm.append(c_l); svs.append(vn_l)
    return (y_p, y_s, jnp.stack(kp), jnp.stack(vp), jnp.stack(cp),
            jnp.stack(ksm), jnp.stack(vsm), jnp.stack(csm), jnp.stack(svs))


_drawn_inputs = setup_inputs


def setup_inputs(seed=0):
    import zlib

    import numpy as np

    out = dict(_drawn_inputs(seed))
    spreads = {}
    factors = {'lambda_q2': 64.0,
     'sgu_ln_bias': 2.993,
     'b_spatial': 15.268,
     'conv_b': 3.468,
     'lambda_q1': 4.275,
     'subln_gain': 5.384}
    for name, (base, spread) in spreads.items():
        noise = np.random.default_rng([zlib.crc32(name.encode()), seed]).standard_normal(out[name].shape)
        drawn = base * np.exp(spread * noise) if base else spread * noise
        out[name] = __import__('jax').numpy.asarray(drawn.astype(out[name].dtype))
    for name, factor in factors.items():
        out[name] = (out[name] * factor).astype(out[name].dtype)
    return out
```

```python
import math
from contextlib import ExitStack

import numpy as np

import concourse.bass as bass
from concourse import mybir

ALU = mybir.AluOpType
ACT = mybir.ActivationFunctionType
AX = mybir.AxisListType
F32 = mybir.dt.float32
F32R = mybir.dt.float32r
I32 = mybir.dt.int32

P = 128
D = 1024
KD = D // P
SEQ = 1024
NB, DS = 8, 8
NS = NB * DS
NTOK = NS + SEQ
CW = 364
NPAD = 3 * CW
STEPS = SEQ // P + 1
H, DH, DV = 4, 64, 128
PAGE, NPAGE = 128, 8
FF = 2816
JF = FF // P
AW = 512
AG = 4
EPS = 1e-6
SUBLN_EPS = 1e-5
LAM_INIT = 0.8 - 0.6 * math.exp(-0.3 * 0)
NEG = -1e30
BUCKETS, MAX_EXACT, MAX_DIST = 32, 16, 128
LINE = 3 * P - 1


def rows(s):
    return P if s < STEPS - 1 else NS


def cols(s):
    return slice(NS + P * s, NS + P * (s + 1)) if s < STEPS - 1 else slice(0, NS)


def wide(s):
    return cols(s) if s < STEPS - 1 else slice(0, P)


def bucket(dist):
    n = np.maximum(dist, 0)
    nf = np.maximum(n, 1).astype(np.float32)
    large = MAX_EXACT + (np.log(nf / np.float32(MAX_EXACT)) / np.float32(math.log(MAX_DIST / MAX_EXACT))
                         * np.float32(BUCKETS - MAX_EXACT)).astype(np.int32)
    return np.where(n < MAX_EXACT, n, np.minimum(large, BUCKETS - 1))


def bucket_lines():
    dist = 2 * P - 1 - np.arange(LINE)
    table = np.zeros((BUCKETS + 1, LINE), np.float32)
    for x, d in enumerate(dist):
        if d >= 0:
            table[bucket(d), x] += 1.0
            table[BUCKETS - 1, x] -= 1.0
        else:
            table[BUCKETS, x] = NEG
    return table


def sample_select():
    r = np.arange(P)
    b2h, m, q = r // 16, r // 8 % 2, r % 8
    table = np.zeros((P, 66), np.float32)
    table[r, b2h * 8 + q] = 1.0
    table[r, 64 + m] = 1.0
    return table


def build(nc, x_prompt, x_sample, cache_k, cache_v, state_conv, page_table, rel_bias,
          norm_mix_pre, norm_mix_post, norm_ffn_pre, norm_ffn_post, w_in,
          lambda_q1, lambda_k1, lambda_q2, lambda_k2, subln_gain, sgu_ln_gain, sgu_ln_bias,
          w_spatial, b_spatial, w_out, w_up, conv_w, conv_b, w_down,
          lines, select,
          y_prompt, y_sample, k_prompt, v_prompt, conv_prompt, k_sample, v_sample, conv_sample, sgu_v_sample):
    ctx = ExitStack()
    with ctx:
        _program(ctx, nc, **{k: v for k, v in locals().items() if k not in ("ctx", "nc")})


def _program(ctx, nc, x_prompt, x_sample, cache_k, cache_v, state_conv, page_table, rel_bias,
             norm_mix_pre, norm_mix_post, norm_ffn_pre, norm_ffn_post, w_in,
             lambda_q1, lambda_k1, lambda_q2, lambda_k2, subln_gain, sgu_ln_gain, sgu_ln_bias,
             w_spatial, b_spatial, w_out, w_up, conv_w, conv_b, w_down,
             lines, select,
             y_prompt, y_sample, k_prompt, v_prompt, conv_prompt, k_sample, v_sample, conv_sample, sgu_v_sample):
    BASE = 16512

    def at(name, offset, shape, dt=F32):
        return nc.alloc_sbuf_tensor_at(name, shape, dt, offset=BASE + offset)

    class Region:

        def __init__(self, start, end):
            self.at, self.end = start, end

        def put(self, name, shape, dt=F32):
            t = at(name, self.at, shape, dt)
            self.at += (int(np.prod(shape[1:])) * 4 + 31) // 32 * 32
            assert self.at <= self.end, (name, self.at, self.end)
            return t

    TOP = 212800
    ACT_BYTES = KD * NPAD * 4
    act_hi = at("act_hi", 0, [P, KD, NPAD], F32R)
    act_lo = at("act_lo", ACT_BYTES, [P, KD, NPAD], F32R)
    keep = Region(2 * ACT_BYTES, 2 * ACT_BYTES + 14000)
    ident = keep.put("ident", [P, P])
    identr = keep.put("identr", [P, P], F32R)
    gain = keep.put("gain", [P, D])
    sub_gain = keep.put("sub_gain", [P, DV])
    small = keep.put("small", [P, 256])
    neg_half = small[:, 0:1]
    ssq = small[:, 16:32]
    rstd = small[:, 32:48]
    mean_sq = small[:, 48:64]
    ln_mv = small[:, 64:96].rearrange("p (s c) -> p s c", c=2)
    ln_rstd = small[:, 96:112]
    lam_sum = small[:, 4:6]
    lam_exp = small[:, 6:8]
    lam_dif = small[:, 8:9]
    neg_lam = small[:, 9:10]
    nmax = small[:, 112:120].rearrange("p (i m) -> p i m", m=2)
    psum_ = small[:, 120:128].rearrange("p (i m) -> p i m", m=2)
    precip = small[:, 128:136].rearrange("p (i m) -> p i m", m=2)
    pcoef = small[:, 136:140]
    o_ssq = small[:, 140:144]
    o_mean = small[:, 144:148]
    o_rstd = small[:, 148:152]
    o_fac = small[:, 152:156]
    row_coef = small[:, 156:157]
    smp_max = small[:, 160:164]
    smp_sum = small[:, 164:168]
    smp_recip = small[:, 168:172]
    smp_coef = small[:, 172:176]
    gain_col = small[:, 176:177]
    ssq2 = small[:, 180:189]
    rstd2 = small[:, 190:199]
    mean_sq2 = small[:, 200:209]
    ssq3 = small[:, 210:219]
    rstd3 = small[:, 220:229]
    mean_sq3 = small[:, 230:239]
    SCRATCH = keep.at
    scratch = keep.put("scratch", [P, 512])
    v_smp = keep.put("v_smp", [P, AW])
    smp_bias = keep.put("smp_bias", [P, P + 14 * DS])
    select_sb = keep.put("select_sb", [P, 66])
    sq_hi, sq_lo, sk_hi, sk_lo = (at(n, 2 * ACT_BYTES + 1024 + 1024 * i, [P, H, NS], F32R)
                                  for i, n in enumerate(("sq_hi", "sq_lo", "sk_hi", "sk_lo")))
    R0 = keep.at

    proj = Region(R0, TOP)
    qT = proj.put("qT", [P, H, NTOK])
    kT = proj.put("kT", [P, H, NTOK])
    R1 = proj.at
    uT = proj.put("uT", [P, AG, NTOK])
    va = proj.put("va", [P, STEPS, AW])
    R2 = proj.at
    GC = 256
    w_raw = proj.put("w_raw", [P, 2, 4, GC])
    w_hi = proj.put("w_hi", [P, 2, KD, GC], F32R)
    w_lo = proj.put("w_lo", [P, 2, KD, GC], F32R)
    norm = Region(R0, R1)
    x_in = norm.put("x_in", [P, 3, D])
    x_nrm = norm.put("x_nrm", [P, 2, D])
    junk = norm.put("junk", [P, D])
    v_rows = proj.put("v_rows", [P, 4, GC])
    ws_nat = norm.put("ws_nat", [P, AG, P])
    ws_bd = norm.put("ws_bd", [NS, AG, NS])
    wsT = norm.put("wsT", [P, AG, P])
    wbT = norm.put("wbT", [NS, AG, NS])
    gate = Region(proj.at, TOP)
    wsT_hi = gate.put("wsT_hi", [P, AG, P], F32R)
    wsT_lo = gate.put("wsT_lo", [P, AG, P], F32R)
    wbT_hi = gate.put("wbT_hi", [NS, AG, NS], F32R)
    wbT_lo = gate.put("wbT_lo", [NS, AG, NS], F32R)
    bs = gate.put("bs", [P, AG, P])
    bs_smp = gate.put("bs_smp", [P, AG, NB, DS])
    ln_g = gate.put("ln_g", [P, AW])
    ln_b = gate.put("ln_b", [P, AW])
    late = Region(R2, proj.at)
    vn_hi = late.put("vn_hi", [P, 2, AW], F32R)
    vn_lo = late.put("vn_lo", [P, 2, AW], F32R)
    g_sum = late.put("g_sum", [P, 2, AG, P])
    k_rows = late.put("k_rows", [P, 2, AW])

    early = Region(R1, R2)
    rel_sb = early.put("rel_sb", [BUCKETS, H])
    rel_rep = early.put("rel_rep", [BUCKETS + 1, H, P])
    lines_sb = early.put("lines_sb", [BUCKETS + 1, LINE])
    line_out = early.put("line_out", [P, H, LINE])
    lam_in = early.put("lam_in", [P, 4, DH])
    lam_prod = early.put("lam_prod", [P, 2, DH])
    toeplitz = nc.dram_tensor("toeplitz", [H, P, LINE], F32)
    att = Region(R1, TOP)
    q_hi = att.put("q_hi", [P, 2, SEQ], F32R)
    q_lo = att.put("q_lo", [P, 2, SEQ], F32R)
    k_hi = att.put("k_hi", [P, 2, SEQ], F32R)
    k_lo = att.put("k_lo", [P, 2, SEQ], F32R)
    v_raw = att.put("v_raw", [P, 8, DV])
    v_hi = att.put("v_hi", [P, 2, 8, DV], F32R)
    v_lo = att.put("v_lo", [P, 2, 8, DV], F32R)
    bias_raw = at("bias_raw", att.at, [P, H, 2 * P])
    prob = att.put("prob", [P, 2, 2, SEQ])
    at_hi = att.put("at_hi", [P, SEQ], F32R)
    at_lo = att.put("at_lo", [P, SEQ], F32R)
    o_nrm = att.put("o_nrm", [P, 2, DV])
    bias_hi = att.put("bias_hi", [P, H, 2 * P], F32R)
    bias_lo = att.put("bias_lo", [P, H, 2 * P], F32R)

    smp = Region(R0, TOP)
    VR = 3
    kpage = smp.put("kpage", [P, 8, 512])
    vpage = smp.put("vpage", [P, VR, NPAGE, 512])
    kt_hi = smp.put("kt_hi", [P, 2, H, 512], F32R)
    kt_lo = smp.put("kt_lo", [P, 2, H, 512], F32R)
    QPAD = 8 * 144
    qp_hi = smp.put("qp_hi", [P, QPAD], F32R)
    qp_lo = smp.put("qp_lo", [P, QPAD], F32R)
    TAIL = smp.at
    s_prob = smp.put("s_prob", [P, SEQ + NS])
    c_mat = smp.put("c_mat", [P, NS])
    s_at = smp.put("s_at", [P, NPAGE, NS])
    s_own = smp.put("s_own", [NS, NS])
    ones = smp.put("ones", [P, P])
    s_sq = at("s_sq", TAIL, [P, H * NS])
    s_rs = at("s_rs", TAIL + 1024, [P, H * NS])
    s_ms = at("s_ms", TAIL + 3072, [P, H * NS])
    s_out = at("s_out", TAIL + 2048, [P, H * NS])
    pages = smp.put("pages", [1, NB * NPAGE], I32)
    prj = Region(R0, TOP)
    wo_raw = prj.put("wo_raw", [P, 2, D])
    wo_hi = prj.put("wo_hi", [P, KD, D], F32R)
    wo_lo = prj.put("wo_lo", [P, KD, D], F32R)
    x_res = prj.put("x_res", [P, 2, D])
    y_nrm = prj.put("y_nrm", [P, 2, D])
    x_mid = prj.put("x_mid", [P, 2, D])
    x2_nrm = prj.put("x2_nrm", [P, 2, D])
    junk2 = prj.put("junk2", [P, D])
    gain2 = prj.put("gain2", [P, D])
    mid_dram = nc.dram_tensor("mid_dram", [STEPS, P, D], F32)
    ahead = Region(prj.at, TOP)
    wu_raw = ahead.put("wu_raw", [P, 2, KD, P])
    st_nat = ahead.put("st_nat", [P, 6, P])
    cw_nat = ahead.put("cw_nat", [2 * JF, 4, P])
    ffn = Region(R0, prj.at)
    y_acc = ffn.put("y_acc", [P, STEPS, D])
    W0 = ffn.at
    wu_hi = ffn.put("wu_hi", [P, 2, KD, P], F32R)
    wu_lo = ffn.put("wu_lo", [P, 2, KD, P], F32R)
    x_back = at("x_back", W0, [P, 3, D])
    wd_raw = ffn.put("wd_raw", [P, 2, D])
    wd_hi = ffn.put("wd_hi", [P, 2, D], F32R)
    wd_lo = ffn.put("wd_lo", [P, 2, D], F32R)
    conv = ffn.put("conv", [P, 2, NTOK])
    g_hi = ffn.put("g_hi", [P, 2, NTOK], F32R)
    g_lo = ffn.put("g_lo", [P, 2, NTOK], F32R)
    stT = ffn.put("stT", [P, 48, NB, 2])
    cpT = ffn.put("cpT", [P, 2 * JF, 2])
    cw = ffn.put("cw", [P, 4, 2, JF])
    cwi = ffn.put("cwi", [P, 4, 2, 2])
    hsw = ffn.put("hsw", [P, 2, 2, NB, 2 + DS])
    cpw = ffn.put("cpw", [P, 2, 2, 2])
    h_sb = [ffn.put("h_gate", [P, NPAD]), at("h_up", SCRATCH, [P, NPAD])]

    PS = ctx.enter_context(nc.psum_tensor("PS", [P, 8, 512], F32))

    def sem(name):
        return ctx.enter_context(nc.semaphore(name))

    dve_step, pool_step = sem("dve_step"), sem("pool_step")
    steps = {id(dve_step): 0, id(pool_step): 0}

    def own_step(eng, step):
        steps[id(step)] += 1
        eng.wait_ge(step, steps[id(step)])

    x_loaded = [sem(f"x_loaded{i}") for i in range(3)]
    gain_loaded = sem("gain_loaded")
    const_ready = sem("const_ready")
    ssq_ready = sem("ssq_ready")
    rstd_ready = sem("rstd_ready")
    nrm_ready = sem("nrm_ready")
    xt_ready = sem("xt_ready")
    xt_hi_ready = sem("xt_hi_ready")
    xt_lo_ready = sem("xt_lo_ready")
    w_loaded = [sem(f"w_loaded{i}") for i in range(2)]
    w_hi_ready = sem("w_hi_ready")
    w_lo_ready = sem("w_lo_ready")
    job_ready = sem("job_ready")
    act_took = sem("act_took")
    dve_took = sem("dve_took")
    rows_stored = [sem(f"rows_stored{i}") for i in range(4)]
    mv_ready = sem("mv_ready")
    ln_rstd_ready = sem("ln_rstd_ready")
    vc_ready = sem("vc_ready")
    vn_ready = sem("vn_ready")
    gate_loaded = sem("gate_loaded")
    krow_stored = [sem(f"krow_stored{i}") for i in range(2)]
    v_kept = sem("v_kept")
    bd_zero = sem("bd_zero")
    pad_zero = sem("pad_zero")
    ws_turned = sem("ws_turned")
    ws_taken = sem("ws_taken")
    ws_cut = sem("ws_cut")
    ws_hi_ready = sem("ws_hi_ready")
    ws_lo_ready = sem("ws_lo_ready")
    vn_hi_ready = sem("vn_hi_ready")
    vn_lo_ready = sem("vn_lo_ready")
    gated = sem("gated")
    gate_sum = sem("gate_sum")
    gate_mul = sem("gate_mul")
    gate_hi_ready = sem("gate_hi_ready")
    gate_lo_ready = sem("gate_lo_ready")
    sgu_stored = sem("sgu_stored")
    setup_loaded = sem("setup_loaded")
    rep_ready = sem("rep_ready")
    line_ready = sem("line_ready")
    line_taken = sem("line_taken")
    line_stored = sem("line_stored")
    lam_step = sem("lam_step")
    lam_exp_ready = sem("lam_exp_ready")
    lam_ready = sem("lam_ready")
    bias_loaded = sem("bias_loaded")
    bias_hi_ready = sem("bias_hi_ready")
    bias_lo_ready = sem("bias_lo_ready")
    v_loaded = sem("v_loaded")
    v_hi_ready = sem("v_hi_ready")
    v_lo_ready = sem("v_lo_ready")
    qk_hi_ready = sem("qk_hi_ready")
    qk_lo_ready = sem("qk_lo_ready")
    score_ready = sem("score_ready")
    nmax_ready = sem("nmax_ready")
    prob_ready = sem("prob_ready")
    mix_ready = sem("mix_ready")
    turn_ready = sem("turn_ready")
    at_hi_ready = sem("at_hi_ready")
    at_lo_ready = sem("at_lo_ready")
    o_ready = sem("o_ready")
    osq_ready = sem("osq_ready")
    ofac_ready = sem("ofac_ready")
    onrm_ready = sem("onrm_ready")
    ot_ready = sem("ot_ready")
    ot_hi_ready = sem("ot_hi_ready")
    ot_lo_ready = sem("ot_lo_ready")

    x_tiles = [x_prompt[0, P * s:P * (s + 1), :] for s in range(STEPS - 1)] + \
              [x_sample.rearrange("b t d -> (b t) d")]
    v_out = [v_prompt[0, 0, P * s:P * (s + 1)].rearrange("t h d -> t (h d)") for s in range(STEPS - 1)] + \
            [v_sample[0].rearrange("b t h d -> (b t) (h d)")]
    k_out = [k_prompt[0, 0, P * s:P * (s + 1)].rearrange("t h d -> t (h d)") for s in range(STEPS - 1)] + \
            [k_sample[0].rearrange("b t h d -> (b t) (h d)")]

    QC, KC, VC, UC, AC = 0, 512, 1024, 1536, 2048
    GROUPS = [("va", 0), ("va", 1), ("u", 0), ("u", 1), ("k", 0), ("k", 1), ("q", 0), ("q", 1), ("v", 0), ("v", 1)]
    W_COL = {"va": AC, "u": UC, "k": KC, "q": QC, "v": VC}
    CHUNKS = [slice(CW * c, CW * (c + 1)) for c in range(3)]
    KEPT = [slice(CW * c, min(CW * (c + 1), NTOK)) for c in range(3)]
    jobs = []
    for g, (kind, half) in enumerate(GROUPS):
        if kind in ("va", "v"):
            jobs += [(kind, g, half, 0, s) for s in range(STEPS)]
        else:
            jobs += [(kind, g, half, f, c) for f in range(2) for c in range(3)]
    jobs += [("krow", len(GROUPS), 0, 0, s) for s in range(STEPS)]
    ON_ACT = ("va", "u", "krow")
    took = []
    n_act = n_dve = 0
    for job in jobs:
        if job[0] in ON_ACT:
            n_act += 1
            took.append((act_took, n_act))
        else:
            n_dve += 1
            took.append((dve_took, n_dve))
    first_of = {}
    for n, job in enumerate(jobs):
        first_of.setdefault(job[1], n)
    last_k_took = took[first_of[6] - 1]

    QB = SEQ // P
    NSTEP = H * QB

    def turns(i):
        return (i % QB + 4) // 4

    def turns_before(i):
        return sum(turns(j) for j in range(i))

    sbias_loaded = sem("sbias_loaded")
    sbias_zero = sem("sbias_zero")
    sel_loaded = sem("sel_loaded")
    page_loaded = sem("page_loaded")
    kp_loaded = [sem(f"kp_loaded{i}") for i in range(2)]
    vp_loaded = [sem(f"vp_loaded{i}") for i in range(3)]
    sqk_hi_ready = sem("sqk_hi_ready")
    sqk_lo_ready = sem("sqk_lo_ready")
    qp_zero = sem("qp_zero")
    qp_hi_ready = sem("qp_hi_ready")
    qp_lo_ready = sem("qp_lo_ready")
    kturn_ready = sem("kturn_ready")
    kt_hi_ready = sem("kt_hi_ready")
    kt_lo_ready = sem("kt_lo_ready")
    sscore_ready = sem("sscore_ready")
    smax_ready = sem("smax_ready")
    sprob_ready = sem("sprob_ready")
    cmat_ready = sem("cmat_ready")
    sat_ready = sem("sat_ready")
    sat_taken = sem("sat_taken")
    pv_ready = sem("pv_ready")
    ssq_s_ready = sem("ssq_s_ready")
    ssum_ready = sem("ssum_ready")
    smean_ready = sem("smean_ready")
    srstd_ready = sem("srstd_ready")
    sout_ready = sem("sout_ready")
    sout_hi_ready = sem("sout_hi_ready")
    sout_lo_ready = sem("sout_lo_ready")
    rowcoef_step = sem("rowcoef_step")
    wo_hi_ready = sem("wo_hi_ready")
    wo_lo_ready = sem("wo_lo_ready")
    xres_loaded = [sem(f"xres_loaded{i}") for i in range(2)]
    y_ready = sem("y_ready")
    yssq_ready = sem("yssq_ready")
    yrstd_ready = sem("yrstd_ready")
    ynrm_ready = sem("ynrm_ready")
    xmid_ready = sem("xmid_ready")
    xmid_stored = [sem(f"xmid_stored{i}") for i in range(2)]
    st_loaded = sem("st_loaded")
    cw_loaded = sem("cw_loaded")
    st_turned = sem("st_turned")
    st_taken = sem("st_taken")
    cw_turned = sem("cw_turned")
    cw_taken = sem("cw_taken")
    yacc_zero = sem("yacc_zero")
    cwi_ready = sem("cwi_ready")
    hsp_ready = sem("hsp_ready")
    wu_hi_ready = sem("wu_hi_ready")
    wu_lo_ready = sem("wu_lo_ready")
    wd_loaded = [sem(f"wd_loaded{i}") for i in range(2)]
    wd_hi_ready = sem("wd_hi_ready")
    wd_lo_ready = sem("wd_lo_ready")
    up_ready = sem("up_ready")
    conv_ready = sem("conv_ready")
    tap1_ready = sem("tap1_ready")
    tap_ready = sem("tap_ready")
    stap_ready = sem("stap_ready")
    h_ready = sem("h_ready")
    hs_ready = sem("hs_ready")
    silu_ready = sem("silu_ready")
    prod_ready = sem("prod_ready")
    g_hi_ready = sem("g_hi_ready")
    g_lo_ready = sem("g_lo_ready")
    down_ready = sem("down_ready")
    ybank_free = sem("ybank_free")
    cs_kept = sem("cs_kept")
    cs_stored = sem("cs_stored")
    fout_ready = sem("fout_ready")
    y_stored = sem("y_stored")

    OUT_BASE = 16 * len(GROUPS)
    UP_BASE = OUT_BASE + 16 * KD // 2

    NIT = JF // 2
    YJ = 2 * STEPS

    block = ctx.enter_context(nc.Block())

    def iterations(eng, body):
        body(0, True, False)
        with eng.Fori(1, NIT - 1) as i:
            body(i, False, False)
        body(NIT - 1, False, True)

    def load_smp_bias(eng):
        eng.wait_ge(line_stored, 16)
        eng.wait_ge(sbias_zero, 1)
        for b2 in range(2):
            for h in range(H):
                for m in range(2):
                    r = 64 * b2 + 16 * h + 8 * m
                    base = h * P * LINE + P - 1
                    eng.dma_start(smp_bias[r:r + 8, 0:P], bass.AP(toeplitz, base, [[LINE - 1, 8], [1, P]])).then_inc(sbias_loaded, 16)
                    c = P + DS * (6 + b2)
                    eng.dma_start(smp_bias[r:r + 8, c:c + DS],
                                  bass.AP(toeplitz, base + P, [[LINE - 1, 8], [1, DS]])).then_inc(sbias_loaded, 16)

    def load_w(sp, p):
        kind, half = GROUPS[p // 2]
        c0 = W_COL[kind] + GC * half
        src = w_in[0, 512 * (p % 2):512 * (p % 2 + 1), c0:c0 + GC].rearrange("(k p) c -> p k c", p=P)
        sp.dma_start(w_raw[:, p % 2], src).then_inc(w_loaded[p % 2], 16)

    def act_split_w(act, g):
        for p in (2 * g, 2 * g + 1):
            act.wait_ge(w_loaded[p % 2], 16 * (p // 2 + 1))
            if g >= 2:
                act.wait_ge(job_ready, first_of[g - 1])
            nc.scalar.copy(w_hi[:, g % 2, 4 * (p % 2):4 * (p % 2) + 4, :], w_raw[:, p % 2]).then_inc(w_hi_ready, 1)

    def dve_split_w(dve, g):
        for p in (2 * g, 2 * g + 1):
            ks = slice(4 * (p % 2), 4 * (p % 2) + 4)
            dve.wait_ge(w_hi_ready, p + 1)
            nc.vector.tensor_tensor(w_lo[:, g % 2, ks, :], w_raw[:, p % 2], w_hi[:, g % 2, ks, :].bitcast(F32),
                                    ALU.subtract).then_inc(w_lo_ready, 1)

    @block.sync
    def _(sp):
        sp.dma_start(rel_sb[:], rel_bias[:, :]).then_inc(setup_loaded, 16)
        sp.dma_start(lines_sb[:], lines[:, :]).then_inc(setup_loaded, 16)
        sp.dma_start(gain[:], norm_mix_pre[0:1, :].to_broadcast([P, D])).then_inc(gain_loaded, 16)
        for s in range(STEPS):
            if s >= 3:
                sp.wait_ge(nrm_ready, s - 2)
            sp.dma_start(x_in[0:rows(s), s % 3, :], x_tiles[s]).then_inc(x_loaded[s % 3], 16)
            if s == 2:
                for p in range(2):
                    load_w(sp, p)
        for p in range(2, 2 * len(GROUPS)):
            sp.wait_ge(w_lo_ready, p - 1)
            load_w(sp, p)
        load_smp_bias(sp)
        sp.dma_start(select_sb[:], select[:, :]).then_inc(sel_loaded, 16)
        sp.dma_start(gain_col, subln_gain.rearrange("a d -> d a")).then_inc(sel_loaded, 16)
        v_jobs = [n for n, job in enumerate(jobs) if job[0] == "v"]
        for i, n in enumerate(v_jobs):
            kind, g, half, f, s = jobs[n]
            sp.wait_ge(*took[n])
            sp.dma_start(v_out[s][:, GC * half:GC * half + GC],
                         v_rows[0:rows(s), i % 4, :]).then_inc(rows_stored[i % 4], 16)
        for i in range(4):
            sp.wait_ge(rows_stored[i], 16 * ((len(v_jobs) + 3 - i) // 4))
        sp.wait_ge(line_stored, 16)
        sp.wait_ge(gate_lo_ready, STEPS)
        sp.wait_ge(sgu_stored, 16)
        skewed = bass.AP(toeplitz, P - 1, [[LINE - 1, P], [P * LINE, H], [1, 2 * P]])
        sp.dma_start(bias_raw[:], skewed).then_inc(bias_loaded, 16)
        for h in range(H):
            if h >= 1:
                sp.wait_ge(v_lo_ready, h)
            sp.dma_start(v_raw[:], v_prompt[0, 0, :, h, :].rearrange("(k p) d -> p k d", p=P)).then_inc(v_loaded, 16)
        sp.wait_ge(ot_lo_ready, NSTEP)
        sp.wait_ge(sqk_lo_ready, 2)
        sp.dma_start(pages[:], page_table.rearrange("b n -> (b n)").rearrange("(a n) -> a n", a=1)).then_inc(page_loaded, 16)
        sp.wait_ge(page_loaded, 16)
        n_pool = cache_k.shape[1]
        for b in range(NB):
            for p in range(NPAGE):
                if b >= 1:
                    sp.wait_ge(kturn_ready, NPAGE * (b - 1) + p + 1)
                page = sp.value_load(pages[0:1, NPAGE * b + p:NPAGE * b + p + 1], min_val=0, max_val=n_pool - 1)
                sp.dma_start(kpage[:, p, :], cache_k[0, bass.ds(page, 1)].rearrange("a t h d -> t (a h d)")).then_inc(kp_loaded[p // 4], 16)
            if b >= VR:
                sp.wait_ge(pv_ready, (b - VR) // 2 + 1)
            for p in range(NPAGE):
                page = sp.value_load(pages[0:1, NPAGE * b + p:NPAGE * b + p + 1], min_val=0, max_val=n_pool - 1)
                sp.dma_start(vpage[:, b % VR, p, :], cache_v[0, bass.ds(page, 1)].rearrange("a t h d -> t (a h d)")).then_inc(vp_loaded[b % VR], 16)
        sp.wait_ge(sout_lo_ready, 1)
        sp.dma_start(gain[:], norm_mix_post[0:1, :].to_broadcast([P, D])).then_inc(gain_loaded, 16)
        sp.dma_start(gain2[:], norm_ffn_pre[0:1, :].to_broadcast([P, D])).then_inc(gain_loaded, 16)
        for k in range(KD):
            if k >= 2:
                sp.wait_ge(wo_lo_ready, k - 1)
            sp.dma_start(wo_raw[:, k % 2, :], w_out[0, P * k:P * k + P, :]).then_inc(w_loaded[k % 2], 16)
        for q in range(6):
            for j in range(8 * q, min(8 * q + 8, 2 * JF)):
                sp.dma_start(st_nat[16 * (j % 8):16 * (j % 8) + 16, q, :],
                             state_conv[0].rearrange("b r c -> (b r) c")[:, P * j:P * j + P]).then_inc(st_loaded, 16)
        for w in range(3):
            sp.dma_start(cw_nat[:, w, :], conv_w[0, w].rearrange("(j c) -> j c", c=P)).then_inc(cw_loaded, 16)
        sp.dma_start(cw_nat[:, 3, :], conv_b[0].rearrange("(j c) -> j c", c=P)).then_inc(cw_loaded, 16)
        sp.wait_ge(wo_lo_ready, KD)
        for t in range(2):
            sp.dma_start(wu_raw[:, t], w_up[0, :, FF * t:FF * t + P].rearrange("(k p) c -> p k c", p=P)).then_inc(w_loaded[t], 16)
        for t in range(STEPS + 1):
            if t < STEPS:
                if t >= 2:
                    sp.wait_ge(xmid_ready, t - 1)
                sp.dma_start(x_res[0:rows(t), t % 2, :], x_tiles[t]).then_inc(xres_loaded[t % 2], 16)
            if t >= 1:
                sp.wait_ge(xmid_ready, t)
                sp.dma_start(mid_dram[t - 1, 0:rows(t - 1), :], x_mid[0:rows(t - 1), (t - 1) % 2, :]).then_inc(xmid_stored[(t - 1) % 2], 16)
        sp.wait_ge(xt_lo_ready, 2 * STEPS + 2 * STEPS)
        for i in range(2):
            sp.wait_ge(xmid_stored[i], 16 * ((STEPS + 1 - i) // 2))
        sp.dma_start(gain[:], norm_ffn_post[0:1, :].to_broadcast([P, D])).then_inc(gain_loaded, 16)

        def load_ffn(i, first, last):
            for t in range(2 if first else 0, 4):
                sp.wait_ge(wu_lo_ready, 4 * i + t - 1)
                c0 = (t % 2) * FF + P * (t // 2) + 2 * P * i
                src = w_up[0, :, bass.ds(c0, P)].rearrange("(k p) c -> p k c", p=P)
                sp.dma_start(wu_raw[:, t % 2], src).then_inc(w_loaded[t % 2], 16)
            for e in range(2):
                if not first:
                    sp.wait_ge(wd_lo_ready, 2 * i + e - 1)
                sp.dma_start(wd_raw[:, e, :], w_down[0, bass.ds(2 * P * i + P * e, P), :]).then_inc(wd_loaded[e], 16)
        iterations(sp, load_ffn)
        sp.wait_ge(up_ready, 4 * NIT)
        for t in range(STEPS + 1):
            if t < STEPS:
                if t >= 3:
                    sp.wait_ge(fout_ready, t - 2)
                sp.dma_start(x_back[0:rows(t), t % 3, :], mid_dram[t, 0:rows(t), :]).then_inc(x_loaded[t % 3], 16)
            if t >= 1:
                sp.wait_ge(fout_ready, t)
                dst = y_prompt[0, P * (t - 1):P * t, :] if t < STEPS else y_sample.rearrange("b t d -> (b t) d")
                sp.dma_start(dst, y_acc[0:rows(t - 1), t - 1, :]).then_inc(y_stored, 16)
        for q in range(6):
            sp.wait_ge(st_taken, 6 + q + 1)
            for j in range(8 * q, min(8 * q + 8, 2 * JF)):
                sp.dma_start(conv_sample[0].rearrange("b r c -> (b r) c")[:, P * j:P * j + P],
                             st_nat[16 * (j % 8):16 * (j % 8) + 16, q, :]).then_inc(cs_stored, 16)
        sp.wait_ge(st_taken, 6 + 7)
        sp.dma_start(conv_prompt[0, 0].rearrange("r (j c) -> j r c", c=P), cw_nat[:, 0:2, :]).then_inc(cs_stored, 16)
        sp.wait_ge(cs_stored, 16 * (2 * JF + 1))
        sp.wait_ge(y_stored, 16 * STEPS)

    @block.scalar
    def _(act):
        for i, lam in enumerate((lambda_q1, lambda_q2, lambda_k1, lambda_k2)):
            act.dma_start(lam_in[:, i, :], lam[0:1, :].to_broadcast([P, DH])).then_inc(setup_loaded, 16)
        act.dma_start(sub_gain[:], subln_gain[0:1, :].to_broadcast([P, DV])).then_inc(setup_loaded, 16)
        act.dma_start(ws_nat[:], w_spatial[0].rearrange("g t s -> t g s")).then_inc(gate_loaded, 16)
        act.dma_start(bs[:], b_spatial[0:1].to_broadcast([P, AG, P])).then_inc(gate_loaded, 16)
        act.dma_start(ln_g[:], sgu_ln_gain[0:1, :].to_broadcast([P, AW])).then_inc(gate_loaded, 16)
        act.dma_start(ln_b[:], sgu_ln_bias[0:1, :].to_broadcast([P, AW])).then_inc(gate_loaded, 16)
        act.wait_ge(bd_zero, 1)
        for b in range(NB):
            o = slice(DS * b, DS * (b + 1))
            act.dma_start(ws_bd[o, :, o], w_spatial[0, :, 0:DS, 0:DS].rearrange("g t s -> t g s")).then_inc(gate_loaded, 16)
            act.dma_start(bs_smp[:, :, b, :], b_spatial[0:1, :, 0:DS].to_broadcast([P, AG, DS])).then_inc(gate_loaded, 16)
        def xt_hi(s):
            for h in range(2):
                act.wait_ge(xt_ready, 2 * s + h + 1)
                src = PS[:, (2 * s + h) % 8, :].rearrange("p (k t) -> p k t", k=4)[:, :, 0:rows(s)]
                nc.scalar.copy(act_hi[:, 4 * h:4 * h + 4, cols(s)], src).then_inc(xt_hi_ready, 1)
        act.wait_ge(line_taken, H)
        act.dma_start(bass.AP(toeplitz, 0, [[LINE, P], [P * LINE, H], [1, LINE]]), line_out[:]).then_inc(line_stored, 16)
        for s in range(STEPS):
            act.wait_ge(x_loaded[s % 3], 16 * (s // 3 + 1))
            if s >= 1:
                act.wait_ge(ssq_ready, s)
            nc.scalar.activation(junk[0:rows(s), :], x_in[0:rows(s), s % 3, :], ACT.Square,
                                 accum_out=ssq[0:rows(s), s:s + 1]).then_inc(ssq_ready, 1)
            if s >= 1:
                xt_hi(s - 1)
            if s == 3:
                act_split_w(act, 0)
        xt_hi(STEPS - 1)
        act.wait_ge(lam_step, 3)
        nc.scalar.activation(lam_exp, lam_sum, ACT.Exp).then_inc(lam_exp_ready, 1)
        act.wait_ge(ws_turned, 1)
        nc.scalar.copy(wsT[:], PS[:, 2, :].rearrange("p (g t) -> p g t", g=AG)).then_inc(ws_taken, 1)
        act.wait_ge(ws_turned, 2)
        nc.scalar.copy(wbT[:], PS[0:NS, 3, 0:AG * NS].rearrange("p (g t) -> p g t", g=AG)).then_inc(ws_taken, 1)
        act_split_w(act, 1)
        act.wait_ge(ws_cut, 2)
        nc.scalar.copy(wsT_hi[:], wsT[:]).then_inc(ws_hi_ready, 1)
        nc.scalar.copy(wbT_hi[:], wbT[:]).then_inc(ws_hi_ready, 1)
        split = 1
        for n, (kind, g, half, f, c) in enumerate(jobs):
            if g > split - 1 and g + 1 < len(GROUPS) and g + 1 > split:
                split = g + 1
                act_split_w(act, split)
            if kind not in ON_ACT:
                continue
            act.wait_ge(job_ready, n + 1)
            if kind == "va":
                nc.scalar.activation(va[0:rows(c), c, GC * half:GC * half + GC], PS[0:rows(c), n % 8, 0:GC],
                                     ACT.Gelu_apprx_tanh).then_inc(act_took, 1)
            elif kind == "u":
                act.wait_ge(line_stored, 16)
                w = KEPT[c].stop - KEPT[c].start
                nc.scalar.activation(uT[:, 2 * half + f, KEPT[c]], PS[:, n % 8, 0:w],
                                     ACT.Gelu_apprx_tanh).then_inc(act_took, 1)
            else:
                if c >= 2:
                    act.wait_ge(krow_stored[c % 2], 16 * (c // 2))
                nc.scalar.copy(k_rows[0:rows(c), c % 2, :], PS[0:rows(c), n % 8, :]).then_inc(act_took, 1)
                act.wait_ge(act_took, took[n][1])
                act.dma_start(k_out[c], k_rows[0:rows(c), c % 2, :]).then_inc(krow_stored[c % 2], 16)
        def gate_hi(s):
            act.wait_ge(gate_mul, s + 1)
            nc.scalar.copy(act_hi[:, 4:8, cols(s)], g_sum[:, s % 2, :, 0:rows(s)]).then_inc(gate_hi_ready, 1)
        for s in range(STEPS):
            act.wait_ge(vn_ready, s + 1)
            if s >= 2:
                act.wait_ge(gated, s - 1)
            nc.scalar.copy(vn_hi[0:rows(s), s % 2, :], va[0:rows(s), s, :]).then_inc(vn_hi_ready, 1)
            if s >= 1:
                gate_hi(s - 1)
        gate_hi(STEPS - 1)
        for i in range(2):
            act.wait_ge(krow_stored[i], 16 * ((STEPS + 1 - i) // 2))
        act.wait_ge(sgu_stored, 16)
        act.wait_ge(gate_lo_ready, STEPS)

        def split_hi(h):
            if h >= 2:
                act.wait_ge(score_ready, 2 * QB * (h - 1))
            nc.scalar.mul(q_hi[:, h % 2, :], qT[:, h, NS:], DH ** -0.5).then_inc(qk_hi_ready, 1)
            nc.scalar.copy(k_hi[:, h % 2, :], kT[:, h, NS:]).then_inc(qk_hi_ready, 1)
            if h >= 2:
                act.wait_ge(o_ready, QB * (h - 1))
            act.wait_ge(v_loaded, 16 * (h + 1))
            nc.scalar.copy(v_hi[:, h % 2], v_raw[:]).then_inc(v_hi_ready, 1)

        def at_hi_part(i):
            n = i % QB + 1
            for t in range(turns(i)):
                act.wait_ge(turn_ready, turns_before(i) + t + 1)
                if i >= 1:
                    act.wait_ge(o_ready, i)
                w = slice(512 * t, min(512 * (t + 1), P * n))
                nc.scalar.copy(at_hi[:, w], PS[:, 4 + t, 0:w.stop - w.start]).then_inc(at_hi_ready, 1)

        def exponent(i):
            for m in range(2):
                act.wait_ge(nmax_ready, 2 * i + m + 1)
                if i >= 2:
                    act.wait_ge(turn_ready, turns_before(i - 1))
                w = P * (i % QB + 1)
                src = PS[:, 2 * m:2 * m + 2, :].rearrange("p a b -> p (a b)")[:, 0:w]
                nc.scalar.activation(prob[:, i % 2, m, 0:w], src, ACT.Exp, bias=nmax[:, i % 4, m:m + 1],
                                     accum_out=psum_[:, i % 4, m:m + 1]).then_inc(prob_ready, 1)

        def out_square(i):
            act.wait_ge(o_ready, i + 1)
            if i >= 1:
                act.wait_ge(osq_ready, i)
            nc.scalar.activation(scratch[:, 0:DV], PS[:, 6, 0:DV], ACT.Square, scale=precip[:, i % 4, 0:1],
                                 accum_out=o_ssq[:, i % 4:i % 4 + 1]).then_inc(osq_ready, 1)

        def out_hi(i):
            act.wait_ge(ot_ready, i + 1)
            nc.scalar.copy(act_hi[:, i // QB, cols(i % QB)], PS[:, 7, 0:P]).then_inc(ot_hi_ready, 1)

        act.wait_ge(bias_loaded, 16)
        nc.scalar.copy(bias_hi[:], bias_raw[:]).then_inc(bias_hi_ready, 1)
        act.wait_ge(bias_lo_ready, 1)
        split_hi(0)
        for i in range(NSTEP + 4):
            if 0 <= i - 2 < NSTEP:
                at_hi_part(i - 2)
            if i < NSTEP:
                exponent(i)
            if 0 <= i - 2 < NSTEP:
                out_square(i - 2)
            if 0 <= i - 3 < NSTEP:
                out_hi(i - 3)
            if i % QB == 4 and i // QB + 1 < H:
                split_hi(i // QB + 1)
        nc.scalar.mul(sq_hi[:], qT[:, :, 0:NS], DH ** -0.5).then_inc(sqk_hi_ready, 1)
        nc.scalar.copy(sk_hi[:], kT[:, :, 0:NS]).then_inc(sqk_hi_ready, 1)
        def kt_hi_part(n):
            u, p = n // 4, n % 4
            act.wait_ge(kturn_ready, n + 1)
            if u >= 2:
                act.wait_ge(sscore_ready, u - 1)
            src = PS[:, 3 + n % 2, :].rearrange("p (h t) -> p h t", h=H)
            nc.scalar.copy(kt_hi[:, u % 2, :, P * p:P * p + P], src).then_inc(kt_hi_ready, 1)

        def q_pad_hi(pr):
            if pr >= 1:
                act.wait_ge(sscore_ready, 4 * pr)
            for m in range(2):
                d = slice(DH * m, DH * m + DH)
                dst = qp_hi[d, :].rearrange("p (b h c) -> p b h c", b=2, h=H)[:, :, :, DS * m:DS * m + DS]
                src = sq_hi[d, :, 16 * pr:16 * pr + 16].bitcast(F32).rearrange("p h (b q) -> p b h q", b=2)
                nc.scalar.copy(dst, src).then_inc(qp_hi_ready, 1)

        def smp_exponent(pr):
            act.wait_ge(smax_ready, pr + 1)
            if pr >= 1:
                act.wait_ge(sat_ready, pr)
            nc.scalar.activation(s_prob[:], PS[:, 0:3, :].rearrange("p a b -> p (a b)")[:, 0:SEQ + NS], ACT.Exp,
                                 bias=smp_max[:, pr:pr + 1], accum_out=smp_sum[:, pr:pr + 1]).then_inc(sprob_ready, 1)

        def smp_take(pr):
            act.wait_ge(sat_ready, pr + 1)
            if pr >= 1:
                act.wait_ge(pv_ready, pr)
            nc.scalar.copy(s_at[:], PS[:, 5, :].rearrange("p (n c) -> p n c", n=NPAGE)).then_inc(sat_taken, 1)
            nc.scalar.copy(s_own[:], PS[0:NS, 6, 0:NS]).then_inc(sat_taken, 1)

        act.wait_ge(ot_lo_ready, NSTEP)
        act.wait_ge(qp_zero, 3)
        for u in range(2 * NB + 1):
            if u < 2 * NB:
                for p in range(4):
                    kt_hi_part(4 * u + p)
            if u % 4 == 0 and u < 2 * NB:
                act.wait_ge(sqk_lo_ready, 2)
                q_pad_hi(u // 4)
            if u % 4 == 0 and u >= 4:
                smp_exponent(u // 4 - 1)
            if u % 4 == 1 and u >= 5:
                smp_take(u // 4 - 1)
        smp_take(NB // 2 - 1)
        act.wait_ge(pv_ready, NB // 2)
        nc.scalar.activation(s_sq[:], PS[:, 7, 0:H * NS], ACT.Square).then_inc(ssq_s_ready, 1)
        act.wait_ge(sout_ready, 1)
        nc.scalar.copy(act_hi[:, 0:H, 0:NS], s_out[:].rearrange("p (h c) -> p h c", h=H)).then_inc(sout_hi_ready, 1)
        for k in range(KD):
            act.wait_ge(w_loaded[k % 2], OUT_BASE + 16 * (k // 2 + 1))
            nc.scalar.copy(wo_hi[:, k, :], wo_raw[:, k % 2, :]).then_inc(wo_hi_ready, 1)

        def x2_hi(t):
            for h in range(2):
                act.wait_ge(xt_ready, 2 * STEPS + 2 * t + h + 1)
                src = PS[:, 4 + (2 * t + h) % 4, :].rearrange("p (k t) -> p k t", k=4)[:, :, 0:rows(t)]
                nc.scalar.copy(act_hi[:, 4 * h:4 * h + 4, cols(t)], src).then_inc(xt_hi_ready, 1)
        for t in range(STEPS + 1):
            if t < STEPS:
                r, j = rows(t), 2 * (t % 2)
                act.wait_ge(y_ready, t + 1)
                if t >= 1:
                    act.wait_ge(ssq_ready, STEPS + t)
                nc.scalar.activation(junk2[0:r, :], PS[0:r, j:j + 2, :].rearrange("p a b -> p (a b)"), ACT.Square,
                                     accum_out=ssq2[0:r, t:t + 1]).then_inc(yssq_ready, 1)
                act.wait_ge(xmid_ready, t + 1)
                act.wait_ge(yssq_ready, t + 1)
                nc.scalar.activation(junk2[0:r, :], x_mid[0:r, t % 2, :], ACT.Square,
                                     accum_out=ssq3[0:r, t:t + 1]).then_inc(ssq_ready, 1)
            if t >= 1:
                x2_hi(t - 1)
        def ffn_act(i, first, last):
            def split(t, ahead):
                n = 4 * i + t + ahead
                act.wait_ge(w_loaded[(t + ahead) % 2], UP_BASE + 8 * (n - (t + ahead) % 2) + 16)
                if ahead == 2:
                    act.wait_ge(up_ready, 4 * i + t + 1)
                nc.scalar.copy(wu_hi[:, (t + ahead) % 2], wu_raw[:, (t + ahead) % 2]).then_inc(wu_hi_ready, 1)

            if first:
                split(0, 0)
                split(1, 0)
                act.wait_ge(yacc_zero, 1)
            act.wait_ge(cwi_ready, i + 1)
            act.wait_ge(hsp_ready, 2 * i + 2)
            for t in range(4):
                e, half = t // 2, t % 2
                act.wait_ge(up_ready, 4 * i + t + 1)
                if not first or t >= 2:
                    act.wait_ge(tap_ready, 4 * i + t - 1)
                h = h_sb[half]
                nc.scalar.copy(h[:].rearrange("p (c t) -> p c t", c=3), PS[:, 3 * half:3 * half + 3, 0:CW]).then_inc(h_ready, 1)
                nc.scalar.copy(hsw[:, half, e, :, 2:], PS[:, 3 * half, 0:NS].rearrange("p (b q) -> p b q", b=NB)).then_inc(hs_ready, 1)
                if not first or t >= 2:
                    act.wait_ge(prod_ready if half == 0 else g_lo_ready, 2 * i + e)
                act.wait_ge(h_ready, 4 * i + t + 1)
                if half == 0 and (not first or t >= 2):
                    act.wait_ge(silu_ready, 2 * i + e)
                tap, bias = cwi[:, 2, half, e:e + 1], cwi[:, 3, half, e:e + 1]
                nc.scalar.activation(conv[:, half, :], h[:, 0:NTOK], ACT.Identity, bias=bias, scale=tap).then_inc(conv_ready, 1)
                if not (last and t >= 2):
                    split(t, 2)
                if half == 0:
                    act.wait_ge(tap_ready, 4 * i + t + 1)
                    nc.scalar.activation(conv[:, 0, :], conv[:, 0, :], ACT.Silu).then_inc(silu_ready, 1)
                else:
                    act.wait_ge(prod_ready, 2 * i + e + 1)
                    if not first:
                        act.wait_ge(down_ready, YJ * i)
                    nc.scalar.copy(g_hi[:, e, :], conv[:, 1, :]).then_inc(g_hi_ready, 1)
                    if t == 1:
                        for k in range(2):
                            act.wait_ge(wd_loaded[k], 16 * i + 16)
                            nc.scalar.copy(wd_hi[:, k, :], wd_raw[:, k, :]).then_inc(wd_hi_ready, 1)
        iterations(act, ffn_act)
        for t in range(STEPS):
            r = rows(t)
            act.wait_ge(ybank_free, YJ * (NIT - 1) + 2 * t + 4)
            if t >= 1:
                act.wait_ge(ssq_ready, 2 * STEPS + t)
            nc.scalar.activation(conv[0:r, 0, 0:D], y_acc[0:r, t, :], ACT.Square, accum_out=ssq[0:r, t:t + 1]).then_inc(ssq_ready, 1)

    @block.gpsimd
    def _(pool):
        nc.gpsimd.memset(ident[:], 0.0).then_inc(const_ready, 1)
        pool.wait_ge(const_ready, 1)
        nc.gpsimd.affine_select(out=ident[:], in_=ident[:], compare_op=ALU.not_equal, fill=1.0, base=0,
                                pattern=[[-1, P]], channel_multiplier=1).then_inc(const_ready, 1)
        nc.gpsimd.memset(small[:], -0.5).then_inc(const_ready, 1)
        nc.gpsimd.memset(smp_bias[:], NEG).then_inc(sbias_zero, 1)
        nc.gpsimd.memset(ws_bd[:], 0.0).then_inc(bd_zero, 1)
        for a in (act_hi, act_lo):
            nc.gpsimd.memset(a[:, :, NTOK:].bitcast(F32), 0.0).then_inc(pad_zero, 1)
        pool.wait_ge(const_ready, 3)
        nc.gpsimd.tensor_copy(identr[:], ident[:]).then_inc(const_ready, 1)

        def root(src, dst, i, n, scale, eps, done_sem):
            nc.gpsimd.tensor_scalar(mean_sq[0:n, i:i + 1], src, scale, eps, ALU.mult, ALU.add).then_inc(pool_step, 1)
            own_step(pool, pool_step)
            nc.gpsimd.tensor_tensor(dst, mean_sq[0:n, i:i + 1], neg_half[0:n], ALU.pow).then_inc(done_sem, 1)

        for s in range(STEPS):
            r = rows(s)
            pool.wait_ge(ssq_ready, s + 1)
            root(ssq[0:r, s:s + 1], rstd[0:r, s:s + 1], s, r, 1.0 / D, EPS, rstd_ready)
        for i, w in enumerate((wsT, wbT)):
            pool.wait_ge(ws_taken, i + 1)
            n = P if i == 0 else NS
            nc.gpsimd.affine_select(out=w[:], in_=w[:], compare_op=ALU.is_ge, fill=0.0, base=0,
                                    pattern=[[0, AG], [1, n]], channel_multiplier=-1).then_inc(ws_cut, 1)
        for s in range(STEPS):
            r = rows(s)
            pool.wait_ge(mv_ready, s + 1)
            root(ln_mv[0:r, s, 1:2], ln_rstd[0:r, s:s + 1], s, r, 1.0, EPS, ln_rstd_ready)
            pool.wait_ge(vc_ready, s + 1)
            nc.gpsimd.tensor_tensor(va[0:r, s, :], va[0:r, s, :], ln_g[0:r, :], ALU.mult).then_inc(pool_step, 1)
            own_step(pool, pool_step)
            nc.gpsimd.tensor_tensor(va[0:r, s, :], va[0:r, s, :], ln_b[0:r, :], ALU.add).then_inc(vn_ready, 1)
        pool.wait_ge(vn_ready, STEPS)
        pool.dma_start(sgu_v_sample[0].rearrange("b t c -> (b t) c"), va[0:NS, STEPS - 1, :]).then_inc(sgu_stored, 16)
        pool.wait_ge(sgu_stored, 16)
        for i in range(NSTEP):
            c = slice(i % 4, i % 4 + 1)
            pool.wait_ge(osq_ready, i + 1)
            nc.gpsimd.tensor_scalar(o_mean[:, c], o_ssq[:, c], 1.0 / DV, SUBLN_EPS, ALU.mult, ALU.add).then_inc(pool_step, 1)
            own_step(pool, pool_step)
            nc.gpsimd.tensor_tensor(o_rstd[:, c], o_mean[:, c], neg_half, ALU.pow).then_inc(pool_step, 1)
            own_step(pool, pool_step)
            nc.gpsimd.tensor_tensor(o_fac[:, c], o_rstd[:, c], precip[:, i % 4, 0:1], ALU.mult).then_inc(ofac_ready, 1)
        pool.wait_ge(smean_ready, 1)
        nc.gpsimd.tensor_tensor(s_rs[:], s_ms[:], neg_half.to_broadcast([P, H * NS]), ALU.pow).then_inc(srstd_ready, 1)
        def root2(src, mean, dst, t, src_sem, n, done_sem):
            r, c = rows(t), slice(t, t + 1)
            pool.wait_ge(src_sem, n)
            nc.gpsimd.tensor_scalar(mean[0:r, c], src[0:r, c], 1.0 / D, EPS, ALU.mult, ALU.add).then_inc(pool_step, 1)
            own_step(pool, pool_step)
            nc.gpsimd.tensor_tensor(dst[0:r, c], mean[0:r, c], neg_half[0:r], ALU.pow).then_inc(done_sem, 1)
        for t in range(STEPS):
            root2(ssq2, mean_sq2, rstd2, t, yssq_ready, t + 1, yrstd_ready)
            root2(ssq3, mean_sq3, rstd3, t, ssq_ready, STEPS + t + 1, rstd_ready)
        pool.wait_ge(xt_lo_ready, 2 * STEPS + 2 * STEPS)
        for i in range(2):
            pool.wait_ge(xmid_stored[i], 16 * ((STEPS + 1 - i) // 2))
        nc.gpsimd.memset(y_acc[:], 0.0).then_inc(yacc_zero, 1)
        pool.wait_ge(st_taken, 6)
        pool.wait_ge(cw_taken, 1)

        def ffn_pool(i, first, last):
            if not first:
                pool.wait_ge(tap_ready, 4 * i)
                pool.wait_ge(hs_ready, 4 * i)
                keep_states(i - 1)
            nc.gpsimd.tensor_copy(cwi[:], cw[:, :, :, bass.ds(2 * i, 2)]).then_inc(cwi_ready, 1)
            for half in range(2):
                nc.gpsimd.tensor_copy(hsw[:, half, :, :, 0:2], stT[:, bass.ds(JF * half + 2 * i, 2)]).then_inc(hsp_ready, 1)

        def keep_states(i):
            for half in range(2):
                nc.gpsimd.tensor_copy(stT[:, bass.ds(JF * half + 2 * i, 2)], hsw[:, half, :, :, DS:]).then_inc(cs_kept, 1)
                nc.gpsimd.tensor_copy(cpT[:, bass.ds(JF * half + 2 * i, 2)], cpw[:, half]).then_inc(cs_kept, 1)
            pool.wait_ge(cs_kept, 4 * i + 4)
        iterations(pool, ffn_pool)
        pool.wait_ge(tap_ready, 4 * NIT)
        pool.wait_ge(hs_ready, 4 * NIT)
        keep_states(NIT - 1)
        def final_add(t):
            r = rows(t)
            pool.wait_ge(ynrm_ready, STEPS + t + 1)
            pool.wait_ge(x_loaded[t % 3], 16 * (STEPS // 3) + 16 * (t // 3 + 1))
            nc.gpsimd.tensor_tensor(y_acc[0:r, t, :], y_acc[0:r, t, :], x_back[0:r, t % 3, :], ALU.add).then_inc(fout_ready, 1)
        for t in range(STEPS):
            r = rows(t)
            pool.wait_ge(ssq_ready, 2 * STEPS + t + 1)
            c = slice(t, t + 1)
            nc.gpsimd.tensor_scalar(mean_sq[0:r, c], ssq[0:r, c], 1.0 / D, EPS, ALU.mult, ALU.add).then_inc(pool_step, 1)
            own_step(pool, pool_step)
            nc.gpsimd.tensor_tensor(rstd[0:r, c], mean_sq[0:r, c], neg_half[0:r], ALU.pow).then_inc(rstd_ready, 1)
            if t >= 1:
                final_add(t - 1)
        final_add(STEPS - 1)

    @block.vector
    def _(dve):
        nc.vector.memset(rel_rep[:], 1.0).then_inc(rep_ready, 1)
        dve.wait_ge(setup_loaded, 16 * 7)
        dve.wait_ge(rep_ready, 1)
        for h in range(H):
            nc.vector.tensor_copy(rel_rep[0:BUCKETS, h, :], rel_sb[:, h:h + 1].to_broadcast([BUCKETS, P])).then_inc(rep_ready, 1)
        nc.vector.tensor_tensor(lam_prod[:], lam_in[:, 0:2, :], lam_in[:, 2:4, :], ALU.mult).then_inc(lam_step, 1)
        nc.vector.tensor_scalar(sub_gain[:], sub_gain[:], 1.0 - LAM_INIT, None, ALU.mult).then_inc(lam_step, 1)
        dve.wait_ge(lam_step, 2)
        dve.wait_ge(const_ready, 3)
        nc.vector.tensor_reduce(lam_sum, lam_prod[:], AX.X, ALU.add).then_inc(lam_step, 1)
        for h in range(H):
            dve.wait_ge(line_ready, h + 1)
            nc.vector.tensor_copy(line_out[:, h, :], PS[:, 4 + h, 0:LINE]).then_inc(line_taken, 1)
        dve.wait_ge(gain_loaded, 16)

        def xt_lo(s):
            for h in range(2):
                src = PS[:, (2 * s + h) % 8, :].rearrange("p (k t) -> p k t", k=4)[:, :, 0:rows(s)]
                dve.wait_ge(xt_hi_ready, 2 * s + h + 1)
                nc.vector.tensor_tensor(act_lo[:, 4 * h:4 * h + 4, cols(s)], src,
                                        act_hi[:, 4 * h:4 * h + 4, cols(s)].bitcast(F32),
                                        ALU.subtract).then_inc(xt_lo_ready, 1)
        for s in range(STEPS):
            r = rows(s)
            dve.wait_ge(rstd_ready, s + 1)
            if s >= 2:
                dve.wait_ge(xt_ready, 2 * (s - 1))
            nc.vector.scalar_tensor_tensor(x_nrm[0:r, s % 2, :], x_in[0:r, s % 3, :], rstd[0:r, s:s + 1],
                                           gain[0:r, :], ALU.mult, ALU.mult).then_inc(nrm_ready, 1)
            if s >= 1:
                xt_lo(s - 1)
            if s == 4:
                dve_split_w(dve, 0)
        xt_lo(STEPS - 1)
        dve.wait_ge(lam_exp_ready, 1)
        nc.vector.tensor_scalar(lam_dif, lam_exp[:, 1:2], LAM_INIT, None, ALU.subtract).then_inc(lam_step, 1)
        dve.wait_ge(lam_step, 4)
        nc.vector.tensor_tensor(neg_lam, lam_dif, lam_exp[:, 0:1], ALU.subtract).then_inc(lam_ready, 1)
        dve_split_w(dve, 1)
        dve.wait_ge(ws_hi_ready, 2)
        nc.vector.tensor_tensor(wsT_lo[:], wsT[:], wsT_hi[:].bitcast(F32), ALU.subtract).then_inc(ws_lo_ready, 1)
        nc.vector.tensor_tensor(wbT_lo[:], wbT[:], wbT_hi[:].bitcast(F32), ALU.subtract).then_inc(ws_lo_ready, 1)
        split = 1
        v_row = 0

        def layer_stats(s):
            r = rows(s)
            dve.wait_ge(act_took, STEPS + s + 1)
            nc.vector.bn_stats(scratch[0:r, 8 * s:8 * s + 6], va[0:r, s, :]).then_inc(dve_step, 1)
            own_step(dve, dve_step)
            nc.vector.bn_aggr(ln_mv[0:r, s, :], scratch[0:r, 8 * s:8 * s + 6]).then_inc(mv_ready, 1)

        def center(s):
            r = rows(s)
            dve.wait_ge(ln_rstd_ready, s + 1)
            nc.vector.tensor_scalar(va[0:r, s, :], va[0:r, s, :], ln_mv[0:r, s, 0:1], ln_rstd[0:r, s:s + 1],
                                    ALU.subtract, ALU.mult).then_inc(vc_ready, 1)

        for n, (kind, g, half, f, c) in enumerate(jobs):
            if g > split - 1 and g + 1 < len(GROUPS) and g + 1 > split:
                split = g + 1
                dve_split_w(dve, split)
                if g == 2:
                    for s in range(STEPS):
                        layer_stats(s)
                        if s >= 1:
                            center(s - 1)
                    center(STEPS - 1)
            if kind in ON_ACT:
                continue
            dve.wait_ge(job_ready, n + 1)
            if kind in ("q", "k"):
                w = KEPT[c].stop - KEPT[c].start
                dst = (qT if kind == "q" else kT)[:, 2 * half + f, KEPT[c]]
                nc.vector.tensor_copy(dst, PS[:, n % 8, 0:w]).then_inc(dve_took, 1)
            else:
                r = rows(c)
                if v_row >= 4:
                    dve.wait_ge(rows_stored[v_row % 4], 16 * (v_row // 4))
                nc.vector.tensor_copy(v_rows[0:r, v_row % 4, :], PS[0:r, n % 8, 0:GC]).then_inc(dve_took, 1)
                if c == STEPS - 1:
                    dve.wait_ge(dve_took, took[n][1])
                    nc.vector.tensor_copy(v_smp[0:NS, GC * half:GC * half + GC],
                                          v_rows[0:NS, v_row % 4, :]).then_inc(v_kept, 1)
                    dve.wait_ge(v_kept, half + 1)
                v_row += 1
        def gate_evict(s):
            w = rows(s)
            dve.wait_ge(gated, s + 1)
            b_of = bs[:] if s < STEPS - 1 else bs_smp[:].rearrange("p g b t -> p g (b t)")
            dve.wait_ge(gate_loaded, 16 * (4 + 2 * NB))
            if s >= 2:
                dve.wait_ge(gate_lo_ready, s - 1)
            ps = PS[:, 4 + s % 2, :].rearrange("p (g t) -> p g t", g=AG)[:, :, 0:w]
            nc.vector.tensor_tensor(g_sum[:, s % 2, :, 0:w], ps, b_of, ALU.add).then_inc(gate_sum, 1)
            dve.wait_ge(gate_sum, s + 1)
            nc.vector.tensor_tensor(g_sum[:, s % 2, :, 0:w], g_sum[:, s % 2, :, 0:w], uT[:, :, cols(s)],
                                    ALU.mult).then_inc(gate_mul, 1)

        def gate_lo(s):
            dve.wait_ge(gate_hi_ready, s + 1)
            nc.vector.tensor_tensor(act_lo[:, 4:8, cols(s)], g_sum[:, s % 2, :, 0:rows(s)],
                                    act_hi[:, 4:8, cols(s)].bitcast(F32), ALU.subtract).then_inc(gate_lo_ready, 1)
        for s in range(STEPS):
            r = rows(s)
            dve.wait_ge(vn_hi_ready, s + 1)
            nc.vector.tensor_tensor(vn_lo[0:r, s % 2, :], va[0:r, s, :], vn_hi[0:r, s % 2, :].bitcast(F32),
                                    ALU.subtract).then_inc(vn_lo_ready, 1)
            if s >= 1:
                gate_evict(s - 1)
            if s >= 2:
                gate_lo(s - 2)
        gate_evict(STEPS - 1)
        gate_lo(STEPS - 2)
        gate_lo(STEPS - 1)
        def split_lo(h):
            dve.wait_ge(qk_hi_ready, 2 * h + 1)
            nc.vector.scalar_tensor_tensor(q_lo[:, h % 2, :], qT[:, h, NS:], DH ** -0.5,
                                           q_hi[:, h % 2, :].bitcast(F32), ALU.mult, ALU.subtract).then_inc(qk_lo_ready, 1)
            dve.wait_ge(qk_hi_ready, 2 * h + 2)
            nc.vector.tensor_tensor(k_lo[:, h % 2, :], kT[:, h, NS:], k_hi[:, h % 2, :].bitcast(F32),
                                    ALU.subtract).then_inc(qk_lo_ready, 1)
            dve.wait_ge(v_hi_ready, h + 1)
            nc.vector.tensor_tensor(v_lo[:, h % 2], v_raw[:], v_hi[:, h % 2].bitcast(F32),
                                    ALU.subtract).then_inc(v_lo_ready, 1)

        def at_lo_part(i):
            n = i % QB + 1
            for t in range(turns(i)):
                dve.wait_ge(at_hi_ready, turns_before(i) + t + 1)
                w = slice(512 * t, min(512 * (t + 1), P * n))
                nc.vector.tensor_tensor(at_lo[:, w], PS[:, 4 + t, 0:w.stop - w.start], at_hi[:, w].bitcast(F32),
                                        ALU.subtract).then_inc(at_lo_ready, 1)

        def row_max(i):
            for m in range(2):
                dve.wait_ge(score_ready, 2 * i + m + 1)
                src = PS[:, 2 * m:2 * m + 2, :].rearrange("p a b -> p (a b)")[:, 0:P * (i % QB + 1)]
                nc.vector.tensor_reduce(nmax[:, i % 4, m:m + 1], src, AX.X, ALU.max, negate=True).then_inc(nmax_ready, 1)

        def mix(i):
            w = P * (i % QB + 1)
            dve.wait_ge(prob_ready, 2 * i + 2)
            if i >= 4:
                dve.wait_ge(ofac_ready, i - 3)
            nc.vector.reciprocal(precip[:, i % 4, :], psum_[:, i % 4, :]).then_inc(dve_step, 1)
            own_step(dve, dve_step)
            nc.vector.scalar_tensor_tensor(pcoef[:, i % 4:i % 4 + 1], precip[:, i % 4, 1:2], neg_lam,
                                           psum_[:, i % 4, 0:1], ALU.mult, ALU.mult).then_inc(dve_step, 1)
            own_step(dve, dve_step)
            nc.vector.scalar_tensor_tensor(prob[:, i % 2, 0, 0:w], prob[:, i % 2, 1, 0:w], pcoef[:, i % 4:i % 4 + 1],
                                           prob[:, i % 2, 0, 0:w], ALU.mult, ALU.add).then_inc(mix_ready, 1)

        def out_norm(i):
            dve.wait_ge(ofac_ready, i + 1)
            if i >= 2:
                dve.wait_ge(ot_ready, i - 1)
            nc.vector.scalar_tensor_tensor(o_nrm[:, i % 2, :], PS[:, 6, 0:DV], o_fac[:, i % 4:i % 4 + 1], sub_gain[:],
                                           ALU.mult, ALU.mult).then_inc(onrm_ready, 1)

        def out_lo(i):
            dve.wait_ge(ot_hi_ready, i + 1)
            dst = cols(i % QB)
            nc.vector.tensor_tensor(act_lo[:, i // QB, dst], PS[:, 7, 0:P], act_hi[:, i // QB, dst].bitcast(F32),
                                    ALU.subtract).then_inc(ot_lo_ready, 1)

        dve.wait_ge(bias_hi_ready, 1)
        nc.vector.tensor_tensor(bias_lo[:], bias_raw[:], bias_hi[:].bitcast(F32), ALU.subtract).then_inc(bias_lo_ready, 1)
        dve.wait_ge(lam_ready, 1)
        split_lo(0)
        for i in range(NSTEP + 4):
            if 0 <= i - 2 < NSTEP:
                at_lo_part(i - 2)
            if 0 <= i - 1 < NSTEP:
                mix(i - 1)
            if i < NSTEP:
                row_max(i)
            if 0 <= i - 2 < NSTEP:
                out_norm(i - 2)
            if 0 <= i - 3 < NSTEP:
                out_lo(i - 3)
            if i % QB == 4 and i // QB + 1 < H:
                split_lo(i // QB + 1)
        dve.wait_ge(sqk_hi_ready, 1)
        nc.vector.scalar_tensor_tensor(sq_lo[:], qT[:, :, 0:NS], DH ** -0.5, sq_hi[:].bitcast(F32),
                                       ALU.mult, ALU.subtract).then_inc(sqk_lo_ready, 1)
        dve.wait_ge(sqk_hi_ready, 2)
        nc.vector.tensor_tensor(sk_lo[:], kT[:, :, 0:NS], sk_hi[:].bitcast(F32), ALU.subtract).then_inc(sqk_lo_ready, 1)
        dve.wait_ge(sel_loaded, 32)
        nc.vector.scalar_tensor_tensor(row_coef, select_sb[:, 65:66], neg_lam, select_sb[:, 64:65], ALU.mult, ALU.add).then_inc(rowcoef_step, 1)
        nc.vector.tensor_scalar(gain_col, gain_col, 1.0 - LAM_INIT, None, ALU.mult).then_inc(rowcoef_step, 1)
        dve.wait_ge(ot_lo_ready, NSTEP)
        dve.wait_ge(ot_ready, NSTEP)
        nc.vector.memset(qp_hi[:].bitcast(F32), 0.0).then_inc(qp_zero, 1)
        nc.vector.memset(qp_lo[:].bitcast(F32), 0.0).then_inc(qp_zero, 1)
        nc.vector.memset(ones[:], 1.0).then_inc(qp_zero, 1)
        dve.wait_ge(qp_zero, 3)

        def kt_lo_part(n):
            u, p = n // 4, n % 4
            dve.wait_ge(kt_hi_ready, n + 1)
            src = PS[:, 3 + n % 2, :].rearrange("p (h t) -> p h t", h=H)
            w = slice(P * p, P * p + P)
            nc.vector.tensor_tensor(kt_lo[:, u % 2, :, w], src, kt_hi[:, u % 2, :, w].bitcast(F32), ALU.subtract).then_inc(kt_lo_ready, 1)

        def q_pad_lo(pr):
            if pr >= 1:
                dve.wait_ge(sscore_ready, 4 * pr)
            for m in range(2):
                d = slice(DH * m, DH * m + DH)
                dst = qp_lo[d, :].rearrange("p (b h c) -> p b h c", b=2, h=H)[:, :, :, DS * m:DS * m + DS]
                src = sq_lo[d, :, 16 * pr:16 * pr + 16].bitcast(F32).rearrange("p h (b q) -> p b h q", b=2)
                nc.vector.tensor_copy(dst, src).then_inc(qp_lo_ready, 1)

        def smp_softmax(pr):
            c = slice(pr, pr + 1)
            dve.wait_ge(sscore_ready, 4 * pr + 4)
            dve.wait_ge(sbias_loaded, 16 * 32)
            last_page = PS[:, 1, 384:512]
            nc.vector.tensor_tensor(last_page, last_page, smp_bias[:, 0:P], ALU.add)
            own = P + DS * (6 - 2 * pr)
            nc.vector.tensor_tensor(PS[:, 2, 0:NS], PS[:, 2, 0:NS], smp_bias[:, own:own + NS], ALU.add).then_inc(dve_step, 1)
            own_step(dve, dve_step)
            nc.vector.tensor_reduce(smp_max[:, c], PS[:, 0:3, :].rearrange("p a b -> p (a b)")[:, 0:SEQ + NS],
                                    AX.X, ALU.max, negate=True).then_inc(smax_ready, 1)
            dve.wait_ge(sprob_ready, pr + 1)
            nc.vector.reciprocal(smp_recip[:, c], smp_sum[:, c]).then_inc(dve_step, 1)
            own_step(dve, dve_step)
            dve.wait_ge(rowcoef_step, 2)
            nc.vector.tensor_tensor(smp_coef[:, c], smp_recip[:, c], row_coef, ALU.mult).then_inc(dve_step, 1)
            own_step(dve, dve_step)
            if pr >= 1:
                dve.wait_ge(sat_ready, pr)
            nc.vector.tensor_scalar(c_mat[:], select_sb[:, 0:NS], smp_coef[:, c], None, ALU.mult).then_inc(cmat_ready, 1)

        for u in range(2 * NB + 1):
            if u < 2 * NB:
                for p in range(4):
                    kt_lo_part(4 * u + p)
            if u % 4 == 0 and u < 2 * NB:
                q_pad_lo(u // 4)
            if u % 4 == 0 and u >= 4:
                smp_softmax(u // 4 - 1)
        dve.wait_ge(ssum_ready, 1)
        dve.wait_ge(sat_ready, NB // 2)
        nc.vector.tensor_scalar(s_ms[:], PS[:, 6, 0:H * NS], 1.0 / DV, SUBLN_EPS, ALU.mult, ALU.add).then_inc(smean_ready, 1)
        dve.wait_ge(srstd_ready, 1)
        nc.vector.scalar_tensor_tensor(s_out[:], PS[:, 7, 0:H * NS], gain_col, s_rs[:], ALU.mult, ALU.mult).then_inc(sout_ready, 1)
        dve.wait_ge(sout_hi_ready, 1)
        nc.vector.tensor_tensor(act_lo[:, 0:H, 0:NS], s_out[:].rearrange("p (h c) -> p h c", h=H),
                                act_hi[:, 0:H, 0:NS].bitcast(F32), ALU.subtract).then_inc(sout_lo_ready, 1)
        for k in range(KD):
            dve.wait_ge(wo_hi_ready, k + 1)
            nc.vector.tensor_tensor(wo_lo[:, k, :], wo_raw[:, k % 2, :], wo_hi[:, k, :].bitcast(F32), ALU.subtract).then_inc(wo_lo_ready, 1)
        dve.wait_ge(gain_loaded, 48)

        def x2_lo(t):
            for h in range(2):
                dve.wait_ge(xt_hi_ready, 2 * STEPS + 2 * t + h + 1)
                src = PS[:, 4 + (2 * t + h) % 4, :].rearrange("p (k t) -> p k t", k=4)[:, :, 0:rows(t)]
                dst = cols(t)
                nc.vector.tensor_tensor(act_lo[:, 4 * h:4 * h + 4, dst], src, act_hi[:, 4 * h:4 * h + 4, dst].bitcast(F32),
                                        ALU.subtract).then_inc(xt_lo_ready, 1)
        for t in range(STEPS + 1):
            if t < STEPS:
                r, j = rows(t), 2 * (t % 2)
                dve.wait_ge(yrstd_ready, t + 1)
                nc.vector.scalar_tensor_tensor(y_nrm[0:r, t % 2, :], PS[0:r, j:j + 2, :].rearrange("p a b -> p (a b)"),
                                               rstd2[0:r, t:t + 1], gain[0:r, :], ALU.mult, ALU.mult).then_inc(ynrm_ready, 1)
                dve.wait_ge(ynrm_ready, t + 1)
                dve.wait_ge(xres_loaded[t % 2], 16 * (t // 2 + 1))
                if t >= 2:
                    dve.wait_ge(xmid_stored[t % 2], 16 * (t // 2))
                    dve.wait_ge(nrm_ready, STEPS + t - 1)
                nc.vector.tensor_tensor(x_mid[0:r, t % 2, :], y_nrm[0:r, t % 2, :], x_res[0:r, t % 2, :], ALU.add).then_inc(xmid_ready, 1)
                dve.wait_ge(rstd_ready, STEPS + t + 1)
                if t >= 2:
                    dve.wait_ge(xt_ready, 2 * STEPS + 2 * (t - 1))
                nc.vector.scalar_tensor_tensor(x2_nrm[0:r, t % 2, :], x_mid[0:r, t % 2, :], rstd3[0:r, t:t + 1], gain2[0:r, :],
                                               ALU.mult, ALU.mult).then_inc(nrm_ready, 1)
            if t >= 1:
                x2_lo(t - 1)
        for q in range(6):
            dve.wait_ge(st_turned, q + 1)
            n = min(8, 2 * JF - 8 * q)
            nc.vector.tensor_copy(stT[:, 8 * q:8 * q + n], PS[:, q % 2, 0:16 * n].rearrange("p (j b r) -> p j b r", b=NB, r=2)).then_inc(st_taken, 1)
        dve.wait_ge(cw_turned, 1)
        nc.vector.tensor_copy(cw[:], PS[:, 2, 0:8 * JF].rearrange("p (w a j) -> p w a j", w=4, a=2)).then_inc(cw_taken, 1)

        def add_down(base, n):
            t, half = n // 2, n % 2
            r = rows(t)
            dve.wait_ge(down_ready, base + n + 1)
            dst = y_acc[0:r, t, 512 * half:512 * half + 512]
            nc.vector.tensor_tensor(dst, dst, PS[0:r, 6 + half, :], ALU.add).then_inc(ybank_free, 1)

        def ffn_dve(i, first, last):
            adds = iter(range(0 if first else YJ))

            def some_adds(t, most):
                if t == 1:
                    for _, n in zip(range(most), adds):
                        add_down(YJ * i - YJ, n)

            def split(t, ahead):
                dve.wait_ge(wu_hi_ready, 4 * i + t + ahead + 1)
                q = (t + ahead) % 2
                nc.vector.tensor_tensor(wu_lo[:, q], wu_raw[:, q], wu_hi[:, q].bitcast(F32), ALU.subtract).then_inc(wu_lo_ready, 1)

            if first:
                split(0, 0)
                split(1, 0)
            for t in range(4):
                e, half = t // 2, t % 2
                u = 4 * i + t
                h = h_sb[half]
                w1, w0 = cwi[:, 1, half, e:e + 1], cwi[:, 0, half, e:e + 1]
                some_adds(t, 1)
                dve.wait_ge(conv_ready, u + 1)
                nc.vector.scalar_tensor_tensor(conv[:, half, NS + 1:], h[:, NS:NTOK - 1], w1, conv[:, half, NS + 1:],
                                               ALU.mult, ALU.add).then_inc(tap1_ready, 1)
                some_adds(t, 1)
                nc.vector.tensor_copy(cpw[:, half, e, :], h[:, NTOK - 2:NTOK]).then_inc(tap1_ready, 1)
                dve.wait_ge(hs_ready, u + 1)
                smp_c = conv[:, half, 0:NS].rearrange("p (b q) -> p b q", b=NB)
                nc.vector.scalar_tensor_tensor(smp_c, hsw[:, half, e, :, 1:DS + 1], w1, smp_c, ALU.mult, ALU.add).then_inc(tap1_ready, 1)
                dve.wait_ge(tap1_ready, 3 * u + 3)
                nc.vector.scalar_tensor_tensor(smp_c, hsw[:, half, e, :, 0:DS], w0, smp_c, ALU.mult, ALU.add).then_inc(stap_ready, 1)
                dve.wait_ge(stap_ready, u + 1)
                nc.vector.scalar_tensor_tensor(conv[:, half, NS + 2:], h[:, NS:NTOK - 2], w0, conv[:, half, NS + 2:],
                                               ALU.mult, ALU.add).then_inc(tap_ready, 1)
                some_adds(t, 2)
                if not (last and t >= 2):
                    split(t, 2)
                some_adds(t, 2)
                if half == 1:
                    dve.wait_ge(silu_ready, 2 * i + e + 1)
                    dve.wait_ge(tap_ready, u + 1)
                    nc.vector.tensor_tensor(conv[:, 1, :], conv[:, 0, :], conv[:, 1, :], ALU.mult).then_inc(prod_ready, 1)
                    some_adds(t, YJ)
                    dve.wait_ge(g_hi_ready, 2 * i + e + 1)
                    nc.vector.tensor_tensor(g_lo[:, e, :], conv[:, 1, :], g_hi[:, e, :].bitcast(F32), ALU.subtract).then_inc(g_lo_ready, 1)
                    if t == 1:
                        for k in range(2):
                            dve.wait_ge(wd_hi_ready, 2 * i + k + 1)
                            nc.vector.tensor_tensor(wd_lo[:, k, :], wd_raw[:, k, :], wd_hi[:, k, :].bitcast(F32), ALU.subtract).then_inc(wd_lo_ready, 1)
        dve.wait_ge(xt_lo_ready, 2 * STEPS + 2 * STEPS)
        for bank in (6, 7):
            nc.vector.memset(PS[:, bank, :], 0.0).then_inc(ybank_free, 1)
        dve.wait_ge(yacc_zero, 1)
        iterations(dve, ffn_dve)
        dve.wait_ge(gain_loaded, 64)

        def final_norm(t):
            r = rows(t)
            dve.wait_ge(rstd_ready, 2 * STEPS + t + 1)
            nc.vector.scalar_tensor_tensor(y_acc[0:r, t, :], y_acc[0:r, t, :], rstd[0:r, t:t + 1], gain[0:r, :],
                                           ALU.mult, ALU.mult).then_inc(ynrm_ready, 1)

        def take_states(q):
            dve.wait_ge(st_turned, 6 + min(q, 6) + 1)
            if q < 6:
                n = min(8, 2 * JF - 8 * q)
                nc.vector.tensor_copy(st_nat[0:16 * n, q, :], PS[0:16 * n, q, 0:P]).then_inc(st_taken, 1)
            else:
                nc.vector.tensor_copy(cw_nat[:, 0:2, :], PS[0:2 * JF, 0, P:3 * P].rearrange("p (r c) -> p r c", r=2)).then_inc(st_taken, 1)
        for t in range(STEPS + 2):
            if t < STEPS:
                add_down(YJ * (NIT - 1), 2 * t)
                add_down(YJ * (NIT - 1), 2 * t + 1)
            if t >= 2:
                final_norm(t - 2)
            if 1 <= t < 8:
                take_states(t - 1)

    @block.tensor
    def _(pe):
        pe.wait_ge(const_ready, 4)
        for h in range(H):
            pe.wait_ge(rep_ready, h + 2)
            nc.tensor.matmul(PS[:, 4 + h, 0:LINE], rel_rep[:, h, :], lines_sb[:], start=True, stop=True).then_inc(line_ready, 1)
        for s in range(STEPS):
            pe.wait_ge(nrm_ready, s + 1)
            for h in range(2):
                j = 2 * s + h
                if j >= 8:
                    pe.wait_ge(xt_lo_ready, j - 7)
                if j == 4:
                    pe.wait_ge(line_taken, H)
                for k in range(4):
                    mm = nc.tensor.transpose(PS[:, j % 8, P * k:P * k + rows(s)],
                                             x_nrm[0:rows(s), s % 2, P * (4 * h + k):P * (4 * h + k + 1)],
                                             ident[0:rows(s), 0:rows(s)])
                mm.then_inc(xt_ready, 1)
        pe.wait_ge(gate_loaded, 16 * (4 + 2 * NB))
        pe.wait_ge(xt_lo_ready, 2 * STEPS)
        for i, (w, n) in enumerate(((ws_nat, P), (ws_bd, NS))):
            for g in range(AG):
                mm = nc.tensor.transpose(PS[0:n, 2 + i, n * g:n * g + n], w[:, g, :], ident[0:n, 0:n])
            mm.then_inc(ws_turned, 1)
        pe.wait_ge(ws_taken, 2)
        pe.wait_ge(pad_zero, 2)
        group = -1
        for n, (kind, g, half, f, c) in enumerate(jobs):
            if g != group and g < len(GROUPS):
                group = g
                pe.wait_ge(w_lo_ready, 2 * g + 2)
            if n >= 8:
                pe.wait_ge(*took[n - 8])
            if kind == "krow":
                if c == 0:
                    pe.wait_ge(*last_k_took)
                for h in range(H):
                    mm = nc.tensor.transpose(PS[0:rows(c), n % 8, P * h:P * h + P], kT[:, h, cols(c)], ident[:])
            else:
                if kind in ("va", "v"):
                    out, stat, mov = PS[:, n % 8, 0:GC], wide(c), slice(0, GC)
                    pairs = [(a[:, k, stat], w[:, g % 2, k, :]) for k in range(KD)
                             for a, w in ((act_hi, w_hi), (act_hi, w_lo), (act_lo, w_hi))]
                else:
                    out = PS[:, n % 8, 0:CW]
                    pairs = [(w[:, g % 2, k, P * f:P * f + P], a[:, k, CHUNKS[c]]) for k in range(KD)
                             for w, a in ((w_hi, act_hi), (w_hi, act_lo), (w_lo, act_hi))]
                for i, (lhs, rhs) in enumerate(pairs):
                    mm = nc.tensor.matmul(out, lhs, rhs, start=(i == 0), stop=(i == len(pairs) - 1))
            mm.then_inc(job_ready, 1)
        pe.wait_ge(ws_lo_ready, 2)
        for q in took[-8:]:
            pe.wait_ge(*q)
        for s in range(STEPS):
            r = rows(s)
            pe.wait_ge(vn_lo_ready, s + 1)
            if s >= 2:
                pe.wait_ge(gate_sum, s - 1)
            th, tl = (wsT_hi, wsT_lo) if s < STEPS - 1 else (wbT_hi, wbT_lo)
            for g in range(AG):
                vs = slice(P * g, P * g + P)
                for i, (a, w) in enumerate(((vn_hi, th), (vn_hi, tl), (vn_lo, th))):
                    mm = nc.tensor.matmul(PS[:, 4 + s % 2, P * g:P * g + r], a[0:r, s % 2, vs], w[:, g, :],
                                          start=(i == 0), stop=(i == 2))
            mm.then_inc(gated, 1)
        def scores(i):
            h, n = i // QB, i % QB + 1
            w = P * n
            if i == 0:
                pe.wait_ge(bias_lo_ready, 1)
            if i % QB == 0:
                pe.wait_ge(qk_lo_ready, 2 * h + 2)
            for m in range(2):
                if i >= 1:
                    pe.wait_ge(prob_ready, 2 * (i - 1) + m + 1)
                d = slice(DH * m, DH * m + DH)
                qs = slice(P * (n - 1), P * n)
                for c in range(0, w, 512):
                    e = min(c + 512, w)
                    out = PS[:, 2 * m + c // 512, :]
                    b0 = max(c, w - 2 * P)
                    for j, (a, b) in enumerate(((q_hi, k_hi), (q_hi, k_lo), (q_lo, k_hi))):
                        mm = nc.tensor.matmul(out[:, 0:e - c], a[d, h % 2, qs], b[d, h % 2, c:e],
                                              start=(j == 0), stop=(j == 2 and b0 >= e))
                    if b0 < e:
                        t = slice(b0 - (w - 2 * P), e - (w - 2 * P))
                        for j, b in enumerate((bias_hi, bias_lo)):
                            mm = nc.tensor.matmul(out[:, b0 - c:e - c], identr[:], b[:, h, t], start=False, stop=(j == 1))
                mm.then_inc(score_ready, 1)

        def turn(i):
            n = i % QB + 1
            pe.wait_ge(mix_ready, i + 1)
            if i >= 1:
                pe.wait_ge(at_lo_ready, turns_before(i))
            for t in range(turns(i)):
                for k in range(4 * t, min(4 * t + 4, n)):
                    mm = nc.tensor.transpose(PS[:, 4 + t, P * (k % 4):P * (k % 4) + P], prob[:, i % 2, 0, P * k:P * k + P], ident[:])
                mm.then_inc(turn_ready, 1)

        def weigh(i):
            h, n = i // QB, i % QB + 1
            pe.wait_ge(v_lo_ready, h + 1)
            pe.wait_ge(at_lo_ready, turns_before(i + 1))
            if i >= 1:
                pe.wait_ge(onrm_ready, i)
            parts = [(a, b, k) for k in range(n) for a, b in ((at_hi, v_hi), (at_hi, v_lo), (at_lo, v_hi))]
            for j, (a, b, k) in enumerate(parts):
                mm = nc.tensor.matmul(PS[:, 6, 0:DV], a[:, P * k:P * k + P], b[:, h % 2, k, :],
                                      start=(j == 0), stop=(j == len(parts) - 1))
            mm.then_inc(o_ready, 1)

        def turn_out(i):
            pe.wait_ge(onrm_ready, i + 1)
            if i >= 1:
                pe.wait_ge(ot_lo_ready, i)
            nc.tensor.transpose(PS[:, 7, 0:P], o_nrm[:, i % 2, :], ident[:]).then_inc(ot_ready, 1)

        pe.wait_ge(gate_sum, STEPS)
        for i in range(NSTEP + 4):
            if 0 <= i - 2 < NSTEP:
                weigh(i - 2)
            if i < NSTEP:
                scores(i)
            if 0 <= i - 3 < NSTEP:
                turn_out(i - 3)
            if 0 <= i - 1 < NSTEP:
                turn(i - 1)
        def turn_keys(u):
            pe.wait_ge(kp_loaded[u % 2], 64 * (u // 2 + 1))
            for p in range(4):
                n = 4 * u + p
                if n >= 2:
                    pe.wait_ge(kt_lo_ready, n - 1)
                for h in range(H):
                    mm = nc.tensor.transpose(PS[:, 3 + n % 2, P * h:P * h + P], kpage[:, n % 8, P * h:P * h + P], ident[:])
                mm.then_inc(kturn_ready, 1)

        def smp_scores(u):
            pr, b2, c = u // 4, u // 2 % 2, u % 2
            pe.wait_ge(kt_lo_ready, 4 * u + 4)
            pe.wait_ge(qp_lo_ready, 2 * pr + 2)
            pe.wait_ge(qp_hi_ready, 2 * pr + 2)
            if pr >= 1:
                pe.wait_ge(sprob_ready, pr)
            for h in range(H):
                n = 4 * b2 + h
                w = slice(P * n, P * n + P)
                for j, (a, b) in enumerate(((qp_hi, kt_hi), (qp_hi, kt_lo), (qp_lo, kt_hi))):
                    mm = nc.tensor.matmul(PS[:, c, :], a[:, w], b[:, u % 2, h, :], start=(n == 0 and j == 0), stop=(n == 7 and j == 2))
                if c == 1:
                    for j, (a, b) in enumerate(((qp_hi, sk_hi), (qp_hi, sk_lo), (qp_lo, sk_hi))):
                        mm = nc.tensor.matmul(PS[:, 2, 0:NS], a[:, w], b[:, h, :], start=(n == 0 and j == 0), stop=(n == 7 and j == 2))
            mm.then_inc(sscore_ready, 1)

        def smp_turn(pr):
            pe.wait_ge(cmat_ready, pr + 1)
            if pr >= 1:
                pe.wait_ge(sat_taken, 2 * pr)
            for p in range(NPAGE):
                nc.tensor.matmul(PS[:, 5, NS * p:NS * p + NS], s_prob[:, P * p:P * p + P], c_mat[:], start=True, stop=True)
            nc.tensor.matmul(PS[0:NS, 6, 0:NS], s_prob[:, SEQ:SEQ + NS], c_mat[:], start=True, stop=True).then_inc(sat_ready, 1)

        def smp_weigh(pr):
            pe.wait_ge(sat_taken, 2 * pr + 2)
            for b2 in range(2):
                b = 2 * pr + b2
                pe.wait_ge(vp_loaded[b % VR], 16 * NPAGE * (b // VR + 1))
                for h in range(H):
                    out = PS[:, 7, NS * h + DS * b:NS * h + DS * b + DS]
                    w = slice(P * h, P * h + P)
                    q = slice(DS * (4 * b2 + h), DS * (4 * b2 + h) + DS)
                    for p in range(NPAGE):
                        nc.tensor.matmul(out, vpage[:, b % VR, p, w], s_at[:, p, q], start=(p == 0), stop=False)
                    mm = nc.tensor.matmul(out, v_smp[0:NS, w], s_own[:, q], start=False, stop=True)
            mm.then_inc(pv_ready, 1)

        pe.wait_ge(sqk_lo_ready, 2)
        pe.wait_ge(at_lo_ready, turns_before(NSTEP))
        pe.wait_ge(ot_lo_ready, NSTEP)
        turn_keys(0)
        for u in range(2 * NB):
            if u + 1 < 2 * NB:
                turn_keys(u + 1)
            if u % 4 == 0 and u >= 4:
                smp_turn(u // 4 - 1)
            smp_scores(u)
            if u % 4 == 0 and u >= 4:
                smp_weigh(u // 4 - 1)
        smp_turn(NB // 2 - 1)
        smp_weigh(NB // 2 - 1)
        pe.wait_ge(ssq_s_ready, 1)
        pe.wait_ge(qp_zero, 3)
        nc.tensor.matmul(PS[:, 6, 0:H * NS], ones[:], s_sq[:], start=True, stop=True).then_inc(ssum_ready, 1)
        def turn_x2(t):
            pe.wait_ge(nrm_ready, STEPS + t + 1)
            for h in range(2):
                j = 2 * t + h
                if j >= 4:
                    pe.wait_ge(xt_lo_ready, 2 * STEPS + j - 3)
                for k in range(4):
                    mm = nc.tensor.transpose(PS[:, 4 + j % 4, P * k:P * k + rows(t)],
                                             x2_nrm[0:rows(t), t % 2, P * (4 * h + k):P * (4 * h + k + 1)],
                                             ident[0:rows(t), 0:rows(t)])
                mm.then_inc(xt_ready, 1)

        pe.wait_ge(sout_lo_ready, 1)
        pe.wait_ge(wo_lo_ready, KD)
        for t in range(STEPS):
            if t >= 2:
                pe.wait_ge(ynrm_ready, t - 1)
            if t == STEPS - 1:
                pe.wait_ge(xt_lo_ready, 2 * STEPS + 2)
            for half in range(2):
                parts = [(a, w, k) for k in range(KD) for a, w in ((act_hi, wo_hi), (act_hi, wo_lo), (act_lo, wo_hi))]
                for j, (a, w, k) in enumerate(parts):
                    mm = nc.tensor.matmul(PS[:, 2 * (t % 2) + half, :], a[:, k, wide(t)], w[:, k, 512 * half:512 * half + 512],
                                          start=(j == 0), stop=(j == len(parts) - 1))
            mm.then_inc(y_ready, 1)
            if t >= 1:
                turn_x2(t - 1)
        turn_x2(STEPS - 1)
        pe.wait_ge(xt_lo_ready, 2 * STEPS + 2 * STEPS)
        pe.wait_ge(st_loaded, 16 * 2 * JF)
        for q in range(6):
            n = min(8, 2 * JF - 8 * q)
            if q >= 2:
                pe.wait_ge(st_taken, q - 1)
            nc.tensor.transpose(PS[:, q % 2, 0:16 * n], st_nat[0:16 * n, q, :], ident[0:16 * n, 0:16 * n]).then_inc(st_turned, 1)
        pe.wait_ge(cw_loaded, 16 * 4)
        for w in range(4):
            mm = nc.tensor.transpose(PS[:, 2, 2 * JF * w:2 * JF * (w + 1)], cw_nat[:, w, :], ident[0:2 * JF, 0:2 * JF])
        mm.then_inc(cw_turned, 1)
        pe.wait_ge(st_taken, 6)
        pe.wait_ge(cw_taken, 1)

        def ffn_pe(i, first, last):
            for t in range(4):
                half = t % 2
                if t == 2 and not first:
                    down_share(i - 1)
                pe.wait_ge(wu_lo_ready, 4 * i + t + 1)
                if not first or t >= 2:
                    pe.wait_ge(h_ready, 4 * i + t - 1)
                    pe.wait_ge(hs_ready, 4 * i + t - 1)
                for c in range(3):
                    parts = [(a, b, k) for k in range(KD) for a, b in ((wu_hi, act_hi), (wu_hi, act_lo), (wu_lo, act_hi))]
                    for j, (a, b, k) in enumerate(parts):
                        mm = nc.tensor.matmul(PS[:, 3 * half + c, 0:CW], a[:, half, k, :], b[:, k, CHUNKS[c]],
                                              start=(j == 0), stop=(j == len(parts) - 1))
                mm.then_inc(up_ready, 1)

        def down_share(i):
            pe.wait_ge(g_lo_ready, 2 * i + 2)
            pe.wait_ge(wd_lo_ready, 2 * i + 2)
            for n in range(YJ):
                t, half = n // 2, n % 2
                pe.wait_ge(ybank_free, YJ * i + n + 1)
                parts = [(g, w, e) for e in range(2) for g, w in ((g_hi, wd_hi), (g_hi, wd_lo), (g_lo, wd_hi))]
                for j, (g, w, e) in enumerate(parts):
                    mm = nc.tensor.matmul(PS[:, 6 + half, :], g[:, e, wide(t)], w[:, e, 512 * half:512 * half + 512],
                                          start=(j == 0), stop=(j == len(parts) - 1))
                mm.then_inc(down_ready, 1)
        iterations(pe, ffn_pe)
        pe.wait_ge(cs_kept, 4 * NIT)
        for q in range(6):
            n = min(8, 2 * JF - 8 * q)
            nc.tensor.transpose(PS[0:16 * n, q, 0:P], stT[:, 8 * q:8 * q + n].rearrange("p j b r -> p (j b r)"), ident[:]).then_inc(st_turned, 1)
        for r in range(2):
            mm = nc.tensor.transpose(PS[0:2 * JF, 0, P * (r + 1):P * (r + 2)], cpT[:, :, r], ident[:])
        mm.then_inc(st_turned, 1)
        down_share(NIT - 1)


_INS = ["x_prompt", "x_sample", "cache_k", "cache_v", "state_conv", "page_table", "rel_bias",
        "norm_mix_pre", "norm_mix_post", "norm_ffn_pre", "norm_ffn_post", "w_in",
        "lambda_q1", "lambda_k1", "lambda_q2", "lambda_k2", "subln_gain", "sgu_ln_gain", "sgu_ln_bias",
        "w_spatial", "b_spatial", "w_out", "w_up", "conv_w", "conv_b", "w_down"]
_OUTS = [(1, SEQ, D), (NB, DS, D), (1, 1, SEQ, H, 2 * DH), (1, 1, SEQ, H, DV), (1, 1, 2, 2 * FF),
         (1, NB, DS, H, 2 * DH), (1, NB, DS, H, DV), (1, NB, 2, 2 * FF), (1, NB, DS, AW)]


def kernel(**inputs):
    import numpy as _np
    import concourse.bacc as _bacc
    from concourse import mybir as _mybir
    from concourse.bass_utils import run_bass_kernel_spmd as _run

    nc = _bacc.Bacc("TRN2", target_bir_lowering=False, num_devices=1)
    arrays, args = {}, []
    given = {name: _np.ascontiguousarray(inputs[name]) for name in _INS}
    given["lines"] = bucket_lines()
    given["select"] = sample_select()
    for name, a in given.items():
        arrays[f"in_{name}_dram"] = a
        args.append(nc.dram_tensor(f"in_{name}_dram", a.shape, _mybir.dt.from_np(a.dtype), kind="ExternalInput").ap())
    for i, shape in enumerate(_OUTS):
        args.append(nc.dram_tensor(f"out_{i}_dram", shape, _mybir.dt.float32, kind="ExternalOutput").ap())
    build(nc, *args)
    r = _run(nc, [arrays], core_ids=[0])
    return tuple(r.results[0][f"out_{i}_dram"] for i in range(len(_OUTS)))
```

```python
import math
from contextlib import ExitStack

import numpy as np

import concourse.bass as bass
from concourse import mybir

ALU = mybir.AluOpType
ACT = mybir.ActivationFunctionType
AX = mybir.AxisListType
F32 = mybir.dt.float32
F32R = mybir.dt.float32r
I32 = mybir.dt.int32

P = 128
D = 1024
KD = D // P
SEQ = 1024
QB = SEQ // P
NB, DS = 8, 8
NS = NB * DS
NTOK = NS + SEQ
CW = 364
NPAD = 3 * CW
STEPS = SEQ // P + 1
H, DH, DV = 4, 64, 128
PAGE, NPAGE = 128, 8
FF = 2816
JF = FF // P
AW = 512
AG = 4
EPS = 1e-6
SUBLN_EPS = 1e-5
LAM_INIT = 0.8 - 0.6 * math.exp(-0.3 * 0)
NEG = -1e30
BUCKETS, MAX_EXACT, MAX_DIST = 32, 16, 128
LINE = 3 * P - 1


def rows(s):
    return P if s < STEPS - 1 else NS


def cols(s):
    return slice(NS + P * s, NS + P * (s + 1)) if s < STEPS - 1 else slice(0, NS)


def wide(s):
    return cols(s) if s < STEPS - 1 else slice(0, P)


def bucket(dist):
    n = np.maximum(dist, 0)
    nf = np.maximum(n, 1).astype(np.float32)
    large = MAX_EXACT + (np.log(nf / np.float32(MAX_EXACT)) / np.float32(math.log(MAX_DIST / MAX_EXACT))
                         * np.float32(BUCKETS - MAX_EXACT)).astype(np.int32)
    return np.where(n < MAX_EXACT, n, np.minimum(large, BUCKETS - 1))


def bucket_lines():
    dist = 2 * P - 1 - np.arange(LINE)
    table = np.zeros((BUCKETS + 1, LINE), np.float32)
    for x, d in enumerate(dist):
        if d >= 0:
            table[bucket(d), x] += 1.0
            table[BUCKETS - 1, x] -= 1.0
        else:
            table[BUCKETS, x] = NEG
    return table


def sample_select():
    r = np.arange(P)
    b2h, m, q = r // 16, r // 8 % 2, r % 8
    table = np.zeros((P, 66), np.float32)
    table[r, b2h * 8 + q] = 1.0
    table[r, 64 + m] = 1.0
    return table


def build(nc, x_prompt, x_sample, cache_k, cache_v, state_conv, page_table, rel_bias,
          norm_mix_pre, norm_mix_post, norm_ffn_pre, norm_ffn_post, w_in,
          lambda_q1, lambda_k1, lambda_q2, lambda_k2, subln_gain, sgu_ln_gain, sgu_ln_bias,
          w_spatial, b_spatial, w_out, w_up, conv_w, conv_b, w_down,
          lines, select,
          y_prompt, y_sample, k_prompt, v_prompt, conv_prompt, k_sample, v_sample, conv_sample, sgu_v_sample):
    ctx = ExitStack()
    with ctx:
        _program(ctx, nc, **{k: v for k, v in locals().items() if k not in ("ctx", "nc")})


def _program(ctx, nc, x_prompt, x_sample, cache_k, cache_v, state_conv, page_table, rel_bias,
             norm_mix_pre, norm_mix_post, norm_ffn_pre, norm_ffn_post, w_in,
             lambda_q1, lambda_k1, lambda_q2, lambda_k2, subln_gain, sgu_ln_gain, sgu_ln_bias,
             w_spatial, b_spatial, w_out, w_up, conv_w, conv_b, w_down,
             lines, select,
             y_prompt, y_sample, k_prompt, v_prompt, conv_prompt, k_sample, v_sample, conv_sample, sgu_v_sample):
    BASE = 16512

    def at(name, offset, shape, dt=F32):
        return nc.alloc_sbuf_tensor_at(name, shape, dt, offset=BASE + offset)

    class Region:

        def __init__(self, start, end):
            self.at, self.end = start, end

        def put(self, name, shape, dt=F32):
            t = at(name, self.at, shape, dt)
            self.at += (int(np.prod(shape[1:])) * 4 + 31) // 32 * 32
            assert self.at <= self.end, (name, self.at, self.end)
            return t

    TOP = 212800
    ACT_BYTES = KD * NPAD * 4
    act_hi = at("act_hi", 0, [P, KD, NPAD], F32R)
    act_lo = at("act_lo", ACT_BYTES, [P, KD, NPAD], F32R)
    keep = Region(2 * ACT_BYTES, 2 * ACT_BYTES + 14000)
    ident = keep.put("ident", [P, P])
    identr = keep.put("identr", [P, P], F32R)
    gain = keep.put("gain", [P, D])
    sub_gain = keep.put("sub_gain", [P, DV])
    small = keep.put("small", [P, 256])
    neg_half = small[:, 0:1]
    ssq = small[:, 16:32]
    rstd = small[:, 32:48]
    mean_sq = small[:, 48:64]
    ln_mv = small[:, 64:96].rearrange("p (s c) -> p s c", c=2)
    ln_rstd = small[:, 96:112]
    lam_sum = small[:, 4:6]
    lam_exp = small[:, 6:8]
    lam_dif = small[:, 8:9]
    neg_lam = small[:, 9:10]
    nmax = small[:, 112:120].rearrange("p (i m) -> p i m", m=2)
    prob_sum = small[:, 120:128].rearrange("p (i m) -> p i m", m=2)
    precip = small[:, 128:136].rearrange("p (i m) -> p i m", m=2)
    pcoef = small[:, 136:140]
    o_ssq = small[:, 140:144]
    o_mean = small[:, 144:148]
    o_rstd = small[:, 148:152]
    o_fac = small[:, 152:156]
    row_coef = small[:, 156:157]
    s_mean = small[:, 240:242]
    s_rstd = small[:, 242:244]
    smp_max = small[:, 160:164]
    smp_sum = small[:, 164:168]
    smp_recip = small[:, 168:172]
    smp_coef = small[:, 172:176]
    gain_col = small[:, 176:177]
    ssq2 = small[:, 180:189]
    rstd2 = small[:, 190:199]
    mean_sq2 = small[:, 200:209]
    ssq3 = small[:, 210:219]
    rstd3 = small[:, 220:229]
    mean_sq3 = small[:, 230:239]
    SCRATCH = keep.at
    scratch = keep.put("scratch", [P, 512])
    v_smp = keep.put("v_smp", [P, AW])
    smp_bias = keep.put("smp_bias", [P, P + 14 * DS])
    select_sb = keep.put("select_sb", [P, 66])
    sq, sk = (at(n, 2 * ACT_BYTES + 1024 + 1024 * i, [P, H, NS]) for i, n in enumerate(("sq", "sk")))
    R0 = keep.at

    proj = Region(R0, TOP)
    qT = proj.put("qT", [P, H, NTOK])
    kT = proj.put("kT", [P, H, NTOK])
    R1 = proj.at
    uT = proj.put("uT", [P, AG, NTOK])
    va = proj.put("va", [P, STEPS, AW])
    R2 = proj.at
    v_all = at("v_all", R2 - STEPS * AW * 4, [P, STEPS, AW])
    GC = 256
    w_raw = proj.put("w_raw", [P, 2, 4, GC])
    w_hi = proj.put("w_hi", [P, 2, KD, GC], F32R)
    w_lo = proj.put("w_lo", [P, 2, KD, GC], F32R)
    norm = Region(R0, R1)
    x_in = norm.put("x_in", [P, 3, D])
    x_nrm = norm.put("x_nrm", [P, 2, D])
    junk = norm.put("junk", [P, D])
    ws_nat = norm.put("ws_nat", [P, AG, P])
    ws_bd = norm.put("ws_bd", [NS, AG, NS])
    gate = Region(proj.at, TOP)
    wsT = gate.put("wsT", [P, AG, P])
    wbT = gate.put("wbT", [NS, AG, NS])
    bs = gate.put("bs", [P, AG, P])
    bs_smp = gate.put("bs_smp", [P, AG, NB, DS])
    ln_g = gate.put("ln_g", [P, AW])
    ln_b = gate.put("ln_b", [P, AW])
    g_sum = gate.put("g_sum", [P, 2, AG, P])
    k_rows = gate.put("k_rows", [P, 2, AW])

    early = Region(R1, R2)
    rel_sb = early.put("rel_sb", [BUCKETS, H])
    rel_rep = early.put("rel_rep", [BUCKETS + 1, H, P])
    lines_sb = early.put("lines_sb", [BUCKETS + 1, LINE])
    line_out = early.put("line_out", [P, H, LINE])
    lam_in = early.put("lam_in", [P, 4, DH])
    lam_prod = early.put("lam_prod", [P, 2, DH])
    toeplitz = nc.dram_tensor("toeplitz", [H, P, LINE], F32)
    att = Region(R2, TOP)
    bias_raw = at("bias_raw", att.at, [P, H, 2 * P])
    prob = att.put("prob", [P, 2, 2, SEQ])
    at_sb = att.put("at_sb", [P, 2, SEQ])
    o_nrm = att.put("o_nrm", [P, QB, DV])
    bias_hi = att.put("bias_hi", [P, H, 2 * P], F32R)
    bias_lo = att.put("bias_lo", [P, H, 2 * P], F32R)
    V_BYTES = NPAGE * 512 * 4
    kpage = at("kpage", R1, [P, 8, 512])
    pages = at("pages", TOP - V_BYTES - 256, [1, NB * NPAGE], I32)
    assert att.at <= TOP - V_BYTES - 256 and 8 * 512 * 4 <= AG * NTOK * 4
    VR = 3

    qk_place = Region(R0, R1)
    kt = qk_place.put("kt", [P, 2, H, 512])
    vpage = [at("vpage0", TOP - V_BYTES, [P, NPAGE, 512]), qk_place.put("vpage1", [P, NPAGE, 512])]
    s_at = qk_place.put("s_at", [P, NPAGE, NS])
    W_OUT = TOP - V_BYTES - 256 - KD * D * 4
    wo_raw = at("wo_raw", W_OUT, [P, KD, D])
    smp = Region(R1 + 8 * 512 * 4, W_OUT)
    vpage.append(smp.put("vpage2", [P, NPAGE, 512]))
    QPAD = 8 * 144
    qp = smp.put("qp", [P, QPAD])
    c_mat = smp.put("c_mat", [P, NS])
    s_own = smp.put("s_own", [NS, NS])
    ones = smp.put("ones", [P, P])
    o_rows = smp.put("o_rows", [DS * H, 512])
    tail = Region(smp.at, W_OUT)
    s_prob = smp.put("s_prob", [P, SEQ + NS])
    s_sq = tail.put("s_sq", [P, H * NS])
    s_rs = tail.put("s_rs", [P, 2, P])
    s_fac = tail.put("s_fac", [P, H * NS])
    s_out = tail.put("s_out", [P, H * NS])
    prj = Region(R0, W_OUT)
    wo_hi = prj.put("wo_hi", [P, KD, D], F32R)
    wo_lo = prj.put("wo_lo", [P, KD, D], F32R)
    x_res = prj.put("x_res", [P, 2, D])
    top = Region(TOP - V_BYTES - 256, TOP)
    y_nrm = top.put("y_nrm", [P, 2, D])
    x_mid = top.put("x_mid", [P, 2, D])
    split_place = Region(W_OUT, top.at)
    x2_nrm = split_place.put("x2_nrm", [P, 2, D])
    junk2 = split_place.put("junk2", [P, D])
    gain2 = split_place.put("gain2", [P, D])
    AHEAD = split_place.at
    wu_raw = split_place.put("wu_raw", [P, 2, KD, P])
    st_nat = split_place.put("st_nat", [P, 6, P])
    cw_nat = split_place.put("cw_nat", [2 * JF, 4, P])
    assert split_place.at <= TOP - V_BYTES - 256
    mid_dram = nc.dram_tensor("mid_dram", [STEPS, P, D], F32)
    ffn = Region(R0, AHEAD)
    ffn2 = Region(split_place.at, TOP)
    y_acc = ffn.put("y_acc", [P, STEPS, D])
    W0 = ffn.at
    wu_hi = ffn.put("wu_hi", [P, 2, KD, P], F32R)
    wu_lo = ffn.put("wu_lo", [P, 2, KD, P], F32R)
    x_back = at("x_back", W0, [P, 3, D])
    wd_raw = ffn.put("wd_raw", [P, 2, D])
    wd_hi = ffn.put("wd_hi", [P, 2, D], F32R)
    wd_lo = ffn.put("wd_lo", [P, 2, D], F32R)
    g_hi = ffn2.put("g_hi", [P, 2, NTOK], F32R)
    g_lo = ffn.put("g_lo", [P, 2, NTOK], F32R)
    conv = ffn2.put("conv", [P, 2, NTOK])
    stT = ffn.put("stT", [P, 48, NB, 2])
    cpT = ffn.put("cpT", [P, 2 * JF, 2])
    cw = ffn.put("cw", [P, 4, 2, JF])
    cwi = ffn.put("cwi", [P, 4, 2, 2])
    hsw = ffn.put("hsw", [P, 2, 2, NB, 2 + DS])
    cpw = ffn.put("cpw", [P, 2, 2, 2])
    h_sb = [ffn.put("h_gate", [P, NPAD]), at("h_up", SCRATCH, [P, NPAD])]

    PS = ctx.enter_context(nc.psum_tensor("PS", [P, 8, 512], F32))

    def sem(name):
        return ctx.enter_context(nc.semaphore(name))

    dve_step, pool_step = sem("dve_step"), sem("pool_step")
    steps = {id(dve_step): 0, id(pool_step): 0}

    def own_step(eng, step):
        steps[id(step)] += 1
        eng.wait_ge(step, steps[id(step)])

    x_loaded = [sem(f"x_loaded{i}") for i in range(3)]
    gain_loaded = sem("gain_loaded")
    const_ready = sem("const_ready")
    ssq_ready = sem("ssq_ready")
    rstd_ready = sem("rstd_ready")
    nrm_ready = sem("nrm_ready")
    xt_ready = sem("xt_ready")
    xt_hi_ready = sem("xt_hi_ready")
    xt_lo_ready = sem("xt_lo_ready")
    w_loaded = [sem(f"w_loaded{i}") for i in range(2)]
    w_hi_ready = sem("w_hi_ready")
    w_lo_ready = sem("w_lo_ready")
    job_ready = sem("job_ready")
    act_took = sem("act_took")
    dve_took = sem("dve_took")
    rows_stored = sem("rows_stored")
    mv_ready = sem("mv_ready")
    ln_rstd_ready = sem("ln_rstd_ready")
    vc_ready = sem("vc_ready")
    vn_ready = sem("vn_ready")
    gate_loaded = sem("gate_loaded")
    krow_stored = [sem(f"krow_stored{i}") for i in range(2)]
    v_kept = sem("v_kept")
    bd_zero = sem("bd_zero")
    pad_zero = sem("pad_zero")
    ws_turned = sem("ws_turned")
    ws_taken = sem("ws_taken")
    ws_cut = sem("ws_cut")
    gate_mul = sem("gate_mul")
    gate_hi_ready = sem("gate_hi_ready")
    gate_lo_ready = sem("gate_lo_ready")
    sgu_stored = sem("sgu_stored")
    setup_loaded = sem("setup_loaded")
    rep_ready = sem("rep_ready")
    line_ready = sem("line_ready")
    line_taken = sem("line_taken")
    line_stored = sem("line_stored")
    lam_step = sem("lam_step")
    lam_exp_ready = sem("lam_exp_ready")
    lam_ready = sem("lam_ready")
    bias_loaded = sem("bias_loaded")
    bias_hi_ready = sem("bias_hi_ready")
    bias_lo_ready = sem("bias_lo_ready")
    score_ready = sem("score_ready")
    nmax_ready = sem("nmax_ready")
    prob_ready = sem("prob_ready")
    mix_ready = sem("mix_ready")
    turn_ready = sem("turn_ready")
    o_ready = sem("o_ready")
    osq_ready = sem("osq_ready")
    ofac_ready = sem("ofac_ready")
    onrm_ready = sem("onrm_ready")
    ot_ready = sem("ot_ready")
    ot_hi_ready = sem("ot_hi_ready")
    ot_lo_ready = sem("ot_lo_ready")

    x_tiles = [x_prompt[0, P * s:P * (s + 1), :] for s in range(STEPS - 1)] + \
              [x_sample.rearrange("b t d -> (b t) d")]
    v_out = [v_prompt[0, 0, P * s:P * (s + 1)].rearrange("t h d -> t (h d)") for s in range(STEPS - 1)] + \
            [v_sample[0].rearrange("b t h d -> (b t) (h d)")]
    k_out = [k_prompt[0, 0, P * s:P * (s + 1)].rearrange("t h d -> t (h d)") for s in range(STEPS - 1)] + \
            [k_sample[0].rearrange("b t h d -> (b t) (h d)")]

    QC, KC, VC, UC, AC = 0, 512, 1024, 1536, 2048
    GROUPS = [("va", 0), ("va", 1), ("u", 0), ("u", 1), ("k", 0), ("k", 1), ("q", 0), ("q", 1), ("v", 0), ("v", 1)]
    W_COL = {"va": AC, "u": UC, "k": KC, "q": QC, "v": VC}
    CHUNKS = [slice(CW * c, CW * (c + 1)) for c in range(3)]
    KEPT = [slice(CW * c, min(CW * (c + 1), NTOK)) for c in range(3)]
    jobs = []
    for g, (kind, half) in enumerate(GROUPS):
        if kind in ("va", "v"):
            jobs += [(kind, g, half, 0, s) for s in range(STEPS)]
        else:
            jobs += [(kind, g, half, f, c) for f in range(2) for c in range(3)]
    plan = list(jobs)
    jobs = []
    gates, krows = iter(range(STEPS)), iter(range(STEPS))
    for job in plan:
        jobs.append(job)
        if job[0] == "k":
            jobs += [("gate", job[1], 0, 0, s) for _, s in zip(range(1), gates)]
        if job[0] == "q":
            jobs += [("krow", job[1], 0, 0, s) for _, s in zip(range(1), krows)]
    ON_ACT = ("va", "u", "krow")
    took = []
    n_act = n_dve = 0
    for job in jobs:
        if job[0] in ON_ACT:
            n_act += 1
            took.append((act_took, n_act))
        else:
            n_dve += 1
            took.append((dve_took, n_dve))
    first_of = {}
    for n, job in enumerate(jobs):
        first_of.setdefault(job[1], n)
    last_k_took = max(took[n][1] for n, job in enumerate(jobs) if job[0] == "k")
    last_gate = max(n for n, job in enumerate(jobs) if job[0] == "gate")
    n_u_done = max(took[n][1] for n, job in enumerate(jobs) if job[0] == "u")

    NSTEP = H * QB

    OB = 4

    def turns(i):
        return (i % QB + 4) // 4

    def turns_before(i):
        return sum(turns(j) for j in range(i))

    sbias_loaded = sem("sbias_loaded")
    sbias_zero = sem("sbias_zero")
    sel_loaded = sem("sel_loaded")
    page_loaded = sem("page_loaded")
    kp_loaded = [sem(f"kp_loaded{i}") for i in range(2)]
    vp_loaded = [sem(f"vp_loaded{i}") for i in range(3)]
    qp_zero = sem("qp_zero")
    at_taken = sem("at_taken")
    sqk_ready = sem("sqk_ready")
    qp_ready = sem("qp_ready")
    kt_ready = [sem(f"kt_ready{i}") for i in range(2)]
    sdiag_ready = sem("sdiag_ready")
    orows_ready = sem("orows_ready")
    osel_ready = sem("osel_ready")
    wo_loaded = sem("wo_loaded")
    sfac_ready = sem("sfac_ready")
    kturn_ready = sem("kturn_ready")
    sscore_ready = sem("sscore_ready")
    smax_ready = sem("smax_ready")
    sprob_ready = sem("sprob_ready")
    cmat_ready = sem("cmat_ready")
    sat_ready = sem("sat_ready")
    sat_taken = sem("sat_taken")
    pv_ready = sem("pv_ready")
    ssq_s_ready = sem("ssq_s_ready")
    ssum_ready = sem("ssum_ready")
    smean_ready = sem("smean_ready")
    srstd_ready = sem("srstd_ready")
    sout_ready = sem("sout_ready")
    sout_hi_ready = sem("sout_hi_ready")
    sout_lo_ready = sem("sout_lo_ready")
    rowcoef_step = sem("rowcoef_step")
    wo_hi_ready = sem("wo_hi_ready")
    wo_lo_ready = sem("wo_lo_ready")
    xres_loaded = [sem(f"xres_loaded{i}") for i in range(2)]
    y_ready = sem("y_ready")
    yssq_ready = sem("yssq_ready")
    yrstd_ready = sem("yrstd_ready")
    ynrm_ready = sem("ynrm_ready")
    xmid_ready = sem("xmid_ready")
    xmid_stored = [sem(f"xmid_stored{i}") for i in range(2)]
    st_loaded = sem("st_loaded")
    cw_loaded = sem("cw_loaded")
    st_turned = sem("st_turned")
    st_taken = sem("st_taken")
    cw_turned = sem("cw_turned")
    cw_taken = sem("cw_taken")
    yacc_zero = sem("yacc_zero")
    cwi_ready = sem("cwi_ready")
    hsp_ready = sem("hsp_ready")
    wu_hi_ready = sem("wu_hi_ready")
    wu_lo_ready = sem("wu_lo_ready")
    wd_loaded = [sem(f"wd_loaded{i}") for i in range(2)]
    wd_hi_ready = sem("wd_hi_ready")
    wd_lo_ready = sem("wd_lo_ready")
    up_ready = sem("up_ready")
    conv_ready = sem("conv_ready")
    tap1_ready = sem("tap1_ready")
    tap_ready = sem("tap_ready")
    stap_ready = sem("stap_ready")
    h_ready = sem("h_ready")
    hs_ready = sem("hs_ready")
    silu_ready = sem("silu_ready")
    prod_ready = sem("prod_ready")
    g_hi_ready = sem("g_hi_ready")
    g_lo_ready = sem("g_lo_ready")
    down_ready = sem("down_ready")
    ybank_free = sem("ybank_free")
    cs_kept = sem("cs_kept")
    cs_stored = sem("cs_stored")
    fout_ready = sem("fout_ready")
    y_stored = sem("y_stored")

    OUT_BASE = 16 * len(GROUPS)
    UP_BASE = OUT_BASE

    NIT = JF // 2
    YJ = 2 * STEPS

    block = ctx.enter_context(nc.Block())

    def iterations(eng, body):
        body(0, True, False)
        with eng.Fori(1, NIT - 1) as i:
            body(i, False, False)
        body(NIT - 1, False, True)

    def load_smp_bias(eng):
        eng.wait_ge(line_stored, 16)
        eng.wait_ge(sbias_zero, 1)
        for b2 in range(2):
            for h in range(H):
                for m in range(2):
                    r = 64 * b2 + 16 * h + 8 * m
                    base = h * P * LINE + P - 1
                    eng.dma_start(smp_bias[r:r + 8, 0:P], bass.AP(toeplitz, base, [[LINE - 1, 8], [1, P]])).then_inc(sbias_loaded, 16)
                    c = P + DS * (6 + b2)
                    eng.dma_start(smp_bias[r:r + 8, c:c + DS],
                                  bass.AP(toeplitz, base + P, [[LINE - 1, 8], [1, DS]])).then_inc(sbias_loaded, 16)

    def load_w(sp, p):
        kind, half = GROUPS[p // 2]
        c0 = W_COL[kind] + GC * half
        src = w_in[0, 512 * (p % 2):512 * (p % 2 + 1), c0:c0 + GC].rearrange("(k p) c -> p k c", p=P)
        sp.dma_start(w_raw[:, p % 2], src).then_inc(w_loaded[p % 2], 16)

    def act_split_w(act, g):
        for p in (2 * g, 2 * g + 1):
            act.wait_ge(w_loaded[p % 2], 16 * (p // 2 + 1))
            if g >= 2:
                act.wait_ge(job_ready, first_of[g - 1])
            nc.scalar.copy(w_hi[:, g % 2, 4 * (p % 2):4 * (p % 2) + 4, :], w_raw[:, p % 2]).then_inc(w_hi_ready, 1)

    def dve_split_w(dve, g):
        for p in (2 * g, 2 * g + 1):
            ks = slice(4 * (p % 2), 4 * (p % 2) + 4)
            dve.wait_ge(w_hi_ready, p + 1)
            nc.vector.tensor_tensor(w_lo[:, g % 2, ks, :], w_raw[:, p % 2], w_hi[:, g % 2, ks, :].bitcast(F32),
                                    ALU.subtract).then_inc(w_lo_ready, 1)

    @block.sync
    def _(sp):
        sp.dma_start(rel_sb[:], rel_bias[:, :]).then_inc(setup_loaded, 16)
        sp.dma_start(lines_sb[:], lines[:, :]).then_inc(setup_loaded, 16)
        sp.dma_start(gain[:], norm_mix_pre[0:1, :].to_broadcast([P, D])).then_inc(gain_loaded, 16)
        for s in range(STEPS):
            if s >= 3:
                sp.wait_ge(nrm_ready, s - 2)
            sp.dma_start(x_in[0:rows(s), s % 3, :], x_tiles[s]).then_inc(x_loaded[s % 3], 16)
            if s == 2:
                for p in range(2):
                    load_w(sp, p)
        for p in range(2, 2 * len(GROUPS)):
            sp.wait_ge(w_lo_ready, p - 1)
            load_w(sp, p)
        load_smp_bias(sp)
        sp.dma_start(select_sb[:], select[:, :]).then_inc(sel_loaded, 16)
        sp.dma_start(gain_col, subln_gain.rearrange("a d -> d a")).then_inc(sel_loaded, 16)
        v_jobs = [n for n, job in enumerate(jobs) if job[0] == "v"]
        for i, n in enumerate(v_jobs):
            kind, g, half, f, s = jobs[n]
            if half == 1:
                sp.wait_ge(*took[n])
                sp.dma_start(v_out[s], v_all[0:rows(s), s, :]).then_inc(rows_stored, 16)
        sp.wait_ge(dve_took, n_dve)
        for i in range(2):
            sp.wait_ge(krow_stored[i], 16 * ((STEPS + 1 - i) // 2))
        skewed = bass.AP(toeplitz, P - 1, [[LINE - 1, P], [P * LINE, H], [1, 2 * P]])
        sp.dma_start(bias_raw[:], skewed).then_inc(bias_loaded, 16)
        sp.dma_start(pages[:], page_table.rearrange("b n -> (b n)").rearrange("(a n) -> a n", a=1)).then_inc(page_loaded, 16)
        sp.wait_ge(page_loaded, 16)
        sp.wait_ge(gate_lo_ready, 1)
        n_pool = cache_k.shape[1]

        def load_keys(b):
            for p in range(NPAGE):
                if b >= 1:
                    sp.wait_ge(kturn_ready, NPAGE * (b - 1) + p + 1)
                page = sp.value_load(pages[0:1, NPAGE * b + p:NPAGE * b + p + 1], min_val=0, max_val=n_pool - 1)
                sp.dma_start(kpage[:, p, :], cache_k[0, bass.ds(page, 1)].rearrange("a t h d -> t (a h d)")).then_inc(kp_loaded[p // 4], 16)

        def load_values(b):
            if b >= VR:
                sp.wait_ge(pv_ready, b - VR + 1)
            elif b == 1:
                sp.wait_ge(ot_ready, NSTEP // OB)
                sp.wait_ge(rows_stored, 16 * STEPS)
            for p in range(NPAGE):
                page = sp.value_load(pages[0:1, NPAGE * b + p:NPAGE * b + p + 1], min_val=0, max_val=n_pool - 1)
                sp.dma_start(vpage[b % VR][:, p, :], cache_v[0, bass.ds(page, 1)].rearrange("a t h d -> t (a h d)")).then_inc(vp_loaded[b % VR], 16)
        load_keys(0)
        load_values(0)
        for b in range(1, NB):
            load_keys(b)
            if b >= 2:
                load_values(b - 1)
            if b == 4:
                for k in range(KD):
                    if k == 0:
                        sp.wait_ge(v_kept, 2)
                    sp.dma_start(wo_raw[:, k, :], w_out[0, P * k:P * k + P, :]).then_inc(wo_loaded, 16)
        load_values(NB - 1)
        sp.wait_ge(sout_lo_ready, 1)
        sp.dma_start(gain[:], norm_mix_post[0:1, :].to_broadcast([P, D])).then_inc(gain_loaded, 16)
        sp.wait_ge(wo_lo_ready, KD)
        sp.dma_start(gain2[:], norm_ffn_pre[0:1, :].to_broadcast([P, D])).then_inc(gain_loaded, 16)
        for t in range(STEPS + 1):
            if t < STEPS:
                if t >= 2:
                    sp.wait_ge(xmid_ready, t - 1)
                sp.dma_start(x_res[0:rows(t), t % 2, :], x_tiles[t]).then_inc(xres_loaded[t % 2], 16)
            if t >= 1:
                sp.wait_ge(xmid_ready, t)
                sp.dma_start(mid_dram[t - 1, 0:rows(t - 1), :], x_mid[0:rows(t - 1), (t - 1) % 2, :]).then_inc(xmid_stored[(t - 1) % 2], 16)
            if t == 0:
                for q in range(6):
                    for j in range(8 * q, min(8 * q + 8, 2 * JF)):
                        sp.dma_start(st_nat[16 * (j % 8):16 * (j % 8) + 16, q, :],
                                     state_conv[0].rearrange("b r c -> (b r) c")[:, P * j:P * j + P]).then_inc(st_loaded, 16)
                for w in range(3):
                    sp.dma_start(cw_nat[:, w, :], conv_w[0, w].rearrange("(j c) -> j c", c=P)).then_inc(cw_loaded, 16)
                sp.dma_start(cw_nat[:, 3, :], conv_b[0].rearrange("(j c) -> j c", c=P)).then_inc(cw_loaded, 16)
                for e in range(2):
                    sp.dma_start(wu_raw[:, e], w_up[0, :, FF * e:FF * e + P].rearrange("(k p) c -> p k c", p=P)).then_inc(w_loaded[e], 16)
        sp.wait_ge(xt_lo_ready, 2 * STEPS + 2 * STEPS)
        for i in range(2):
            sp.wait_ge(xmid_stored[i], 16 * ((STEPS + 1 - i) // 2))
        sp.dma_start(gain[:], norm_ffn_post[0:1, :].to_broadcast([P, D])).then_inc(gain_loaded, 16)

        def load_ffn(i, first, last):
            for t in range(2 if first else 0, 4):
                sp.wait_ge(wu_lo_ready, 4 * i + t - 1)
                c0 = (t % 2) * FF + P * (t // 2) + 2 * P * i
                src = w_up[0, :, bass.ds(c0, P)].rearrange("(k p) c -> p k c", p=P)
                sp.dma_start(wu_raw[:, t % 2], src).then_inc(w_loaded[t % 2], 16)
            for e in range(2):
                if not first:
                    sp.wait_ge(wd_lo_ready, 2 * i + e - 1)
                sp.dma_start(wd_raw[:, e, :], w_down[0, bass.ds(2 * P * i + P * e, P), :]).then_inc(wd_loaded[e], 16)
        iterations(sp, load_ffn)
        sp.wait_ge(up_ready, 4 * NIT)
        for t in range(STEPS + 1):
            if t < STEPS:
                if t >= 3:
                    sp.wait_ge(fout_ready, t - 2)
                sp.dma_start(x_back[0:rows(t), t % 3, :], mid_dram[t, 0:rows(t), :]).then_inc(x_loaded[t % 3], 16)
            if t >= 1:
                sp.wait_ge(fout_ready, t)
                dst = y_prompt[0, P * (t - 1):P * t, :] if t < STEPS else y_sample.rearrange("b t d -> (b t) d")
                sp.dma_start(dst, y_acc[0:rows(t - 1), t - 1, :]).then_inc(y_stored, 16)
        for q in range(6):
            sp.wait_ge(st_taken, 6 + q + 1)
            for j in range(8 * q, min(8 * q + 8, 2 * JF)):
                sp.dma_start(conv_sample[0].rearrange("b r c -> (b r) c")[:, P * j:P * j + P],
                             st_nat[16 * (j % 8):16 * (j % 8) + 16, q, :]).then_inc(cs_stored, 16)
        sp.wait_ge(st_taken, 6 + 7)
        sp.dma_start(conv_prompt[0, 0].rearrange("r (j c) -> j r c", c=P), cw_nat[:, 0:2, :]).then_inc(cs_stored, 16)
        sp.wait_ge(cs_stored, 16 * (2 * JF + 1))
        sp.wait_ge(y_stored, 16 * STEPS)

    @block.scalar
    def _(act):
        for i, lam in enumerate((lambda_q1, lambda_q2, lambda_k1, lambda_k2)):
            act.dma_start(lam_in[:, i, :], lam[0:1, :].to_broadcast([P, DH])).then_inc(setup_loaded, 16)
        act.dma_start(sub_gain[:], subln_gain[0:1, :].to_broadcast([P, DV])).then_inc(setup_loaded, 16)
        act.dma_start(ws_nat[:], w_spatial[0].rearrange("g t s -> t g s")).then_inc(gate_loaded, 16)
        act.dma_start(bs[:], b_spatial[0:1].to_broadcast([P, AG, P])).then_inc(gate_loaded, 16)
        act.dma_start(ln_g[:], sgu_ln_gain[0:1, :].to_broadcast([P, AW])).then_inc(gate_loaded, 16)
        act.dma_start(ln_b[:], sgu_ln_bias[0:1, :].to_broadcast([P, AW])).then_inc(gate_loaded, 16)
        act.wait_ge(bd_zero, 1)
        for b in range(NB):
            o = slice(DS * b, DS * (b + 1))
            act.dma_start(ws_bd[o, :, o], w_spatial[0, :, 0:DS, 0:DS].rearrange("g t s -> t g s")).then_inc(gate_loaded, 16)
            act.dma_start(bs_smp[:, :, b, :], b_spatial[0:1, :, 0:DS].to_broadcast([P, AG, DS])).then_inc(gate_loaded, 16)
        def xt_hi(s):
            for h in range(2):
                act.wait_ge(xt_ready, 2 * s + h + 1)
                src = PS[:, (2 * s + h) % 8, :].rearrange("p (k t) -> p k t", k=4)[:, :, 0:rows(s)]
                nc.scalar.copy(act_hi[:, 4 * h:4 * h + 4, cols(s)], src).then_inc(xt_hi_ready, 1)
        act.wait_ge(line_taken, H)
        act.dma_start(bass.AP(toeplitz, 0, [[LINE, P], [P * LINE, H], [1, LINE]]), line_out[:]).then_inc(line_stored, 16)
        for s in range(STEPS):
            act.wait_ge(x_loaded[s % 3], 16 * (s // 3 + 1))
            if s >= 1:
                act.wait_ge(ssq_ready, s)
            nc.scalar.activation(junk[0:rows(s), :], x_in[0:rows(s), s % 3, :], ACT.Square,
                                 accum_out=ssq[0:rows(s), s:s + 1]).then_inc(ssq_ready, 1)
            if s >= 1:
                xt_hi(s - 1)
            if s == 3:
                act_split_w(act, 0)
        xt_hi(STEPS - 1)
        act.wait_ge(lam_step, 3)
        nc.scalar.activation(lam_exp, lam_sum, ACT.Exp).then_inc(lam_exp_ready, 1)
        act.wait_ge(ws_turned, 1)
        nc.scalar.copy(wsT[:], PS[:, 2, :].rearrange("p (g t) -> p g t", g=AG)).then_inc(ws_taken, 1)
        act.wait_ge(ws_turned, 2)
        nc.scalar.copy(wbT[:], PS[0:NS, 3, 0:AG * NS].rearrange("p (g t) -> p g t", g=AG)).then_inc(ws_taken, 1)
        act_split_w(act, 1)
        split = 1
        for n, (kind, g, half, f, c) in enumerate(jobs):
            if g > split - 1 and g + 1 < len(GROUPS) and g + 1 > split:
                split = g + 1
                act_split_w(act, split)
            if kind not in ON_ACT:
                continue
            act.wait_ge(job_ready, n + 1)
            if kind == "va":
                nc.scalar.activation(va[0:rows(c), c, GC * half:GC * half + GC], PS[0:rows(c), n % 8, 0:GC],
                                     ACT.Gelu_apprx_tanh).then_inc(act_took, 1)
            elif kind == "u":
                act.wait_ge(line_stored, 16)
                act.wait_ge(lam_ready, 1)
                w = KEPT[c].stop - KEPT[c].start
                nc.scalar.activation(uT[:, 2 * half + f, KEPT[c]], PS[:, n % 8, 0:w],
                                     ACT.Gelu_apprx_tanh).then_inc(act_took, 1)
            else:
                if c >= 2:
                    act.wait_ge(krow_stored[c % 2], 16 * (c // 2))
                nc.scalar.copy(k_rows[0:rows(c), c % 2, :], PS[0:rows(c), n % 8, :]).then_inc(act_took, 1)
                act.wait_ge(act_took, took[n][1])
                act.dma_start(k_out[c], k_rows[0:rows(c), c % 2, :]).then_inc(krow_stored[c % 2], 16)
        act.wait_ge(dve_took, n_dve)
        act.wait_ge(gate_mul, STEPS)
        nc.scalar.copy(act_hi[:, 4:8, 0:NTOK], uT[:]).then_inc(gate_hi_ready, 1)
        for i in range(2):
            act.wait_ge(krow_stored[i], 16 * ((STEPS + 1 - i) // 2))
        def take_turned(i):
            for t in range(turns(i)):
                act.wait_ge(turn_ready, turns_before(i) + t + 1)
                if i >= 2:
                    act.wait_ge(o_ready, i - 1)
                w = slice(512 * t, min(512 * (t + 1), P * (i % QB + 1)))
                bank = 4 + (turns_before(i) + t) % 2
                nc.scalar.copy(at_sb[:, i % 2, w], PS[:, bank, 0:w.stop - w.start]).then_inc(at_taken, 1)

        def exponent(i, m):
            act.wait_ge(nmax_ready, 2 * i + m + 1)
            if i >= 2:
                act.wait_ge(turn_ready, turns_before(i - 1))
            w = P * (i % QB + 1)
            src = PS[:, 2 * m:2 * m + 2, :].rearrange("p a b -> p (a b)")[:, 0:w]
            nc.scalar.activation(prob[:, i % 2, m, 0:w], src, ACT.Exp, bias=nmax[:, i % 4, m:m + 1],
                                 accum_out=prob_sum[:, i % 4, m:m + 1]).then_inc(prob_ready, 1)

        def out_square(i):
            act.wait_ge(o_ready, i + 1)
            if i >= 1:
                act.wait_ge(osq_ready, i)
            nc.scalar.activation(scratch[:, 0:DV], PS[:, 6, 0:DV], ACT.Square, scale=precip[:, i % 4, 0:1],
                                 accum_out=o_ssq[:, i % 4:i % 4 + 1]).then_inc(osq_ready, 1)

        def out_hi(g):
            act.wait_ge(ot_ready, g + 1)
            c0 = NS + P * OB * (g % (QB // OB))
            nc.scalar.copy(act_hi[:, g * OB // QB, c0:c0 + P * OB], PS[:, 7, :]).then_inc(ot_hi_ready, 1)

        act.wait_ge(bias_loaded, 16)
        nc.scalar.copy(bias_hi[:], bias_raw[:]).then_inc(bias_hi_ready, 1)
        act.wait_ge(bias_lo_ready, 1)
        nc.scalar.copy(sq[:], qT[:, :, 0:NS]).then_inc(sqk_ready, 1)
        nc.scalar.copy(sk[:], kT[:, :, 0:NS]).then_inc(sqk_ready, 1)
        for i in range(NSTEP + 4):
            if i < NSTEP:
                exponent(i, 0)
            if 0 <= i - 2 < NSTEP:
                out_square(i - 2)
            if i < NSTEP:
                exponent(i, 1)
            if 0 <= i - 1 < NSTEP:
                take_turned(i - 1)
            if i >= OB + 3 and (i - OB - 3) % OB == 0:
                out_hi((i - OB - 3) // OB)
        def take_keys(n):
            u, p = n // 4, n % 4
            act.wait_ge(kturn_ready, n + 1)
            if u >= 2:
                act.wait_ge(sscore_ready, u - 1)
            src = PS[:, 3 + n % 2, :].rearrange("p (h t) -> p h t", h=H)
            nc.scalar.copy(kt[:, u % 2, :, P * p:P * p + P], src).then_inc(kt_ready[1], 1)

        def smp_exponent(pr):
            act.wait_ge(smax_ready, pr + 1)
            if pr >= 1:
                act.wait_ge(sat_ready, 2 * pr)
            nc.scalar.activation(s_prob[:], PS[:, 0:3, :].rearrange("p a b -> p (a b)")[:, 0:SEQ + NS], ACT.Exp,
                                 bias=smp_max[:, pr:pr + 1], accum_out=smp_sum[:, pr:pr + 1]).then_inc(sprob_ready, 1)

        def smp_take(pr):
            act.wait_ge(sat_ready, 2 * pr + 1)
            if pr >= 1:
                act.wait_ge(pv_ready, 2 * pr)
            nc.scalar.copy(s_at[:], PS[:, 5, :].rearrange("p (n c) -> p n c", n=NPAGE)).then_inc(sat_taken, 1)

        def smp_take_own(pr):
            act.wait_ge(sat_ready, 2 * pr + 2)
            nc.scalar.copy(s_own[:], PS[0:NS, 5, 0:NS]).then_inc(sat_taken, 1)

        act.wait_ge(ot_lo_ready, NSTEP // OB)
        act.wait_ge(ot_ready, NSTEP // OB)
        for u in range(2 * NB + 1):
            if u < 2 * NB:
                take_keys(4 * u + 1)
                take_keys(4 * u + 3)
            if u % 4 == 0 and u >= 4:
                smp_exponent(u // 4 - 1)
            if u % 4 == 1 and u >= 5:
                smp_take(u // 4 - 1)
            if u % 4 == 2 and u >= 6:
                smp_take_own(u // 4 - 1)
        smp_take(NB // 2 - 1)
        smp_take_own(NB // 2 - 1)
        act.wait_ge(osel_ready, NB)
        nc.scalar.activation(s_sq[:], PS[:, 7, 0:H * NS], ACT.Square).then_inc(ssq_s_ready, 1)
        act.wait_ge(sout_ready, 1)
        nc.scalar.copy(act_hi[:, 0:H, 0:NS], s_out[:].rearrange("p (h c) -> p h c", h=H)).then_inc(sout_hi_ready, 1)
        act.wait_ge(wo_loaded, 16 * KD)
        for k in range(KD):
            nc.scalar.copy(wo_hi[:, k, :], wo_raw[:, k, :]).then_inc(wo_hi_ready, 1)
        act.wait_ge(wo_lo_ready, KD)

        def x2_hi(t):
            for h in range(2):
                act.wait_ge(xt_ready, 2 * STEPS + 2 * t + h + 1)
                src = PS[:, 4 + (2 * t + h) % 4, :].rearrange("p (k t) -> p k t", k=4)[:, :, 0:rows(t)]
                nc.scalar.copy(act_hi[:, 4 * h:4 * h + 4, cols(t)], src).then_inc(xt_hi_ready, 1)
        for t in range(STEPS + 1):
            if t < STEPS:
                r, j = rows(t), 2 * (t % 2)
                act.wait_ge(y_ready, t + 1)
                if t >= 1:
                    act.wait_ge(ssq_ready, STEPS + t)
                nc.scalar.activation(junk2[0:r, :], PS[0:r, j:j + 2, :].rearrange("p a b -> p (a b)"), ACT.Square,
                                     accum_out=ssq2[0:r, t:t + 1]).then_inc(yssq_ready, 1)
                act.wait_ge(xmid_ready, t + 1)
                act.wait_ge(yssq_ready, t + 1)
                nc.scalar.activation(junk2[0:r, :], x_mid[0:r, t % 2, :], ACT.Square,
                                     accum_out=ssq3[0:r, t:t + 1]).then_inc(ssq_ready, 1)
            if t >= 1:
                x2_hi(t - 1)
        def ffn_act(i, first, last):
            def split(t, ahead):
                n = 4 * i + t + ahead
                act.wait_ge(w_loaded[(t + ahead) % 2], UP_BASE + 8 * (n - (t + ahead) % 2) + 16)
                if ahead == 2:
                    act.wait_ge(up_ready, 4 * i + t + 1)
                nc.scalar.copy(wu_hi[:, (t + ahead) % 2], wu_raw[:, (t + ahead) % 2]).then_inc(wu_hi_ready, 1)

            if first:
                split(0, 0)
                split(1, 0)
                act.wait_ge(yacc_zero, 1)
            act.wait_ge(cwi_ready, i + 1)
            act.wait_ge(hsp_ready, 2 * i + 2)
            for t in range(4):
                e, half = t // 2, t % 2
                act.wait_ge(up_ready, 4 * i + t + 1)
                if not first or t >= 2:
                    act.wait_ge(tap_ready, 4 * i + t - 1)
                h = h_sb[half]
                nc.scalar.copy(h[:].rearrange("p (c t) -> p c t", c=3), PS[:, 3 * half:3 * half + 3, 0:CW]).then_inc(h_ready, 1)
                nc.scalar.copy(hsw[:, half, e, :, 2:], PS[:, 3 * half, 0:NS].rearrange("p (b q) -> p b q", b=NB)).then_inc(hs_ready, 1)
                if not first or t >= 2:
                    act.wait_ge(prod_ready if half == 0 else g_lo_ready, 2 * i + e)
                act.wait_ge(h_ready, 4 * i + t + 1)
                if half == 0 and (not first or t >= 2):
                    act.wait_ge(silu_ready, 2 * i + e)
                tap, bias = cwi[:, 2, half, e:e + 1], cwi[:, 3, half, e:e + 1]
                nc.scalar.activation(conv[:, half, :], h[:, 0:NTOK], ACT.Identity, bias=bias, scale=tap).then_inc(conv_ready, 1)
                if not (last and t >= 2):
                    split(t, 2)
                if half == 0:
                    act.wait_ge(tap_ready, 4 * i + t + 1)
                    nc.scalar.activation(conv[:, 0, :], conv[:, 0, :], ACT.Silu).then_inc(silu_ready, 1)
                else:
                    act.wait_ge(prod_ready, 2 * i + e + 1)
                    if not first:
                        act.wait_ge(down_ready, YJ * i)
                    nc.scalar.copy(g_hi[:, e, :], conv[:, 1, :]).then_inc(g_hi_ready, 1)
                    if t == 1:
                        for k in range(2):
                            act.wait_ge(wd_loaded[k], 16 * i + 16)
                            nc.scalar.copy(wd_hi[:, k, :], wd_raw[:, k, :]).then_inc(wd_hi_ready, 1)
        iterations(act, ffn_act)
        for t in range(STEPS):
            r = rows(t)
            act.wait_ge(ybank_free, YJ * (NIT - 1) + 2 * t + 4)
            if t >= 1:
                act.wait_ge(ssq_ready, 2 * STEPS + t)
            nc.scalar.activation(conv[0:r, 0, 0:D], y_acc[0:r, t, :], ACT.Square, accum_out=ssq[0:r, t:t + 1]).then_inc(ssq_ready, 1)

    @block.gpsimd
    def _(pool):
        nc.gpsimd.memset(ident[:], 0.0).then_inc(const_ready, 1)
        pool.wait_ge(const_ready, 1)
        nc.gpsimd.affine_select(out=ident[:], in_=ident[:], compare_op=ALU.not_equal, fill=1.0, base=0,
                                pattern=[[-1, P]], channel_multiplier=1).then_inc(const_ready, 1)
        nc.gpsimd.memset(small[:], -0.5).then_inc(const_ready, 1)
        nc.gpsimd.memset(smp_bias[:], NEG).then_inc(sbias_zero, 1)
        nc.gpsimd.memset(ws_bd[:], 0.0).then_inc(bd_zero, 1)
        for a in (act_hi, act_lo):
            nc.gpsimd.memset(a[:, :, NTOK:].bitcast(F32), 0.0).then_inc(pad_zero, 1)
        pool.wait_ge(const_ready, 3)
        nc.gpsimd.tensor_copy(identr[:], ident[:]).then_inc(const_ready, 1)

        def root(src, dst, i, n, scale, eps, done_sem):
            nc.gpsimd.tensor_scalar(mean_sq[0:n, i:i + 1], src, scale, eps, ALU.mult, ALU.add).then_inc(pool_step, 1)
            own_step(pool, pool_step)
            nc.gpsimd.tensor_tensor(dst, mean_sq[0:n, i:i + 1], neg_half[0:n], ALU.pow).then_inc(done_sem, 1)

        for s in range(STEPS):
            r = rows(s)
            pool.wait_ge(ssq_ready, s + 1)
            root(ssq[0:r, s:s + 1], rstd[0:r, s:s + 1], s, r, 1.0 / D, EPS, rstd_ready)
        for i, w in enumerate((wsT, wbT)):
            pool.wait_ge(ws_taken, i + 1)
            n = P if i == 0 else NS
            nc.gpsimd.affine_select(out=w[:], in_=w[:], compare_op=ALU.is_ge, fill=0.0, base=0,
                                    pattern=[[0, AG], [1, n]], channel_multiplier=-1).then_inc(ws_cut, 1)
        for s in range(STEPS):
            r = rows(s)
            pool.wait_ge(mv_ready, s + 1)
            root(ln_mv[0:r, s, 1:2], ln_rstd[0:r, s:s + 1], s, r, 1.0, EPS, ln_rstd_ready)
            pool.wait_ge(vc_ready, s + 1)
            nc.gpsimd.tensor_tensor(va[0:r, s, :], va[0:r, s, :], ln_g[0:r, :], ALU.mult).then_inc(pool_step, 1)
            own_step(pool, pool_step)
            nc.gpsimd.tensor_tensor(va[0:r, s, :], va[0:r, s, :], ln_b[0:r, :], ALU.add).then_inc(vn_ready, 1)
        pool.wait_ge(vn_ready, STEPS)
        pool.dma_start(sgu_v_sample[0].rearrange("b t c -> (b t) c"), va[0:NS, STEPS - 1, :]).then_inc(sgu_stored, 16)
        pool.wait_ge(sgu_stored, 16)
        for i in range(NSTEP):
            c = slice(i % 4, i % 4 + 1)
            pool.wait_ge(osq_ready, i + 1)
            nc.gpsimd.tensor_scalar(o_mean[:, c], o_ssq[:, c], 1.0 / DV, SUBLN_EPS, ALU.mult, ALU.add).then_inc(pool_step, 1)
            own_step(pool, pool_step)
            nc.gpsimd.tensor_tensor(o_rstd[:, c], o_mean[:, c], neg_half, ALU.pow).then_inc(pool_step, 1)
            own_step(pool, pool_step)
            nc.gpsimd.tensor_tensor(o_fac[:, c], o_rstd[:, c], precip[:, i % 4, 0:1], ALU.mult).then_inc(ofac_ready, 1)
        pool.wait_ge(smean_ready, 1)
        nc.gpsimd.tensor_tensor(s_rstd, s_mean, neg_half.to_broadcast([P, 2]), ALU.pow).then_inc(srstd_ready, 1)
        def root2(src, mean, dst, t, src_sem, n, done_sem):
            r, c = rows(t), slice(t, t + 1)
            pool.wait_ge(src_sem, n)
            nc.gpsimd.tensor_scalar(mean[0:r, c], src[0:r, c], 1.0 / D, EPS, ALU.mult, ALU.add).then_inc(pool_step, 1)
            own_step(pool, pool_step)
            nc.gpsimd.tensor_tensor(dst[0:r, c], mean[0:r, c], neg_half[0:r], ALU.pow).then_inc(done_sem, 1)
        for t in range(STEPS):
            root2(ssq2, mean_sq2, rstd2, t, yssq_ready, t + 1, yrstd_ready)
            root2(ssq3, mean_sq3, rstd3, t, ssq_ready, STEPS + t + 1, rstd_ready)
        pool.wait_ge(xt_lo_ready, 2 * STEPS + 2 * STEPS)
        for i in range(2):
            pool.wait_ge(xmid_stored[i], 16 * ((STEPS + 1 - i) // 2))
        nc.gpsimd.memset(y_acc[:], 0.0).then_inc(yacc_zero, 1)
        pool.wait_ge(st_taken, 6)
        pool.wait_ge(cw_taken, 1)

        def ffn_pool(i, first, last):
            if not first:
                pool.wait_ge(tap_ready, 4 * i)
                pool.wait_ge(hs_ready, 4 * i)
                keep_states(i - 1)
            nc.gpsimd.tensor_copy(cwi[:], cw[:, :, :, bass.ds(2 * i, 2)]).then_inc(cwi_ready, 1)
            for half in range(2):
                nc.gpsimd.tensor_copy(hsw[:, half, :, :, 0:2], stT[:, bass.ds(JF * half + 2 * i, 2)]).then_inc(hsp_ready, 1)

        def keep_states(i):
            for half in range(2):
                nc.gpsimd.tensor_copy(stT[:, bass.ds(JF * half + 2 * i, 2)], hsw[:, half, :, :, DS:]).then_inc(cs_kept, 1)
                nc.gpsimd.tensor_copy(cpT[:, bass.ds(JF * half + 2 * i, 2)], cpw[:, half]).then_inc(cs_kept, 1)
            pool.wait_ge(cs_kept, 4 * i + 4)
        iterations(pool, ffn_pool)
        pool.wait_ge(tap_ready, 4 * NIT)
        pool.wait_ge(hs_ready, 4 * NIT)
        keep_states(NIT - 1)
        def final_add(t):
            r = rows(t)
            pool.wait_ge(ynrm_ready, STEPS + t + 1)
            pool.wait_ge(x_loaded[t % 3], 16 * (STEPS // 3) + 16 * (t // 3 + 1))
            nc.gpsimd.tensor_tensor(y_acc[0:r, t, :], y_acc[0:r, t, :], x_back[0:r, t % 3, :], ALU.add).then_inc(fout_ready, 1)
        for t in range(STEPS):
            r = rows(t)
            pool.wait_ge(ssq_ready, 2 * STEPS + t + 1)
            c = slice(t, t + 1)
            nc.gpsimd.tensor_scalar(mean_sq[0:r, c], ssq[0:r, c], 1.0 / D, EPS, ALU.mult, ALU.add).then_inc(pool_step, 1)
            own_step(pool, pool_step)
            nc.gpsimd.tensor_tensor(rstd[0:r, c], mean_sq[0:r, c], neg_half[0:r], ALU.pow).then_inc(rstd_ready, 1)
            if t >= 1:
                final_add(t - 1)
        final_add(STEPS - 1)

    @block.vector
    def _(dve):
        nc.vector.memset(rel_rep[:], 1.0).then_inc(rep_ready, 1)
        dve.wait_ge(setup_loaded, 16 * 7)
        dve.wait_ge(rep_ready, 1)
        for h in range(H):
            nc.vector.tensor_copy(rel_rep[0:BUCKETS, h, :], rel_sb[:, h:h + 1].to_broadcast([BUCKETS, P])).then_inc(rep_ready, 1)
        nc.vector.tensor_tensor(lam_prod[:], lam_in[:, 0:2, :], lam_in[:, 2:4, :], ALU.mult).then_inc(lam_step, 1)
        nc.vector.tensor_scalar(sub_gain[:], sub_gain[:], 1.0 - LAM_INIT, None, ALU.mult).then_inc(lam_step, 1)
        dve.wait_ge(lam_step, 2)
        dve.wait_ge(const_ready, 3)
        nc.vector.tensor_reduce(lam_sum, lam_prod[:], AX.X, ALU.add).then_inc(lam_step, 1)
        for h in range(H):
            dve.wait_ge(line_ready, h + 1)
            nc.vector.tensor_copy(line_out[:, h, :], PS[:, 4 + h, 0:LINE]).then_inc(line_taken, 1)
        dve.wait_ge(gain_loaded, 16)

        def xt_lo(s):
            for h in range(2):
                src = PS[:, (2 * s + h) % 8, :].rearrange("p (k t) -> p k t", k=4)[:, :, 0:rows(s)]
                dve.wait_ge(xt_hi_ready, 2 * s + h + 1)
                nc.vector.tensor_tensor(act_lo[:, 4 * h:4 * h + 4, cols(s)], src,
                                        act_hi[:, 4 * h:4 * h + 4, cols(s)].bitcast(F32),
                                        ALU.subtract).then_inc(xt_lo_ready, 1)
        for s in range(STEPS):
            r = rows(s)
            dve.wait_ge(rstd_ready, s + 1)
            if s >= 2:
                dve.wait_ge(xt_ready, 2 * (s - 1))
            nc.vector.scalar_tensor_tensor(x_nrm[0:r, s % 2, :], x_in[0:r, s % 3, :], rstd[0:r, s:s + 1],
                                           gain[0:r, :], ALU.mult, ALU.mult).then_inc(nrm_ready, 1)
            if s >= 1:
                xt_lo(s - 1)
            if s == 4:
                dve_split_w(dve, 0)
        xt_lo(STEPS - 1)
        dve.wait_ge(lam_exp_ready, 1)
        nc.vector.tensor_scalar(lam_dif, lam_exp[:, 1:2], LAM_INIT, None, ALU.subtract).then_inc(lam_step, 1)
        dve.wait_ge(lam_step, 4)
        nc.vector.tensor_tensor(neg_lam, lam_dif, lam_exp[:, 0:1], ALU.subtract).then_inc(lam_ready, 1)
        dve_split_w(dve, 1)
        split = 1

        def layer_stats(s):
            r = rows(s)
            dve.wait_ge(act_took, STEPS + s + 1)
            nc.vector.bn_stats(scratch[0:r, 8 * s:8 * s + 6], va[0:r, s, :]).then_inc(dve_step, 1)
            own_step(dve, dve_step)
            nc.vector.bn_aggr(ln_mv[0:r, s, :], scratch[0:r, 8 * s:8 * s + 6]).then_inc(mv_ready, 1)

        def center(s):
            r = rows(s)
            dve.wait_ge(ln_rstd_ready, s + 1)
            nc.vector.tensor_scalar(va[0:r, s, :], va[0:r, s, :], ln_mv[0:r, s, 0:1], ln_rstd[0:r, s:s + 1],
                                    ALU.subtract, ALU.mult).then_inc(vc_ready, 1)

        for n, (kind, g, half, f, c) in enumerate(jobs):
            if g > split - 1 and g + 1 < len(GROUPS) and g + 1 > split:
                split = g + 1
                dve_split_w(dve, split)
                if g == 2:
                    for s in range(STEPS):
                        layer_stats(s)
                        if s >= 1:
                            center(s - 1)
                    center(STEPS - 1)
            if kind in ON_ACT:
                continue
            dve.wait_ge(job_ready, n + 1)
            if kind in ("q", "k"):
                w = KEPT[c].stop - KEPT[c].start
                dst = (qT if kind == "q" else kT)[:, 2 * half + f, KEPT[c]]
                if kind == "q":
                    nc.vector.tensor_scalar(dst, PS[:, n % 8, 0:w], DH ** -0.5, None, ALU.mult).then_inc(dve_took, 1)
                else:
                    nc.vector.tensor_copy(dst, PS[:, n % 8, 0:w]).then_inc(dve_took, 1)
            elif kind == "gate":
                s, w = c, rows(c)
                b_of = bs[:] if s < STEPS - 1 else bs_smp[:].rearrange("p g b t -> p g (b t)")
                if s == 0:
                    dve.wait_ge(act_took, n_u_done)
                if s >= 2:
                    dve.wait_ge(gate_mul, s - 1)
                ps = PS[:, n % 8, :].rearrange("p (g t) -> p g t", g=AG)[:, :, 0:w]
                nc.vector.tensor_tensor(g_sum[:, s % 2, :, 0:w], ps, b_of, ALU.add).then_inc(dve_took, 1)
                dve.wait_ge(dve_took, took[n][1])
                nc.vector.tensor_tensor(uT[:, :, cols(s)], g_sum[:, s % 2, :, 0:w], uT[:, :, cols(s)],
                                        ALU.mult).then_inc(gate_mul, 1)
            else:
                r = rows(c)
                vh = slice(GC * half, GC * half + GC)
                if c == 0 and half == 0:
                    dve.wait_ge(job_ready, last_gate + 1)
                    dve.wait_ge(sgu_stored, 16)
                nc.vector.tensor_copy(v_all[0:r, c, vh], PS[0:r, n % 8, 0:GC]).then_inc(dve_took, 1)
                if c == STEPS - 1:
                    dve.wait_ge(dve_took, took[n][1])
                    nc.vector.tensor_copy(v_smp[0:NS, vh], v_all[0:NS, c, vh]).then_inc(v_kept, 1)
        dve.wait_ge(gate_hi_ready, 1)
        nc.vector.tensor_tensor(act_lo[:, 4:8, 0:NTOK], uT[:], act_hi[:, 4:8, 0:NTOK].bitcast(F32),
                                ALU.subtract).then_inc(gate_lo_ready, 1)
        def row_max(i, m):
            dve.wait_ge(score_ready, 2 * i + m + 1)
            src = PS[:, 2 * m:2 * m + 2, :].rearrange("p a b -> p (a b)")[:, 0:P * (i % QB + 1)]
            nc.vector.tensor_reduce(nmax[:, i % 4, m:m + 1], src, AX.X, ALU.max, negate=True).then_inc(nmax_ready, 1)

        def mix(i):
            w = P * (i % QB + 1)
            dve.wait_ge(prob_ready, 2 * i + 2)
            if i >= 4:
                dve.wait_ge(ofac_ready, i - 3)
            nc.vector.reciprocal(precip[:, i % 4, :], prob_sum[:, i % 4, :]).then_inc(dve_step, 1)
            own_step(dve, dve_step)
            nc.vector.scalar_tensor_tensor(pcoef[:, i % 4:i % 4 + 1], precip[:, i % 4, 1:2], neg_lam,
                                           prob_sum[:, i % 4, 0:1], ALU.mult, ALU.mult).then_inc(dve_step, 1)
            own_step(dve, dve_step)
            nc.vector.scalar_tensor_tensor(prob[:, i % 2, 0, 0:w], prob[:, i % 2, 1, 0:w], pcoef[:, i % 4:i % 4 + 1],
                                           prob[:, i % 2, 0, 0:w], ALU.mult, ALU.add).then_inc(mix_ready, 1)

        def out_norm(i):
            dve.wait_ge(ofac_ready, i + 1)
            if i >= QB:
                dve.wait_ge(ot_ready, (i - QB) // OB + 1)
            nc.vector.scalar_tensor_tensor(o_nrm[:, i % QB, :], PS[:, 6, 0:DV], o_fac[:, i % 4:i % 4 + 1], sub_gain[:],
                                           ALU.mult, ALU.mult).then_inc(onrm_ready, 1)

        def out_lo(g):
            dve.wait_ge(ot_hi_ready, g + 1)
            c0 = NS + P * OB * (g % (QB // OB))
            dst = slice(c0, c0 + P * OB)
            nc.vector.tensor_tensor(act_lo[:, g * OB // QB, dst], PS[:, 7, :], act_hi[:, g * OB // QB, dst].bitcast(F32),
                                    ALU.subtract).then_inc(ot_lo_ready, 1)

        dve.wait_ge(bias_hi_ready, 1)
        nc.vector.tensor_tensor(bias_lo[:], bias_raw[:], bias_hi[:].bitcast(F32), ALU.subtract).then_inc(bias_lo_ready, 1)
        dve.wait_ge(lam_ready, 1)
        for i in range(NSTEP + 4):
            if 0 <= i - 1 < NSTEP:
                mix(i - 1)
            if i < NSTEP:
                row_max(i, 0)
                row_max(i, 1)
            if 0 <= i - 2 < NSTEP:
                out_norm(i - 2)
            if i >= OB + 3 and (i - OB - 3) % OB == 0:
                out_lo((i - OB - 3) // OB)
        dve.wait_ge(sel_loaded, 32)
        nc.vector.scalar_tensor_tensor(row_coef, select_sb[:, 65:66], neg_lam, select_sb[:, 64:65], ALU.mult, ALU.add).then_inc(rowcoef_step, 1)
        nc.vector.tensor_scalar(gain_col, gain_col, 1.0 - LAM_INIT, None, ALU.mult).then_inc(rowcoef_step, 1)
        dve.wait_ge(ot_lo_ready, NSTEP // OB)
        nc.vector.memset(qp[:], 0.0).then_inc(qp_zero, 1)
        nc.vector.memset(ones[:], 1.0).then_inc(qp_zero, 1)
        dve.wait_ge(qp_zero, 2)

        def take_keys(n):
            u, p = n // 4, n % 4
            dve.wait_ge(kturn_ready, n + 1)
            if u >= 2:
                dve.wait_ge(sscore_ready, u - 1)
            src = PS[:, 3 + n % 2, :].rearrange("p (h t) -> p h t", h=H)
            nc.vector.tensor_copy(kt[:, u % 2, :, P * p:P * p + P], src).then_inc(kt_ready[0], 1)

        def take_rows(b):
            dve.wait_ge(pv_ready, b + 1)
            if b >= 1:
                dve.wait_ge(osel_ready, b)
            nc.vector.tensor_copy(o_rows[:], PS[0:DS * H, 6, :]).then_inc(orows_ready, 1)

        def q_pad(pr):
            if pr >= 1:
                dve.wait_ge(sscore_ready, 4 * pr)
            for m in range(2):
                d = slice(DH * m, DH * m + DH)
                dst = qp[d, :].rearrange("p (b h c) -> p b h c", b=2, h=H)[:, :, :, DS * m:DS * m + DS]
                src = sq[d, :, 16 * pr:16 * pr + 16].rearrange("p h (b q) -> p b h q", b=2)
                nc.vector.tensor_copy(dst, src).then_inc(qp_ready, 1)

        def smp_softmax(pr):
            c = slice(pr, pr + 1)
            dve.wait_ge(sscore_ready, 4 * pr + 4)
            dve.wait_ge(sbias_loaded, 16 * 32)
            last_page = PS[:, 1, 384:512]
            nc.vector.tensor_tensor(last_page, last_page, smp_bias[:, 0:P], ALU.add)
            own = P + DS * (6 - 2 * pr)
            nc.vector.tensor_tensor(PS[:, 2, 0:NS], PS[:, 2, 0:NS], smp_bias[:, own:own + NS], ALU.add).then_inc(dve_step, 1)
            own_step(dve, dve_step)
            nc.vector.tensor_reduce(smp_max[:, c], PS[:, 0:3, :].rearrange("p a b -> p (a b)")[:, 0:SEQ + NS],
                                    AX.X, ALU.max, negate=True).then_inc(smax_ready, 1)

        def smp_factors(pr):
            c = slice(pr, pr + 1)
            dve.wait_ge(sprob_ready, pr + 1)
            nc.vector.reciprocal(smp_recip[:, c], smp_sum[:, c]).then_inc(dve_step, 1)
            own_step(dve, dve_step)
            dve.wait_ge(rowcoef_step, 2)
            nc.vector.tensor_tensor(smp_coef[:, c], smp_recip[:, c], row_coef, ALU.mult).then_inc(dve_step, 1)
            own_step(dve, dve_step)
            if pr >= 1:
                dve.wait_ge(sat_ready, 2 * pr)
            nc.vector.tensor_scalar(c_mat[:], select_sb[:, 0:NS], smp_coef[:, c], None, ALU.mult).then_inc(cmat_ready, 1)

        dve.wait_ge(sqk_ready, 2)
        for u in range(2 * NB + 1):
            if u < 2 * NB:
                take_keys(4 * u)
                take_keys(4 * u + 2)
            if u % 2 == 0 and u >= 6:
                take_rows((u - 6) // 2)
            if u % 4 == 0 and u < 2 * NB:
                q_pad(u // 4)
            if u % 4 == 0 and u >= 4:
                smp_softmax(u // 4 - 1)
            if u % 4 == 1 and u >= 5:
                smp_factors(u // 4 - 1)
        smp_factors(NB // 2 - 1)
        take_rows(NB - 2)
        take_rows(NB - 1)
        dve.wait_ge(ssum_ready, 1)
        dve.wait_ge(sat_ready, NB)
        nc.vector.tensor_scalar(s_mean, PS[:, 6, 0:2], 1.0 / DV, SUBLN_EPS, ALU.mult, ALU.add).then_inc(smean_ready, 1)
        dve.wait_ge(srstd_ready, 1)
        for j in range(2):
            nc.vector.tensor_scalar(s_rs[:, j, :], ident[:], s_rstd[:, j:j + 1], None, ALU.mult).then_inc(sdiag_ready, 1)
        dve.wait_ge(sfac_ready, 1)
        nc.vector.tensor_copy(s_fac[:], PS[:, 5, 0:H * NS]).then_inc(dve_step, 1)
        own_step(dve, dve_step)
        nc.vector.scalar_tensor_tensor(s_out[:], PS[:, 7, 0:H * NS], gain_col, s_fac[:], ALU.mult, ALU.mult).then_inc(sout_ready, 1)
        dve.wait_ge(sout_hi_ready, 1)
        nc.vector.tensor_tensor(act_lo[:, 0:H, 0:NS], s_out[:].rearrange("p (h c) -> p h c", h=H),
                                act_hi[:, 0:H, 0:NS].bitcast(F32), ALU.subtract).then_inc(sout_lo_ready, 1)
        for k in range(KD):
            dve.wait_ge(wo_hi_ready, k + 1)
            nc.vector.tensor_tensor(wo_lo[:, k, :], wo_raw[:, k, :], wo_hi[:, k, :].bitcast(F32), ALU.subtract).then_inc(wo_lo_ready, 1)
        dve.wait_ge(gain_loaded, 48)

        def x2_lo(t):
            for h in range(2):
                dve.wait_ge(xt_hi_ready, 2 * STEPS + 2 * t + h + 1)
                src = PS[:, 4 + (2 * t + h) % 4, :].rearrange("p (k t) -> p k t", k=4)[:, :, 0:rows(t)]
                dst = cols(t)
                nc.vector.tensor_tensor(act_lo[:, 4 * h:4 * h + 4, dst], src, act_hi[:, 4 * h:4 * h + 4, dst].bitcast(F32),
                                        ALU.subtract).then_inc(xt_lo_ready, 1)
        for t in range(STEPS + 1):
            if t < STEPS:
                r, j = rows(t), 2 * (t % 2)
                dve.wait_ge(yrstd_ready, t + 1)
                nc.vector.scalar_tensor_tensor(y_nrm[0:r, t % 2, :], PS[0:r, j:j + 2, :].rearrange("p a b -> p (a b)"),
                                               rstd2[0:r, t:t + 1], gain[0:r, :], ALU.mult, ALU.mult).then_inc(ynrm_ready, 1)
                dve.wait_ge(ynrm_ready, t + 1)
                dve.wait_ge(xres_loaded[t % 2], 16 * (t // 2 + 1))
                if t >= 2:
                    dve.wait_ge(xmid_stored[t % 2], 16 * (t // 2))
                    dve.wait_ge(nrm_ready, STEPS + t - 1)
                nc.vector.tensor_tensor(x_mid[0:r, t % 2, :], y_nrm[0:r, t % 2, :], x_res[0:r, t % 2, :], ALU.add).then_inc(xmid_ready, 1)
                dve.wait_ge(rstd_ready, STEPS + t + 1)
                if t >= 2:
                    dve.wait_ge(xt_ready, 2 * STEPS + 2 * (t - 1))
                nc.vector.scalar_tensor_tensor(x2_nrm[0:r, t % 2, :], x_mid[0:r, t % 2, :], rstd3[0:r, t:t + 1], gain2[0:r, :],
                                               ALU.mult, ALU.mult).then_inc(nrm_ready, 1)
            if t >= 1:
                x2_lo(t - 1)
        for q in range(6):
            dve.wait_ge(st_turned, q + 1)
            n = min(8, 2 * JF - 8 * q)
            nc.vector.tensor_copy(stT[:, 8 * q:8 * q + n], PS[:, q % 2, 0:16 * n].rearrange("p (j b r) -> p j b r", b=NB, r=2)).then_inc(st_taken, 1)
        dve.wait_ge(cw_turned, 1)
        nc.vector.tensor_copy(cw[:], PS[:, 2, 0:8 * JF].rearrange("p (w a j) -> p w a j", w=4, a=2)).then_inc(cw_taken, 1)

        def add_down(base, n):
            t, half = n // 2, n % 2
            r = rows(t)
            dve.wait_ge(down_ready, base + n + 1)
            dst = y_acc[0:r, t, 512 * half:512 * half + 512]
            nc.vector.tensor_tensor(dst, dst, PS[0:r, 6 + half, :], ALU.add).then_inc(ybank_free, 1)

        def ffn_dve(i, first, last):
            adds = iter(range(0 if first else YJ))

            def some_adds(t, most):
                if t == 1:
                    for _, n in zip(range(most), adds):
                        add_down(YJ * i - YJ, n)

            def split(t, ahead):
                dve.wait_ge(wu_hi_ready, 4 * i + t + ahead + 1)
                q = (t + ahead) % 2
                nc.vector.tensor_tensor(wu_lo[:, q], wu_raw[:, q], wu_hi[:, q].bitcast(F32), ALU.subtract).then_inc(wu_lo_ready, 1)

            if first:
                split(0, 0)
                split(1, 0)
            for t in range(4):
                e, half = t // 2, t % 2
                u = 4 * i + t
                h = h_sb[half]
                w1, w0 = cwi[:, 1, half, e:e + 1], cwi[:, 0, half, e:e + 1]
                some_adds(t, 1)
                dve.wait_ge(conv_ready, u + 1)
                nc.vector.scalar_tensor_tensor(conv[:, half, NS + 1:], h[:, NS:NTOK - 1], w1, conv[:, half, NS + 1:],
                                               ALU.mult, ALU.add).then_inc(tap1_ready, 1)
                some_adds(t, 1)
                nc.vector.tensor_copy(cpw[:, half, e, :], h[:, NTOK - 2:NTOK]).then_inc(tap1_ready, 1)
                dve.wait_ge(hs_ready, u + 1)
                smp_c = conv[:, half, 0:NS].rearrange("p (b q) -> p b q", b=NB)
                nc.vector.scalar_tensor_tensor(smp_c, hsw[:, half, e, :, 1:DS + 1], w1, smp_c, ALU.mult, ALU.add).then_inc(tap1_ready, 1)
                dve.wait_ge(tap1_ready, 3 * u + 3)
                nc.vector.scalar_tensor_tensor(smp_c, hsw[:, half, e, :, 0:DS], w0, smp_c, ALU.mult, ALU.add).then_inc(stap_ready, 1)
                dve.wait_ge(stap_ready, u + 1)
                nc.vector.scalar_tensor_tensor(conv[:, half, NS + 2:], h[:, NS:NTOK - 2], w0, conv[:, half, NS + 2:],
                                               ALU.mult, ALU.add).then_inc(tap_ready, 1)
                some_adds(t, 2)
                if not (last and t >= 2):
                    split(t, 2)
                some_adds(t, 2)
                if half == 1:
                    dve.wait_ge(silu_ready, 2 * i + e + 1)
                    dve.wait_ge(tap_ready, u + 1)
                    nc.vector.tensor_tensor(conv[:, 1, :], conv[:, 0, :], conv[:, 1, :], ALU.mult).then_inc(prod_ready, 1)
                    some_adds(t, YJ)
                    dve.wait_ge(g_hi_ready, 2 * i + e + 1)
                    nc.vector.tensor_tensor(g_lo[:, e, :], conv[:, 1, :], g_hi[:, e, :].bitcast(F32), ALU.subtract).then_inc(g_lo_ready, 1)
                    if t == 1:
                        for k in range(2):
                            dve.wait_ge(wd_hi_ready, 2 * i + k + 1)
                            nc.vector.tensor_tensor(wd_lo[:, k, :], wd_raw[:, k, :], wd_hi[:, k, :].bitcast(F32), ALU.subtract).then_inc(wd_lo_ready, 1)
        dve.wait_ge(xt_lo_ready, 2 * STEPS + 2 * STEPS)
        for bank in (6, 7):
            nc.vector.memset(PS[:, bank, :], 0.0).then_inc(ybank_free, 1)
        dve.wait_ge(yacc_zero, 1)
        iterations(dve, ffn_dve)
        dve.wait_ge(gain_loaded, 64)

        def final_norm(t):
            r = rows(t)
            dve.wait_ge(rstd_ready, 2 * STEPS + t + 1)
            nc.vector.scalar_tensor_tensor(y_acc[0:r, t, :], y_acc[0:r, t, :], rstd[0:r, t:t + 1], gain[0:r, :],
                                           ALU.mult, ALU.mult).then_inc(ynrm_ready, 1)

        def take_states(q):
            dve.wait_ge(st_turned, 6 + 7)
            if q < 6:
                n = min(8, 2 * JF - 8 * q)
                nc.vector.tensor_copy(st_nat[0:16 * n, q, :], PS[0:16 * n, q, 0:P]).then_inc(st_taken, 1)
            else:
                nc.vector.tensor_copy(cw_nat[:, 0:2, :], PS[0:2 * JF, 0, P:3 * P].rearrange("p (r c) -> p r c", r=2)).then_inc(st_taken, 1)
        for t in range(STEPS + 2):
            if t < STEPS:
                add_down(YJ * (NIT - 1), 2 * t)
                add_down(YJ * (NIT - 1), 2 * t + 1)
            if t >= 2:
                final_norm(t - 2)
            if 1 <= t < 8:
                take_states(t - 1)

    @block.tensor
    def _(pe):
        pe.wait_ge(const_ready, 4)
        for h in range(H):
            pe.wait_ge(rep_ready, h + 2)
            nc.tensor.matmul(PS[:, 4 + h, 0:LINE], rel_rep[:, h, :], lines_sb[:], start=True, stop=True).then_inc(line_ready, 1)
        for s in range(STEPS):
            pe.wait_ge(nrm_ready, s + 1)
            for h in range(2):
                j = 2 * s + h
                if j >= 8:
                    pe.wait_ge(xt_lo_ready, j - 7)
                if j == 4:
                    pe.wait_ge(line_taken, H)
                for k in range(4):
                    mm = nc.tensor.transpose(PS[:, j % 8, P * k:P * k + rows(s)],
                                             x_nrm[0:rows(s), s % 2, P * (4 * h + k):P * (4 * h + k + 1)],
                                             ident[0:rows(s), 0:rows(s)])
                mm.then_inc(xt_ready, 1)
        pe.wait_ge(gate_loaded, 16 * (4 + 2 * NB))
        pe.wait_ge(xt_lo_ready, 2 * STEPS)
        for i, (w, n) in enumerate(((ws_nat, P), (ws_bd, NS))):
            for g in range(AG):
                mm = nc.tensor.transpose(PS[0:n, 2 + i, n * g:n * g + n], w[:, g, :], ident[0:n, 0:n])
            mm.then_inc(ws_turned, 1)
        pe.wait_ge(ws_taken, 2)
        pe.wait_ge(pad_zero, 2)
        group = -1
        for n, (kind, g, half, f, c) in enumerate(jobs):
            if g != group:
                group = g
                pe.wait_ge(w_lo_ready, 2 * g + 2)
            if n >= 8:
                pe.wait_ge(*took[n - 8])
            if kind == "krow":
                if c == 0:
                    pe.wait_ge(dve_took, last_k_took)
                for h in range(H):
                    mm = nc.tensor.transpose(PS[0:rows(c), n % 8, P * h:P * h + P], kT[:, h, cols(c)], ident[:])
            elif kind == "gate":
                if c == 0:
                    pe.wait_ge(ws_cut, 2)
                pe.wait_ge(vn_ready, c + 1)
                r, w = rows(c), wsT if c < STEPS - 1 else wbT
                for a in range(AG):
                    mm = nc.tensor.matmul(PS[:, n % 8, P * a:P * a + r], va[0:r, c, P * a:P * a + P], w[:, a, :],
                                          start=True, stop=True)
            else:
                if kind in ("va", "v"):
                    out, stat, mov = PS[:, n % 8, 0:GC], wide(c), slice(0, GC)
                    pairs = [(a[:, k, stat], w[:, g % 2, k, :]) for k in range(KD)
                             for a, w in ((act_hi, w_hi), (act_hi, w_lo), (act_lo, w_hi))]
                else:
                    out = PS[:, n % 8, 0:CW]
                    pairs = [(w[:, g % 2, k, P * f:P * f + P], a[:, k, CHUNKS[c]]) for k in range(KD)
                             for w, a in ((w_hi, act_hi), (w_hi, act_lo), (w_lo, act_hi))]
                for i, (lhs, rhs) in enumerate(pairs):
                    mm = nc.tensor.matmul(out, lhs, rhs, start=(i == 0), stop=(i == len(pairs) - 1))
            mm.then_inc(job_ready, 1)
        for q in took[-8:]:
            pe.wait_ge(*q)
        def scores(i, m):
            h, n = i // QB, i % QB + 1
            w = P * n
            if i == 0:
                pe.wait_ge(bias_lo_ready, 1)
            if i >= 1:
                pe.wait_ge(prob_ready, 2 * (i - 1) + m + 1)
            d = slice(DH * m, DH * m + DH)
            qs = slice(NS + P * (n - 1), NS + P * n)
            for c in range(0, w, 512):
                e = min(c + 512, w)
                out = PS[:, 2 * m + c // 512, :]
                b0 = max(c, w - 2 * P)
                mm = nc.tensor.matmul(out[:, 0:e - c], qT[d, h, qs], kT[d, h, NS + c:NS + e], start=True, stop=b0 >= e)
                if b0 < e:
                    t = slice(b0 - (w - 2 * P), e - (w - 2 * P))
                    for j, b in enumerate((bias_hi, bias_lo)):
                        mm = nc.tensor.matmul(out[:, b0 - c:e - c], identr[:], b[:, h, t], start=False, stop=(j == 1))
            mm.then_inc(score_ready, 1)

        def turn(i):
            n = i % QB + 1
            pe.wait_ge(mix_ready, i + 1)
            for t in range(turns(i)):
                at_turn = turns_before(i) + t
                if at_turn >= 2:
                    pe.wait_ge(at_taken, at_turn - 1)
                for k in range(4 * t, min(4 * t + 4, n)):
                    mm = nc.tensor.transpose(PS[:, 4 + at_turn % 2, P * (k % 4):P * (k % 4) + P],
                                             prob[:, i % 2, 0, P * k:P * k + P], ident[:])
                mm.then_inc(turn_ready, 1)

        def weigh(i):
            h, n = i // QB, i % QB + 1
            pe.wait_ge(at_taken, turns_before(i + 1))
            if i >= 1:
                pe.wait_ge(onrm_ready, i)
            for k in range(n):
                mm = nc.tensor.matmul(PS[:, 6, 0:DV], at_sb[:, i % 2, P * k:P * k + P], v_all[:, k, DV * h:DV * h + DV],
                                      start=(k == 0), stop=(k == n - 1))
            mm.then_inc(o_ready, 1)

        def turn_out(g):
            pe.wait_ge(onrm_ready, OB * (g + 1))
            if g >= 1:
                pe.wait_ge(ot_lo_ready, g)
            for j in range(OB):
                mm = nc.tensor.transpose(PS[:, 7, P * j:P * j + P], o_nrm[:, (OB * g + j) % QB, :], ident[:])
            mm.then_inc(ot_ready, 1)

        for i in range(NSTEP + 4):
            if i < NSTEP:
                scores(i, 0)
            if 0 <= i - 2 < NSTEP:
                weigh(i - 2)
            if i < NSTEP:
                scores(i, 1)
            if 0 <= i - 1 < NSTEP:
                turn(i - 1)
            if i >= OB + 3 and (i - OB - 3) % OB == 0:
                turn_out((i - OB - 3) // OB)
        def turn_keys(u):
            pe.wait_ge(kp_loaded[u % 2], 64 * (u // 2 + 1))
            for p in range(4):
                n = 4 * u + p
                if n >= 2:
                    pe.wait_ge(kt_ready[n % 2], n // 2)
                for h in range(H):
                    mm = nc.tensor.transpose(PS[:, 3 + n % 2, P * h:P * h + P], kpage[:, n % 8, P * h:P * h + P], ident[:])
                mm.then_inc(kturn_ready, 1)

        def smp_scores(u):
            pr, b2, c = u // 4, u // 2 % 2, u % 2
            for i in range(2):
                pe.wait_ge(kt_ready[i], 2 * u + 2)
            pe.wait_ge(qp_ready, 2 * pr + 2)
            if pr >= 1:
                pe.wait_ge(sprob_ready, pr)
            for h in range(H):
                n = 4 * b2 + h
                w = slice(P * n, P * n + P)
                mm = nc.tensor.matmul(PS[:, c, :], qp[:, w], kt[:, u % 2, h, :], start=(n == 0), stop=(n == 7))
                if c == 1:
                    mm = nc.tensor.matmul(PS[:, 2, 0:NS], qp[:, w], sk[:, h, :], start=(n == 0), stop=(n == 7))
            mm.then_inc(sscore_ready, 1)

        def smp_turn(pr):
            pe.wait_ge(cmat_ready, pr + 1)
            if pr >= 1:
                pe.wait_ge(sat_taken, 2 * pr)
            for p in range(NPAGE):
                mm = nc.tensor.matmul(PS[:, 5, NS * p:NS * p + NS], s_prob[:, P * p:P * p + P], c_mat[:], start=True, stop=True)
            mm.then_inc(sat_ready, 1)

        def smp_turn_own(pr):
            pe.wait_ge(sat_taken, 2 * pr + 1)
            nc.tensor.matmul(PS[0:NS, 5, 0:NS], s_prob[:, SEQ:SEQ + NS], c_mat[:], start=True, stop=True).then_inc(sat_ready, 1)

        def smp_weigh(b, first_page, last_page):
            pr, q = b // 2, slice(DS * H * (b % 2), DS * H * (b % 2) + DS * H)
            out = PS[0:DS * H, 6, :]
            if first_page == 0:
                pe.wait_ge(sat_taken, 2 * pr + 1)
                pe.wait_ge(vp_loaded[b % VR], 16 * NPAGE * (b // VR + 1))
                if b >= 1:
                    pe.wait_ge(orows_ready, b)
            for p in range(first_page, last_page):
                nc.tensor.matmul(out, s_at[:, p, q], vpage[b % VR][:, p, :], start=(p == 0), stop=False)
            if last_page == NPAGE:
                pe.wait_ge(sat_taken, 2 * pr + 2)
                nc.tensor.matmul(out, s_own[:, q], v_smp[0:NS, :], start=False, stop=True).then_inc(pv_ready, 1)

        def smp_select(b):
            pe.wait_ge(orows_ready, b + 1)
            for h in range(H):
                mm = nc.tensor.matmul(PS[:, 7, NS * h + DS * b:NS * h + DS * b + DS], o_rows[:, P * h:P * h + P],
                                      ident[0:DS * H, DS * h:DS * h + DS], start=True, stop=True)
            mm.then_inc(osel_ready, 1)

        pe.wait_ge(sqk_ready, 2)
        pe.wait_ge(v_kept, 2)
        pe.wait_ge(at_taken, turns_before(NSTEP))
        pe.wait_ge(ot_lo_ready, NSTEP // OB)
        turn_keys(0)
        for u in range(2 * NB):
            if u + 1 < 2 * NB:
                turn_keys(u + 1)
            smp_scores(u)
            if u >= 4:
                pr = u // 4 - 1
                if u % 4 == 0:
                    if pr >= 1:
                        smp_select(2 * pr - 1)
                    smp_turn(pr)
                elif u % 4 == 1:
                    smp_turn_own(pr)
                    smp_weigh(2 * pr, 0, NPAGE)
                elif u % 4 == 2:
                    smp_select(2 * pr)
                    smp_weigh(2 * pr + 1, 0, NPAGE // 2)
                else:
                    smp_weigh(2 * pr + 1, NPAGE // 2, NPAGE)
        smp_select(NB - 3)
        smp_turn(NB // 2 - 1)
        smp_turn_own(NB // 2 - 1)
        smp_weigh(NB - 2, 0, NPAGE)
        smp_select(NB - 2)
        smp_weigh(NB - 1, 0, NPAGE)
        smp_select(NB - 1)
        pe.wait_ge(ssq_s_ready, 1)
        pe.wait_ge(qp_zero, 2)
        for j in range(2):
            mm = nc.tensor.matmul(PS[:, 6, j:j + 1], s_sq[:, P * j:P * j + P], ones[:, 0:1], start=True, stop=True)
        mm.then_inc(ssum_ready, 1)
        pe.wait_ge(sdiag_ready, 2)
        for j in range(2):
            mm = nc.tensor.matmul(PS[:, 5, P * j:P * j + P], ones[:], s_rs[:, j, :], start=True, stop=True)
        mm.then_inc(sfac_ready, 1)
        def turn_x2(t):
            pe.wait_ge(nrm_ready, STEPS + t + 1)
            for h in range(2):
                j = 2 * t + h
                if j >= 4:
                    pe.wait_ge(xt_lo_ready, 2 * STEPS + j - 3)
                for k in range(4):
                    mm = nc.tensor.transpose(PS[:, 4 + j % 4, P * k:P * k + rows(t)],
                                             x2_nrm[0:rows(t), t % 2, P * (4 * h + k):P * (4 * h + k + 1)],
                                             ident[0:rows(t), 0:rows(t)])
                mm.then_inc(xt_ready, 1)

        pe.wait_ge(sout_lo_ready, 1)
        for t in range(STEPS):
            if t >= 2:
                pe.wait_ge(ynrm_ready, t - 1)
            if t == STEPS - 1:
                pe.wait_ge(xt_lo_ready, 2 * STEPS + 2)
            for half in range(2):
                parts = [(a, w, k) for k in range(KD) for a, w in ((act_hi, wo_hi), (act_hi, wo_lo), (act_lo, wo_hi))]
                for j, (a, w, k) in enumerate(parts):
                    if t == 0 and half == 0 and j % 3 == 0:
                        pe.wait_ge(wo_lo_ready, k + 1)
                    mm = nc.tensor.matmul(PS[:, 2 * (t % 2) + half, :], a[:, k, wide(t)], w[:, k, 512 * half:512 * half + 512],
                                          start=(j == 0), stop=(j == len(parts) - 1))
            mm.then_inc(y_ready, 1)
            if t >= 1:
                turn_x2(t - 1)
        turn_x2(STEPS - 1)
        pe.wait_ge(xt_lo_ready, 2 * STEPS + 2 * STEPS)
        pe.wait_ge(st_loaded, 16 * 2 * JF)
        for q in range(6):
            n = min(8, 2 * JF - 8 * q)
            if q >= 2:
                pe.wait_ge(st_taken, q - 1)
            nc.tensor.transpose(PS[:, q % 2, 0:16 * n], st_nat[0:16 * n, q, :], ident[0:16 * n, 0:16 * n]).then_inc(st_turned, 1)
        pe.wait_ge(cw_loaded, 16 * 4)
        for w in range(4):
            mm = nc.tensor.transpose(PS[:, 2, 2 * JF * w:2 * JF * (w + 1)], cw_nat[:, w, :], ident[0:2 * JF, 0:2 * JF])
        mm.then_inc(cw_turned, 1)
        pe.wait_ge(st_taken, 6)
        pe.wait_ge(cw_taken, 1)

        def ffn_pe(i, first, last):
            for t in range(4):
                half = t % 2
                if t == 2 and not first:
                    down_share(i - 1)
                pe.wait_ge(wu_lo_ready, 4 * i + t + 1)
                if not first or t >= 2:
                    pe.wait_ge(h_ready, 4 * i + t - 1)
                    pe.wait_ge(hs_ready, 4 * i + t - 1)
                for c in range(3):
                    parts = [(a, b, k) for k in range(KD) for a, b in ((wu_hi, act_hi), (wu_hi, act_lo), (wu_lo, act_hi))]
                    for j, (a, b, k) in enumerate(parts):
                        mm = nc.tensor.matmul(PS[:, 3 * half + c, 0:CW], a[:, half, k, :], b[:, k, CHUNKS[c]],
                                              start=(j == 0), stop=(j == len(parts) - 1))
                mm.then_inc(up_ready, 1)

        def down_share(i):
            pe.wait_ge(g_lo_ready, 2 * i + 2)
            pe.wait_ge(wd_lo_ready, 2 * i + 2)
            for n in range(YJ):
                t, half = n // 2, n % 2
                pe.wait_ge(ybank_free, YJ * i + n + 1)
                parts = [(g, w, e) for e in range(2) for g, w in ((g_hi, wd_hi), (g_hi, wd_lo), (g_lo, wd_hi))]
                for j, (g, w, e) in enumerate(parts):
                    mm = nc.tensor.matmul(PS[:, 6 + half, :], g[:, e, wide(t)], w[:, e, 512 * half:512 * half + 512],
                                          start=(j == 0), stop=(j == len(parts) - 1))
                mm.then_inc(down_ready, 1)
        iterations(pe, ffn_pe)
        pe.wait_ge(cs_kept, 4 * NIT)
        for q in range(6):
            n = min(8, 2 * JF - 8 * q)
            nc.tensor.transpose(PS[0:16 * n, q, 0:P], stT[:, 8 * q:8 * q + n].rearrange("p j b r -> p (j b r)"), ident[:]).then_inc(st_turned, 1)
        for r in range(2):
            mm = nc.tensor.transpose(PS[0:2 * JF, 0, P * (r + 1):P * (r + 2)], cpT[:, :, r], ident[:])
        mm.then_inc(st_turned, 1)
        down_share(NIT - 1)


_INS = ["x_prompt", "x_sample", "cache_k", "cache_v", "state_conv", "page_table", "rel_bias",
        "norm_mix_pre", "norm_mix_post", "norm_ffn_pre", "norm_ffn_post", "w_in",
        "lambda_q1", "lambda_k1", "lambda_q2", "lambda_k2", "subln_gain", "sgu_ln_gain", "sgu_ln_bias",
        "w_spatial", "b_spatial", "w_out", "w_up", "conv_w", "conv_b", "w_down"]
_OUTS = [(1, SEQ, D), (NB, DS, D), (1, 1, SEQ, H, 2 * DH), (1, 1, SEQ, H, DV), (1, 1, 2, 2 * FF),
         (1, NB, DS, H, 2 * DH), (1, NB, DS, H, DV), (1, NB, 2, 2 * FF), (1, NB, DS, AW)]


def kernel(**inputs):
    import numpy as _np
    import concourse.bacc as _bacc
    from concourse import mybir as _mybir
    from concourse.bass_utils import run_bass_kernel_spmd as _run

    nc = _bacc.Bacc("TRN2", target_bir_lowering=False, num_devices=1)
    arrays, args = {}, []
    given = {name: _np.ascontiguousarray(inputs[name]) for name in _INS}
    given["lines"] = bucket_lines()
    given["select"] = sample_select()
    for name, a in given.items():
        arrays[f"in_{name}_dram"] = a
        args.append(nc.dram_tensor(f"in_{name}_dram", a.shape, _mybir.dt.from_np(a.dtype), kind="ExternalInput").ap())
    for i, shape in enumerate(_OUTS):
        args.append(nc.dram_tensor(f"out_{i}_dram", shape, _mybir.dt.float32, kind="ExternalOutput").ap())
    build(nc, *args)
    r = _run(nc, [arrays], core_ids=[0])
    return tuple(r.results[0][f"out_{i}_dram"] for i in range(len(_OUTS)))
```

```python
import math
from contextlib import ExitStack

import numpy as np

import concourse.bass as bass
from concourse import mybir

ALU = mybir.AluOpType
ACT = mybir.ActivationFunctionType
AX = mybir.AxisListType
F32 = mybir.dt.float32
F32R = mybir.dt.float32r
I32 = mybir.dt.int32

P = 128
D = 1024
KD = D // P
SEQ = 1024
QB = SEQ // P
NB, DS = 8, 8
NS = NB * DS
NTOK = NS + SEQ
CW = 364
NPAD = 3 * CW
STEPS = SEQ // P + 1
H, DH, DV = 4, 64, 128
PAGE, NPAGE = 128, 8
FF = 2816
JF = FF // P
AW = 512
AG = 4
EPS = 1e-6
SUBLN_EPS = 1e-5
LAM_INIT = 0.8 - 0.6 * math.exp(-0.3 * 0)
NEG = -1e30
BUCKETS, MAX_EXACT, MAX_DIST = 32, 16, 128
LINE = 3 * P - 1


def rows(s):
    return P if s < STEPS - 1 else NS


def cols(s):
    return slice(NS + P * s, NS + P * (s + 1)) if s < STEPS - 1 else slice(0, NS)


def wide(s):
    return cols(s) if s < STEPS - 1 else slice(0, P)


def bucket(dist):
    n = np.maximum(dist, 0)
    nf = np.maximum(n, 1).astype(np.float32)
    large = MAX_EXACT + (np.log(nf / np.float32(MAX_EXACT)) / np.float32(math.log(MAX_DIST / MAX_EXACT))
                         * np.float32(BUCKETS - MAX_EXACT)).astype(np.int32)
    return np.where(n < MAX_EXACT, n, np.minimum(large, BUCKETS - 1))


def bucket_lines():
    dist = 2 * P - 1 - np.arange(LINE)
    table = np.zeros((BUCKETS + 1, LINE), np.float32)
    for x, d in enumerate(dist):
        if d >= 0:
            table[bucket(d), x] += 1.0
            table[BUCKETS - 1, x] -= 1.0
        else:
            table[BUCKETS, x] = NEG
    return table


def sample_select():
    r = np.arange(P)
    b2h, m, q = r // 16, r // 8 % 2, r % 8
    table = np.zeros((P, 66), np.float32)
    table[r, b2h * 8 + q] = 1.0
    table[r, 64 + m] = 1.0
    return table


def build(nc, x_prompt, x_sample, cache_k, cache_v, state_conv, page_table, rel_bias,
          norm_mix_pre, norm_mix_post, norm_ffn_pre, norm_ffn_post, w_in,
          lambda_q1, lambda_k1, lambda_q2, lambda_k2, subln_gain, sgu_ln_gain, sgu_ln_bias,
          w_spatial, b_spatial, w_out, w_up, conv_w, conv_b, w_down,
          lines, select,
          y_prompt, y_sample, k_prompt, v_prompt, conv_prompt, k_sample, v_sample, conv_sample, sgu_v_sample):
    ctx = ExitStack()
    with ctx:
        _program(ctx, nc, **{k: v for k, v in locals().items() if k not in ("ctx", "nc")})


def _program(ctx, nc, x_prompt, x_sample, cache_k, cache_v, state_conv, page_table, rel_bias,
             norm_mix_pre, norm_mix_post, norm_ffn_pre, norm_ffn_post, w_in,
             lambda_q1, lambda_k1, lambda_q2, lambda_k2, subln_gain, sgu_ln_gain, sgu_ln_bias,
             w_spatial, b_spatial, w_out, w_up, conv_w, conv_b, w_down,
             lines, select,
             y_prompt, y_sample, k_prompt, v_prompt, conv_prompt, k_sample, v_sample, conv_sample, sgu_v_sample):
    BASE = 16512

    def at(name, offset, shape, dt=F32):
        return nc.alloc_sbuf_tensor_at(name, shape, dt, offset=BASE + offset)

    class Region:

        def __init__(self, start, end):
            self.at, self.end = start, end

        def put(self, name, shape, dt=F32):
            t = at(name, self.at, shape, dt)
            self.at += (int(np.prod(shape[1:])) * 4 + 31) // 32 * 32
            assert self.at <= self.end, (name, self.at, self.end)
            return t

    TOP = 212800
    ACT_BYTES = KD * NPAD * 4
    act_hi = at("act_hi", 0, [P, KD, NPAD], F32R)
    act_lo = at("act_lo", ACT_BYTES, [P, KD, NPAD], F32R)
    keep = Region(2 * ACT_BYTES, 2 * ACT_BYTES + 14000)
    ident = keep.put("ident", [P, P])
    identr = keep.put("identr", [P, P], F32R)
    gain = keep.put("gain", [P, D])
    sub_gain = keep.put("sub_gain", [P, DV])
    small = keep.put("small", [P, 256])
    neg_half = small[:, 0:1]
    ssq = small[:, 16:32]
    rstd = small[:, 32:48]
    mean_sq = small[:, 48:64]
    ln_mv = small[:, 64:96].rearrange("p (s c) -> p s c", c=2)
    ln_rstd = small[:, 96:112]
    lam_sum = small[:, 4:6]
    lam_exp = small[:, 6:8]
    lam_dif = small[:, 8:9]
    neg_lam = small[:, 9:10]
    nmax = small[:, 112:120].rearrange("p (i m) -> p i m", m=2)
    prob_sum = small[:, 120:128].rearrange("p (i m) -> p i m", m=2)
    precip = small[:, 128:136].rearrange("p (i m) -> p i m", m=2)
    pcoef = small[:, 136:140]
    o_ssq = small[:, 140:144]
    o_mean = small[:, 144:148]
    o_rstd = small[:, 148:152]
    o_fac = small[:, 152:156]
    row_coef = small[:, 156:157]
    s_mean = small[:, 240:242]
    s_rstd = small[:, 242:244]
    smp_max = small[:, 160:164]
    smp_sum = small[:, 164:168]
    smp_recip = small[:, 168:172]
    smp_coef = small[:, 172:176]
    gain_col = small[:, 176:177]
    ssq2 = small[:, 180:189]
    rstd2 = small[:, 190:199]
    mean_sq2 = small[:, 200:209]
    ssq3 = small[:, 210:219]
    rstd3 = small[:, 220:229]
    mean_sq3 = small[:, 230:239]
    SCRATCH = keep.at
    scratch = keep.put("scratch", [P, 512])
    v_smp = keep.put("v_smp", [P, AW])
    smp_bias = keep.put("smp_bias", [P, P + 14 * DS])
    select_sb = keep.put("select_sb", [P, 66])
    sq, sk = (at(n, 2 * ACT_BYTES + 1024 + 1024 * i, [P, H, NS]) for i, n in enumerate(("sq", "sk")))
    R0 = keep.at

    proj = Region(R0, TOP)
    qT = proj.put("qT", [P, H, NTOK])
    kT = proj.put("kT", [P, H, NTOK])
    R1 = proj.at
    uT = proj.put("uT", [P, AG, NTOK])
    va = proj.put("va", [P, STEPS, AW])
    R2 = proj.at
    v_all = at("v_all", R2 - STEPS * AW * 4, [P, STEPS, AW])
    GC = 256
    w_raw = proj.put("w_raw", [P, 2, 4, GC])
    w_hi = proj.put("w_hi", [P, 2, KD, GC], F32R)
    w_lo = proj.put("w_lo", [P, 2, KD, GC], F32R)
    norm = Region(R0, R1)
    x_in = norm.put("x_in", [P, 3, D])
    x_nrm = norm.put("x_nrm", [P, 2, D])
    junk = norm.put("junk", [P, D])
    ws_nat = norm.put("ws_nat", [P, AG, P])
    ws_bd = norm.put("ws_bd", [NS, AG, NS])
    gate = Region(proj.at, TOP)
    wsT = gate.put("wsT", [P, AG, P])
    wbT = gate.put("wbT", [NS, AG, NS])
    bs = gate.put("bs", [P, AG, P])
    bs_smp = gate.put("bs_smp", [P, AG, NB, DS])
    ln_g = gate.put("ln_g", [P, AW])
    ln_b = gate.put("ln_b", [P, AW])
    g_sum = gate.put("g_sum", [P, 2, AG, P])
    k_rows = gate.put("k_rows", [P, 2, AW])

    early = Region(R1, R2)
    rel_sb = early.put("rel_sb", [BUCKETS, H])
    rel_rep = early.put("rel_rep", [BUCKETS + 1, H, P])
    lines_sb = early.put("lines_sb", [BUCKETS + 1, LINE])
    line_out = early.put("line_out", [P, H, LINE])
    lam_in = early.put("lam_in", [P, 4, DH])
    lam_prod = early.put("lam_prod", [P, 2, DH])
    toeplitz = nc.dram_tensor("toeplitz", [H, P, LINE], F32)
    att = Region(R2, TOP)
    prob = att.put("prob", [P, 2, 2, SEQ])
    at_sb = att.put("at_sb", [P, 2, SEQ])
    o_nrm = att.put("o_nrm", [P, QB, DV])
    BIAS = TOP - 3 * H * 2 * P * 4
    bias = Region(BIAS, TOP)
    bias_raw = bias.put("bias_raw", [P, H, 2 * P])
    bias_hi = bias.put("bias_hi", [P, H, 2 * P], F32R)
    bias_lo = bias.put("bias_lo", [P, H, 2 * P], F32R)
    V_BYTES = NPAGE * 512 * 4
    V_FIRST = BIAS - V_BYTES - 256
    kpage = at("kpage", R1, [P, 8, 512])
    pages = at("pages", V_FIRST, [1, NB * NPAGE], I32)
    assert att.at <= V_FIRST and 8 * 512 * 4 <= AG * NTOK * 4
    VR = 3

    qk_place = Region(R0, R1)
    kt = qk_place.put("kt", [P, 2, H, 512])
    vpage = [at("vpage0", V_FIRST + 256, [P, NPAGE, 512]), qk_place.put("vpage1", [P, NPAGE, 512])]
    s_at = qk_place.put("s_at", [P, NPAGE, NS])
    W_OUT = V_FIRST - KD * D * 4
    wo_raw = at("wo_raw", W_OUT, [P, KD, D])
    smp = Region(R1 + 8 * 512 * 4, W_OUT)
    vpage.append(smp.put("vpage2", [P, NPAGE, 512]))
    smp = Region(BIAS, TOP)
    QPAD = 8 * 144
    qp = smp.put("qp", [P, QPAD])
    c_mat = smp.put("c_mat", [P, NS])
    s_own = smp.put("s_own", [NS, NS])
    ones = smp.put("ones", [P, P])
    o_rows = smp.put("o_rows", [DS * H, 512])
    tail = Region(smp.at, TOP)
    s_prob = smp.put("s_prob", [P, SEQ + NS])
    s_sq = tail.put("s_sq", [P, H * NS])
    s_rs = tail.put("s_rs", [P, 2, P])
    s_fac = tail.put("s_fac", [P, H * NS])
    s_out = tail.put("s_out", [P, H * NS])
    prj = Region(R0, W_OUT)
    wo_hi = prj.put("wo_hi", [P, KD, D], F32R)
    wo_lo = prj.put("wo_lo", [P, KD, D], F32R)
    top = Region(V_FIRST, TOP)
    x_res = top.put("x_res", [P, 2, D])
    y_nrm = top.put("y_nrm", [P, 2, D])
    x_mid = top.put("x_mid", [P, 2, D])
    split_place = Region(W_OUT, top.at)
    x2_nrm = split_place.put("x2_nrm", [P, 2, D])
    junk2 = split_place.put("junk2", [P, D])
    gain2 = split_place.put("gain2", [P, D])
    AHEAD = split_place.at
    wu_raw = split_place.put("wu_raw", [P, 2, KD, P])
    st_nat = split_place.put("st_nat", [P, 6, P])
    cw_nat = split_place.put("cw_nat", [2 * JF, 4, P])
    assert split_place.at <= V_FIRST
    mid_dram = nc.dram_tensor("mid_dram", [STEPS, P, D], F32)
    ffn = Region(R0, AHEAD)
    ffn2 = Region(split_place.at, TOP)
    y_acc = ffn.put("y_acc", [P, STEPS, D])
    W0 = ffn.at
    wu_hi = ffn.put("wu_hi", [P, 2, KD, P], F32R)
    wu_lo = ffn.put("wu_lo", [P, 2, KD, P], F32R)
    x_back = at("x_back", W0, [P, 3, D])
    wd_raw = ffn.put("wd_raw", [P, 2, D])
    wd_hi = ffn.put("wd_hi", [P, 2, D], F32R)
    wd_lo = ffn.put("wd_lo", [P, 2, D], F32R)
    g_hi = ffn2.put("g_hi", [P, 2, NTOK], F32R)
    g_lo = ffn2.put("g_lo", [P, 2, NTOK], F32R)
    conv = ffn2.put("conv", [P, 2, NTOK])
    stT = ffn.put("stT", [P, 48, NB, 2])
    cpT = ffn.put("cpT", [P, 2 * JF, 2])
    cw = ffn.put("cw", [P, 4, 2, JF])
    cwi = ffn.put("cwi", [P, 4, 2, 2])
    hsw = ffn.put("hsw", [P, 2, 2, NB, 2 + DS])
    cpw = ffn.put("cpw", [P, 2, 2, 2])
    h_sb = [ffn2.put("h_gate", [P, NPAD]), at("h_up", SCRATCH, [P, NPAD])]

    PS = ctx.enter_context(nc.psum_tensor("PS", [P, 8, 512], F32))

    def sem(name):
        return ctx.enter_context(nc.semaphore(name))

    dve_step, pool_step = sem("dve_step"), sem("pool_step")
    steps = {id(dve_step): 0, id(pool_step): 0}

    def own_step(eng, step):
        steps[id(step)] += 1
        eng.wait_ge(step, steps[id(step)])

    x_loaded = [sem(f"x_loaded{i}") for i in range(3)]
    gain_loaded = sem("gain_loaded")
    const_ready = sem("const_ready")
    ssq_ready = sem("ssq_ready")
    rstd_ready = sem("rstd_ready")
    nrm_ready = sem("nrm_ready")
    xt_ready = sem("xt_ready")
    xt_hi_ready = sem("xt_hi_ready")
    xt_lo_ready = sem("xt_lo_ready")
    w_loaded = [sem(f"w_loaded{i}") for i in range(2)]
    w_hi_ready = sem("w_hi_ready")
    w_lo_ready = sem("w_lo_ready")
    job_ready = sem("job_ready")
    act_took = sem("act_took")
    dve_took = sem("dve_took")
    rows_stored = sem("rows_stored")
    mv_ready = sem("mv_ready")
    ln_rstd_ready = sem("ln_rstd_ready")
    vc_ready = sem("vc_ready")
    vn_ready = sem("vn_ready")
    gate_loaded = sem("gate_loaded")
    krow_stored = [sem(f"krow_stored{i}") for i in range(2)]
    v_kept = sem("v_kept")
    bd_zero = sem("bd_zero")
    pad_zero = sem("pad_zero")
    bs_ready = sem("bs_ready")
    ws_turned = sem("ws_turned")
    ws_taken = sem("ws_taken")
    ws_cut = sem("ws_cut")
    gate_mul = sem("gate_mul")
    gate_hi_ready = sem("gate_hi_ready")
    gate_lo_ready = sem("gate_lo_ready")
    sgu_stored = sem("sgu_stored")
    setup_loaded = sem("setup_loaded")
    rep_ready = sem("rep_ready")
    line_ready = sem("line_ready")
    line_taken = sem("line_taken")
    line_stored = sem("line_stored")
    lam_step = sem("lam_step")
    lam_exp_ready = sem("lam_exp_ready")
    lam_ready = sem("lam_ready")
    bias_loaded = sem("bias_loaded")
    bias_hi_ready = sem("bias_hi_ready")
    bias_lo_ready = sem("bias_lo_ready")
    score_ready = sem("score_ready")
    nmax_ready = sem("nmax_ready")
    prob_ready = sem("prob_ready")
    mix_ready = sem("mix_ready")
    turn_ready = sem("turn_ready")
    o_ready = sem("o_ready")
    osq_ready = sem("osq_ready")
    ofac_ready = sem("ofac_ready")
    onrm_ready = sem("onrm_ready")
    ot_ready = sem("ot_ready")
    ot_hi_ready = sem("ot_hi_ready")
    ot_lo_ready = sem("ot_lo_ready")

    x_tiles = [x_prompt[0, P * s:P * (s + 1), :] for s in range(STEPS - 1)] + \
              [x_sample.rearrange("b t d -> (b t) d")]
    v_out = [v_prompt[0, 0, P * s:P * (s + 1)].rearrange("t h d -> t (h d)") for s in range(STEPS - 1)] + \
            [v_sample[0].rearrange("b t h d -> (b t) (h d)")]
    k_out = [k_prompt[0, 0, P * s:P * (s + 1)].rearrange("t h d -> t (h d)") for s in range(STEPS - 1)] + \
            [k_sample[0].rearrange("b t h d -> (b t) (h d)")]

    QC, KC, VC, UC, AC = 0, 512, 1024, 1536, 2048
    GROUPS = [("va", 0), ("va", 1), ("u", 0), ("u", 1), ("k", 0), ("k", 1), ("q", 0), ("q", 1), ("v", 0), ("v", 1)]
    W_COL = {"va": AC, "u": UC, "k": KC, "q": QC, "v": VC}
    CHUNKS = [slice(CW * c, CW * (c + 1)) for c in range(3)]
    KEPT = [slice(CW * c, min(CW * (c + 1), NTOK)) for c in range(3)]
    jobs = []
    for g, (kind, half) in enumerate(GROUPS):
        if kind in ("va", "v"):
            jobs += [(kind, g, half, 0, s) for s in range(STEPS)]
        else:
            jobs += [(kind, g, half, f, c) for f in range(2) for c in range(3)]
    plan = list(jobs)
    jobs = []
    gates, krows = iter(range(STEPS)), iter(range(STEPS))
    for job in plan:
        jobs.append(job)
        if job[0] == "k":
            jobs += [("gate", job[1], 0, 0, s) for _, s in zip(range(1), gates)]
        if job[0] == "q":
            jobs += [("krow", job[1], 0, 0, s) for _, s in zip(range(1), krows)]
    ON_ACT = ("va", "u", "krow")
    bank_of = [4 + n % 4 if n < STEPS else n % 8 for n in range(len(jobs))]
    took = []
    n_act = n_dve = 0
    for job in jobs:
        if job[0] in ON_ACT:
            n_act += 1
            took.append((act_took, n_act))
        else:
            n_dve += 1
            took.append((dve_took, n_dve))
    first_of = {}
    for n, job in enumerate(jobs):
        first_of.setdefault(job[1], n)
    last_k_took = max(took[n][1] for n, job in enumerate(jobs) if job[0] == "k")
    last_gate = max(n for n, job in enumerate(jobs) if job[0] == "gate")
    n_u_done = max(took[n][1] for n, job in enumerate(jobs) if job[0] == "u")

    NSTEP = H * QB

    OB = 4

    def turns(i):
        return (i % QB + 4) // 4

    def turns_before(i):
        return sum(turns(j) for j in range(i))

    sbias_loaded = sem("sbias_loaded")
    sbias_zero = sem("sbias_zero")
    sel_loaded = sem("sel_loaded")
    page_loaded = sem("page_loaded")
    kp_loaded = [sem(f"kp_loaded{i}") for i in range(2)]
    vp_loaded = [sem(f"vp_loaded{i}") for i in range(3)]
    qp_zero = sem("qp_zero")
    at_taken = sem("at_taken")
    sqk_ready = sem("sqk_ready")
    qp_ready = sem("qp_ready")
    kt_ready = [sem(f"kt_ready{i}") for i in range(2)]
    sdiag_ready = sem("sdiag_ready")
    orows_ready = sem("orows_ready")
    osel_ready = sem("osel_ready")
    wo_loaded = sem("wo_loaded")
    sfac_ready = sem("sfac_ready")
    kturn_ready = sem("kturn_ready")
    sscore_ready = sem("sscore_ready")
    smax_ready = sem("smax_ready")
    sprob_ready = sem("sprob_ready")
    cmat_ready = sem("cmat_ready")
    sat_ready = sem("sat_ready")
    sat_taken = sem("sat_taken")
    pv_ready = sem("pv_ready")
    ssq_s_ready = sem("ssq_s_ready")
    ssum_ready = sem("ssum_ready")
    smean_ready = sem("smean_ready")
    srstd_ready = sem("srstd_ready")
    sout_ready = sem("sout_ready")
    sout_hi_ready = sem("sout_hi_ready")
    sout_lo_ready = sem("sout_lo_ready")
    rowcoef_step = sem("rowcoef_step")
    wo_hi_ready = sem("wo_hi_ready")
    wo_lo_ready = sem("wo_lo_ready")
    xres_loaded = [sem(f"xres_loaded{i}") for i in range(2)]
    y_ready = sem("y_ready")
    yssq_ready = sem("yssq_ready")
    yrstd_ready = sem("yrstd_ready")
    ynrm_ready = sem("ynrm_ready")
    xmid_ready = sem("xmid_ready")
    xmid_stored = [sem(f"xmid_stored{i}") for i in range(2)]
    st_loaded = sem("st_loaded")
    cw_loaded = sem("cw_loaded")
    st_turned = sem("st_turned")
    st_taken = sem("st_taken")
    cw_turned = sem("cw_turned")
    cw_taken = sem("cw_taken")
    yacc_zero = sem("yacc_zero")
    cwi_ready = sem("cwi_ready")
    hsp_ready = sem("hsp_ready")
    wu_hi_ready = sem("wu_hi_ready")
    wu_lo_ready = sem("wu_lo_ready")
    wd_loaded = [sem(f"wd_loaded{i}") for i in range(2)]
    wd_hi_ready = sem("wd_hi_ready")
    wd_lo_ready = sem("wd_lo_ready")
    up_ready = sem("up_ready")
    conv_ready = sem("conv_ready")
    tap1_ready = sem("tap1_ready")
    tap_ready = sem("tap_ready")
    stap_ready = sem("stap_ready")
    h_ready = sem("h_ready")
    hs_ready = sem("hs_ready")
    silu_ready = sem("silu_ready")
    prod_ready = sem("prod_ready")
    g_hi_ready = sem("g_hi_ready")
    g_lo_ready = sem("g_lo_ready")
    down_ready = sem("down_ready")
    ybank_free = sem("ybank_free")
    cs_kept = sem("cs_kept")
    cs_stored = sem("cs_stored")
    fout_ready = sem("fout_ready")
    y_stored = sem("y_stored")

    OUT_BASE = 16 * len(GROUPS)
    UP_BASE = OUT_BASE

    Y_BANK = [4, 6]
    TURN_BANK = [0, 3, 1, 2]
    CW_AT = 192
    LAST_BANK = [6, 7, 2, 3, 4, 5]

    NIT = JF // 2
    YJ = 2 * STEPS

    block = ctx.enter_context(nc.Block())

    def iterations(eng, body):
        body(0, True, False)
        with eng.Fori(1, NIT - 1) as i:
            body(i, False, False)
        body(NIT - 1, False, True)

    def load_smp_bias(eng):
        eng.wait_ge(line_stored, 16)
        eng.wait_ge(sbias_zero, 1)
        for b2 in range(2):
            for h in range(H):
                for m in range(2):
                    r = 64 * b2 + 16 * h + 8 * m
                    base = h * P * LINE + P - 1
                    eng.dma_start(smp_bias[r:r + 8, 0:P], bass.AP(toeplitz, base, [[LINE - 1, 8], [1, P]])).then_inc(sbias_loaded, 16)
                    c = P + DS * (6 + b2)
                    eng.dma_start(smp_bias[r:r + 8, c:c + DS],
                                  bass.AP(toeplitz, base + P, [[LINE - 1, 8], [1, DS]])).then_inc(sbias_loaded, 16)

    def state_rows(states, q, n):
        return states[0].rearrange("b r (j c) -> j (b r) c", c=P)[8 * q:8 * q + n]

    def load_w(sp, p):
        kind, half = GROUPS[p // 2]
        c0 = W_COL[kind] + GC * half
        src = w_in[0, 512 * (p % 2):512 * (p % 2 + 1), c0:c0 + GC].rearrange("(k p) c -> p k c", p=P)
        sp.dma_start(w_raw[:, p % 2], src).then_inc(w_loaded[p % 2], 16)

    def act_split_w(act, g):
        for p in (2 * g, 2 * g + 1):
            act.wait_ge(w_loaded[p % 2], 16 * (p // 2 + 1))
            if g >= 2:
                act.wait_ge(job_ready, first_of[g - 1])
            nc.scalar.copy(w_hi[:, g % 2, 4 * (p % 2):4 * (p % 2) + 4, :], w_raw[:, p % 2]).then_inc(w_hi_ready, 1)

    def dve_split_w(dve, g):
        for p in (2 * g, 2 * g + 1):
            ks = slice(4 * (p % 2), 4 * (p % 2) + 4)
            dve.wait_ge(w_hi_ready, p + 1)
            nc.vector.tensor_tensor(w_lo[:, g % 2, ks, :], w_raw[:, p % 2], w_hi[:, g % 2, ks, :].bitcast(F32),
                                    ALU.subtract).then_inc(w_lo_ready, 1)

    @block.sync
    def _(sp):
        for s in range(STEPS):
            if s >= 3:
                sp.wait_ge(nrm_ready, s - 2)
            sp.dma_start(x_in[0:rows(s), s % 3, :], x_tiles[s]).then_inc(x_loaded[s % 3], 16)
            if s == 0:
                sp.dma_start(gain[:], norm_mix_pre[0:1, :].to_broadcast([P, D])).then_inc(gain_loaded, 16)
            if s == 2:
                for p in range(2):
                    load_w(sp, p)
                sp.dma_start(rel_sb[:], rel_bias[:, :]).then_inc(setup_loaded, 16)
                sp.dma_start(lines_sb[:], lines[:, :]).then_inc(setup_loaded, 16)
                for i, lam in enumerate((lambda_q1, lambda_q2, lambda_k1, lambda_k2)):
                    sp.dma_start(lam_in[:, i, :], lam[0:1, :].to_broadcast([P, DH])).then_inc(setup_loaded, 16)
                sp.dma_start(sub_gain[:], subln_gain[0:1, :].to_broadcast([P, DV])).then_inc(setup_loaded, 16)
            if s == 4:
                for p in range(2, 4):
                    sp.wait_ge(w_lo_ready, p - 1)
                    load_w(sp, p)
            if s == 5:
                sp.dma_start(ws_nat[:], w_spatial[0].rearrange("g t s -> t g s")).then_inc(gate_loaded, 16)
                sp.wait_ge(bd_zero, 1)
                for b in range(NB):
                    o = slice(DS * b, DS * (b + 1))
                    sp.dma_start(ws_bd[o, :, o], w_spatial[0, :, 0:DS, 0:DS].rearrange("g t s -> t g s")).then_inc(gate_loaded, 16)
                sp.dma_start(bs[:], b_spatial[0:1].to_broadcast([P, AG, P])).then_inc(gate_loaded, 16)
                sp.dma_start(ln_g[:], sgu_ln_gain[0:1, :].to_broadcast([P, AW])).then_inc(gate_loaded, 16)
                sp.dma_start(ln_b[:], sgu_ln_bias[0:1, :].to_broadcast([P, AW])).then_inc(gate_loaded, 16)
        for p in range(4, 2 * len(GROUPS)):
            sp.wait_ge(w_lo_ready, p - 1)
            load_w(sp, p)
        load_smp_bias(sp)
        sp.dma_start(select_sb[:], select[:, :]).then_inc(sel_loaded, 16)
        sp.dma_start(gain_col, subln_gain.rearrange("a d -> d a")).then_inc(sel_loaded, 16)
        sp.wait_ge(gate_mul, STEPS)
        for i in range(2):
            sp.wait_ge(krow_stored[i], 16 * ((STEPS + 1 - i) // 2))
        skewed = bass.AP(toeplitz, P - 1, [[LINE - 1, P], [P * LINE, H], [1, 2 * P]])
        sp.dma_start(bias_raw[:], skewed).then_inc(bias_loaded, 16)
        v_jobs = [n for n, job in enumerate(jobs) if job[0] == "v"]
        for i, n in enumerate(v_jobs):
            kind, g, half, f, s = jobs[n]
            if half == 1:
                sp.wait_ge(*took[n])
                sp.dma_start(v_out[s], v_all[0:rows(s), s, :]).then_inc(rows_stored, 16)
        sp.wait_ge(dve_took, n_dve)
        sp.dma_start(pages[:], page_table.rearrange("b n -> (b n)").rearrange("(a n) -> a n", a=1)).then_inc(page_loaded, 16)
        sp.wait_ge(page_loaded, 16)
        sp.wait_ge(gate_lo_ready, AG)
        n_pool = cache_k.shape[1]

        def load_keys(b):
            for p in range(NPAGE):
                if b >= 1:
                    sp.wait_ge(kturn_ready, NPAGE * (b - 1) + p + 1)
                page = sp.value_load(pages[0:1, NPAGE * b + p:NPAGE * b + p + 1], min_val=0, max_val=n_pool - 1)
                sp.dma_start(kpage[:, p, :], cache_k[0, bass.ds(page, 1)].rearrange("a t h d -> t (a h d)")).then_inc(kp_loaded[p // 4], 16)

        def load_values(b):
            if b >= VR:
                sp.wait_ge(pv_ready, b - VR + 1)
            elif b == 1:
                sp.wait_ge(ot_ready, NSTEP // OB)
                sp.wait_ge(rows_stored, 16 * STEPS)
            for p in range(NPAGE):
                page = sp.value_load(pages[0:1, NPAGE * b + p:NPAGE * b + p + 1], min_val=0, max_val=n_pool - 1)
                sp.dma_start(vpage[b % VR][:, p, :], cache_v[0, bass.ds(page, 1)].rearrange("a t h d -> t (a h d)")).then_inc(vp_loaded[b % VR], 16)
        load_keys(0)
        load_values(0)
        for b in range(1, NB):
            load_keys(b)
            if b >= 2:
                load_values(b - 1)
            if b >= 4:
                for k in range(2 * (b - 4), 2 * (b - 4) + 2):
                    if k == 0:
                        sp.wait_ge(v_kept, 2)
                    sp.dma_start(wo_raw[:, k, :], w_out[0, P * k:P * k + P, :]).then_inc(wo_loaded, 16)
        load_values(NB - 1)
        sp.wait_ge(sout_lo_ready, 1)
        sp.dma_start(gain[:], norm_mix_post[0:1, :].to_broadcast([P, D])).then_inc(gain_loaded, 16)
        sp.wait_ge(wo_lo_ready, KD)
        sp.dma_start(gain2[:], norm_ffn_pre[0:1, :].to_broadcast([P, D])).then_inc(gain_loaded, 16)
        for t in range(STEPS + 1):
            if t < STEPS:
                if t >= 2:
                    sp.wait_ge(xmid_ready, t - 1)
                sp.dma_start(x_res[0:rows(t), t % 2, :], x_tiles[t]).then_inc(xres_loaded[t % 2], 16)
            if t >= 1:
                sp.wait_ge(xmid_ready, t)
                sp.dma_start(mid_dram[t - 1, 0:rows(t - 1), :], x_mid[0:rows(t - 1), (t - 1) % 2, :]).then_inc(xmid_stored[(t - 1) % 2], 16)
            if t == 0:
                for q in range(6):
                    n = min(8, 2 * JF - 8 * q)
                    sp.dma_start(st_nat[0:16 * n, q, :], state_rows(state_conv, q, n)).then_inc(st_loaded, 16)
                for w in range(3):
                    sp.dma_start(cw_nat[:, w, :], conv_w[0, w].rearrange("(j c) -> j c", c=P)).then_inc(cw_loaded, 16)
                sp.dma_start(cw_nat[:, 3, :], conv_b[0].rearrange("(j c) -> j c", c=P)).then_inc(cw_loaded, 16)
                for e in range(2):
                    sp.dma_start(wu_raw[:, e], w_up[0, :, FF * e:FF * e + P].rearrange("(k p) c -> p k c", p=P)).then_inc(w_loaded[e], 16)
        sp.wait_ge(xt_lo_ready, 2 * STEPS + 2 * STEPS)
        for i in range(2):
            sp.wait_ge(xmid_stored[i], 16 * ((STEPS + 1 - i) // 2))
        sp.dma_start(gain[:], norm_ffn_post[0:1, :].to_broadcast([P, D])).then_inc(gain_loaded, 16)

        def load_ffn(i, first, last):
            for t in range(2 if first else 0, 4):
                sp.wait_ge(wu_lo_ready, 4 * i + t - 1)
                c0 = (t % 2) * FF + P * (t // 2) + 2 * P * i
                src = w_up[0, :, bass.ds(c0, P)].rearrange("(k p) c -> p k c", p=P)
                sp.dma_start(wu_raw[:, t % 2], src).then_inc(w_loaded[t % 2], 16)
            for e in range(2):
                if not first:
                    sp.wait_ge(wd_lo_ready, 2 * i + e - 1)
                sp.dma_start(wd_raw[:, e, :], w_down[0, bass.ds(2 * P * i + P * e, P), :]).then_inc(wd_loaded[e], 16)
        iterations(sp, load_ffn)
        sp.wait_ge(up_ready, 4 * NIT)
        for t in range(STEPS + 1):
            if t < STEPS:
                if t >= 3:
                    sp.wait_ge(fout_ready, t - 2)
                sp.dma_start(x_back[0:rows(t), t % 3, :], mid_dram[t, 0:rows(t), :]).then_inc(x_loaded[t % 3], 16)
            if t >= 1:
                sp.wait_ge(fout_ready, t)
                dst = y_prompt[0, P * (t - 1):P * t, :] if t < STEPS else y_sample.rearrange("b t d -> (b t) d")
                sp.dma_start(dst, y_acc[0:rows(t - 1), t - 1, :]).then_inc(y_stored, 16)
        for q in range(6):
            sp.wait_ge(st_taken, 2 + q + 1)
            n = min(8, 2 * JF - 8 * q)
            sp.dma_start(state_rows(conv_sample, q, n), st_nat[0:16 * n, q, :]).then_inc(cs_stored, 16)
        sp.wait_ge(st_taken, 2 + 7)
        sp.dma_start(conv_prompt[0, 0].rearrange("r (j c) -> j r c", c=P), cw_nat[:, 0:2, :]).then_inc(cs_stored, 16)
        sp.wait_ge(cs_stored, 16 * (6 + 1))
        sp.wait_ge(y_stored, 16 * STEPS)

    @block.scalar
    def _(act):
        def take_job(n):
            kind, g, half, f, c = jobs[n]
            act.wait_ge(job_ready, n + 1)
            if kind == "va":
                nc.scalar.activation(va[0:rows(c), c, GC * half:GC * half + GC], PS[0:rows(c), bank_of[n], 0:GC],
                                     ACT.Gelu_apprx_tanh).then_inc(act_took, 1)
            elif kind == "u":
                act.wait_ge(line_stored, 16)
                act.wait_ge(lam_ready, 1)
                w = KEPT[c].stop - KEPT[c].start
                nc.scalar.activation(uT[:, 2 * half + f, KEPT[c]], PS[:, bank_of[n], 0:w],
                                     ACT.Gelu_apprx_tanh).then_inc(act_took, 1)
            else:
                if c >= 2:
                    act.wait_ge(krow_stored[c % 2], 16 * (c // 2))
                nc.scalar.copy(k_rows[0:rows(c), c % 2, :], PS[0:rows(c), bank_of[n], :]).then_inc(act_took, 1)
                act.wait_ge(act_took, took[n][1])
                act.dma_start(k_out[c], k_rows[0:rows(c), c % 2, :]).then_inc(krow_stored[c % 2], 16)

        def xt_hi(s):
            for h in range(2):
                act.wait_ge(xt_ready, 2 * s + h + 1)
                src = PS[:, (2 * s + h) % 4, :].rearrange("p (k t) -> p k t", k=4)[:, :, 0:rows(s)]
                nc.scalar.copy(act_hi[:, 4 * h:4 * h + 4, cols(s)], src).then_inc(xt_hi_ready, 1)
        act.wait_ge(const_ready, 3)
        for s in range(STEPS):
            act.wait_ge(x_loaded[s % 3], 16 * (s // 3 + 1))
            if s >= 1:
                act.wait_ge(ssq_ready, s)
            nc.scalar.activation(junk[0:rows(s), :], x_in[0:rows(s), s % 3, :], ACT.Square,
                                 accum_out=ssq[0:rows(s), s:s + 1]).then_inc(ssq_ready, 1)
            if s >= 1:
                xt_hi(s - 1)
            if s == 0:
                act_split_w(act, 0)
            if s >= 3:
                take_job(s - 3)
            if s == 7:
                act_split_w(act, 1)
            if s == 4:
                act.wait_ge(line_taken, H)
                act.dma_start(bass.AP(toeplitz, 0, [[LINE, P], [P * LINE, H], [1, LINE]]), line_out[:]).then_inc(line_stored, 16)
        xt_hi(STEPS - 1)
        act.wait_ge(ws_turned, 1)
        nc.scalar.copy(wsT[:], PS[:, 2, :].rearrange("p (g t) -> p g t", g=AG)).then_inc(ws_taken, 1)
        act.wait_ge(ws_turned, 2)
        nc.scalar.copy(wbT[:], PS[0:NS, 3, 0:AG * NS].rearrange("p (g t) -> p g t", g=AG)).then_inc(ws_taken, 1)
        for n in range(STEPS - 3, STEPS):
            take_job(n)
        act.wait_ge(lam_step, 3)
        nc.scalar.activation(lam_exp, lam_sum, ACT.Exp).then_inc(lam_exp_ready, 1)
        split = 1
        for n, (kind, g, half, f, c) in enumerate(jobs):
            if g > split - 1 and g + 1 < len(GROUPS) and g + 1 > split:
                split = g + 1
                act_split_w(act, split)
            if kind in ON_ACT and n >= STEPS:
                take_job(n)
        act.wait_ge(bias_loaded, 16)
        nc.scalar.copy(bias_hi[:], bias_raw[:]).then_inc(bias_hi_ready, 1)
        act.wait_ge(dve_took, n_dve)
        act.wait_ge(gate_mul, STEPS)

        def gated_hi(g):
            nc.scalar.copy(act_hi[:, 4 + g, 0:NTOK], uT[:, g, :]).then_inc(gate_hi_ready, 1)
        for i in range(2):
            act.wait_ge(krow_stored[i], 16 * ((STEPS + 1 - i) // 2))
        def take_turned(i):
            for t in range(turns(i)):
                act.wait_ge(turn_ready, turns_before(i) + t + 1)
                if i >= 2:
                    act.wait_ge(o_ready, i - 1)
                w = slice(512 * t, min(512 * (t + 1), P * (i % QB + 1)))
                bank = 4 + (turns_before(i) + t) % 2
                nc.scalar.copy(at_sb[:, i % 2, w], PS[:, bank, 0:w.stop - w.start]).then_inc(at_taken, 1)

        def exponent(i, m):
            act.wait_ge(nmax_ready, 2 * i + m + 1)
            if i >= 2:
                act.wait_ge(turn_ready, turns_before(i - 1))
            w = P * (i % QB + 1)
            src = PS[:, 2 * m:2 * m + 2, :].rearrange("p a b -> p (a b)")[:, 0:w]
            nc.scalar.activation(prob[:, i % 2, m, 0:w], src, ACT.Exp, bias=nmax[:, i % 4, m:m + 1],
                                 accum_out=prob_sum[:, i % 4, m:m + 1]).then_inc(prob_ready, 1)

        def out_square(i):
            act.wait_ge(o_ready, i + 1)
            if i >= 1:
                act.wait_ge(osq_ready, i)
            nc.scalar.activation(scratch[:, 0:DV], PS[:, 6, 0:DV], ACT.Square, scale=precip[:, i % 4, 0:1],
                                 accum_out=o_ssq[:, i % 4:i % 4 + 1]).then_inc(osq_ready, 1)

        def out_hi(g):
            act.wait_ge(ot_ready, g + 1)
            c0 = NS + P * OB * (g % (QB // OB))
            nc.scalar.copy(act_hi[:, g * OB // QB, c0:c0 + P * OB], PS[:, 7, :]).then_inc(ot_hi_ready, 1)

        nc.scalar.copy(sq[:], qT[:, :, 0:NS]).then_inc(sqk_ready, 1)
        nc.scalar.copy(sk[:], kT[:, :, 0:NS]).then_inc(sqk_ready, 1)
        for i in range(NSTEP + 4):
            if i < NSTEP:
                exponent(i, 0)
            if 0 <= i - 2 < NSTEP:
                out_square(i - 2)
            if 0 <= i - 1 < NSTEP:
                take_turned(i - 1)
            if i < NSTEP:
                exponent(i, 1)
            if i < AG:
                gated_hi(i)
            if i >= OB + 3 and (i - OB - 3) % OB == 0:
                out_hi((i - OB - 3) // OB)
        def take_keys(n):
            u, p = n // 4, n % 4
            act.wait_ge(kturn_ready, n + 1)
            if u >= 2:
                act.wait_ge(sscore_ready, u - 1)
            src = PS[:, 3 + n % 2, :].rearrange("p (h t) -> p h t", h=H)
            nc.scalar.copy(kt[:, u % 2, :, P * p:P * p + P], src).then_inc(kt_ready[1], 1)

        def smp_exponent(pr):
            act.wait_ge(smax_ready, pr + 1)
            if pr >= 1:
                act.wait_ge(sat_ready, 2 * pr)
            nc.scalar.activation(s_prob[:], PS[:, 0:3, :].rearrange("p a b -> p (a b)")[:, 0:SEQ + NS], ACT.Exp,
                                 bias=smp_max[:, pr:pr + 1], accum_out=smp_sum[:, pr:pr + 1]).then_inc(sprob_ready, 1)

        def smp_take(pr):
            act.wait_ge(sat_ready, 2 * pr + 1)
            if pr >= 1:
                act.wait_ge(pv_ready, 2 * pr)
            nc.scalar.copy(s_at[:], PS[:, 5, :].rearrange("p (n c) -> p n c", n=NPAGE)).then_inc(sat_taken, 1)

        def smp_take_own(pr):
            act.wait_ge(sat_ready, 2 * pr + 2)
            nc.scalar.copy(s_own[:], PS[0:NS, 5, 0:NS]).then_inc(sat_taken, 1)

        act.wait_ge(ot_lo_ready, NSTEP // OB)
        act.wait_ge(ot_ready, NSTEP // OB)
        for u in range(2 * NB + 1):
            if u < 2 * NB:
                take_keys(4 * u + 1)
            if u % 4 == 2 and u >= 6:
                smp_take(u // 4 - 1)
            if u % 4 == 3 and u >= 7:
                smp_take_own(u // 4 - 1)
            if u < 2 * NB:
                take_keys(4 * u + 3)
            if u % 4 == 0 and u >= 4:
                smp_exponent(u // 4 - 1)
        smp_take(NB // 2 - 1)
        smp_take_own(NB // 2 - 1)
        act.wait_ge(osel_ready, NB)
        nc.scalar.activation(s_sq[:], PS[:, 7, 0:H * NS], ACT.Square).then_inc(ssq_s_ready, 1)
        act.wait_ge(sout_ready, 1)
        nc.scalar.copy(act_hi[:, 0:H, 0:NS], s_out[:].rearrange("p (h c) -> p h c", h=H)).then_inc(sout_hi_ready, 1)
        act.wait_ge(wo_loaded, 16 * KD)
        for k in range(KD):
            nc.scalar.copy(wo_hi[:, k, :], wo_raw[:, k, :]).then_inc(wo_hi_ready, 1)
        act.wait_ge(wo_lo_ready, KD)

        def x2_hi(t):
            for h in range(2):
                act.wait_ge(xt_ready, 2 * STEPS + 2 * t + h + 1)
                src = PS[:, TURN_BANK[(2 * t + h) % 4], :].rearrange("p (k t) -> p k t", k=4)[:, :, 0:rows(t)]
                nc.scalar.copy(act_hi[:, 4 * h:4 * h + 4, cols(t)], src).then_inc(xt_hi_ready, 1)
        def wu_hi_first(half):
            act.wait_ge(w_loaded[half], UP_BASE + 16)
            nc.scalar.copy(wu_hi[:, half], wu_raw[:, half]).then_inc(wu_hi_ready, 1)

        for t in range(STEPS):
            r, j = rows(t), Y_BANK[t % 2]
            act.wait_ge(y_ready, t + 1)
            if t >= 1:
                act.wait_ge(ssq_ready, STEPS + t)
            nc.scalar.activation(junk2[0:r, :], PS[0:r, j:j + 2, :].rearrange("p a b -> p (a b)"), ACT.Square,
                                 accum_out=ssq2[0:r, t:t + 1]).then_inc(yssq_ready, 1)
            if t == STEPS - 1:
                x2_hi(t - 2)
                x2_hi(t - 1)
                wu_hi_first(0)
            act.wait_ge(xmid_ready, t + 1)
            act.wait_ge(yssq_ready, t + 1)
            nc.scalar.activation(junk2[0:r, :], x_mid[0:r, t % 2, :], ACT.Square,
                                 accum_out=ssq3[0:r, t:t + 1]).then_inc(ssq_ready, 1)
            if 2 <= t < STEPS - 1:
                x2_hi(t - 2)
        wu_hi_first(1)
        x2_hi(STEPS - 1)
        def ffn_act(i, first, last):
            def split(t, ahead):
                n = 4 * i + t + ahead
                act.wait_ge(w_loaded[(t + ahead) % 2], UP_BASE + 8 * (n - (t + ahead) % 2) + 16)
                if ahead == 2:
                    act.wait_ge(up_ready, 4 * i + t + 1)
                nc.scalar.copy(wu_hi[:, (t + ahead) % 2], wu_raw[:, (t + ahead) % 2]).then_inc(wu_hi_ready, 1)

            if first:
                act.wait_ge(yacc_zero, 1)
            act.wait_ge(cwi_ready, i + 1)
            act.wait_ge(hsp_ready, 2 * i + 2)
            for t in range(4):
                e, half = t // 2, t % 2
                act.wait_ge(up_ready, 4 * i + t + 1)
                if not first or t >= 2:
                    act.wait_ge(tap_ready, 4 * i + t - 1)
                h = h_sb[half]
                nc.scalar.copy(h[:].rearrange("p (c t) -> p c t", c=3), PS[:, 3 * half:3 * half + 3, 0:CW]).then_inc(h_ready, 1)
                nc.scalar.copy(hsw[:, half, e, :, 2:], PS[:, 3 * half, 0:NS].rearrange("p (b q) -> p b q", b=NB)).then_inc(hs_ready, 1)
                if not first or t >= 2:
                    act.wait_ge(prod_ready if half == 0 else g_lo_ready, 2 * i + e)
                act.wait_ge(h_ready, 4 * i + t + 1)
                if half == 0 and (not first or t >= 2):
                    act.wait_ge(silu_ready, 2 * i + e)
                tap, bias = cwi[:, 2, half, e:e + 1], cwi[:, 3, half, e:e + 1]
                nc.scalar.activation(conv[:, half, :], h[:, 0:NTOK], ACT.Identity, bias=bias, scale=tap).then_inc(conv_ready, 1)
                if not (last and t >= 2):
                    split(t, 2)
                if half == 0:
                    act.wait_ge(tap_ready, 4 * i + t + 1)
                    nc.scalar.activation(conv[:, 0, :], conv[:, 0, :], ACT.Silu).then_inc(silu_ready, 1)
                else:
                    act.wait_ge(prod_ready, 2 * i + e + 1)
                    if not first:
                        act.wait_ge(down_ready, YJ * i)
                    nc.scalar.copy(g_hi[:, e, :], conv[:, 1, :]).then_inc(g_hi_ready, 1)
                    if t == 1:
                        for k in range(2):
                            act.wait_ge(wd_loaded[k], 16 * i + 16)
                            nc.scalar.copy(wd_hi[:, k, :], wd_raw[:, k, :]).then_inc(wd_hi_ready, 1)
        iterations(act, ffn_act)
        for t in range(STEPS):
            r = rows(t)
            act.wait_ge(ybank_free, YJ * (NIT - 1) + 2 * t + 4)
            if t >= 1:
                act.wait_ge(ssq_ready, 2 * STEPS + t)
            nc.scalar.activation(conv[0:r, 0, 0:D], y_acc[0:r, t, :], ACT.Square, accum_out=ssq[0:r, t:t + 1]).then_inc(ssq_ready, 1)

    @block.gpsimd
    def _(pool):
        nc.gpsimd.memset(ident[:], 0.0).then_inc(const_ready, 1)
        pool.wait_ge(const_ready, 1)
        nc.gpsimd.affine_select(out=ident[:], in_=ident[:], compare_op=ALU.not_equal, fill=1.0, base=0,
                                pattern=[[-1, P]], channel_multiplier=1).then_inc(const_ready, 1)
        nc.gpsimd.memset(small[:], -0.5).then_inc(const_ready, 1)
        nc.gpsimd.memset(smp_bias[:], NEG).then_inc(sbias_zero, 1)
        nc.gpsimd.memset(ws_bd[:], 0.0).then_inc(bd_zero, 1)
        for a in (act_hi, act_lo):
            nc.gpsimd.memset(a[:, :, NTOK:].bitcast(F32), 0.0).then_inc(pad_zero, 1)
        pool.wait_ge(const_ready, 3)
        nc.gpsimd.tensor_copy(identr[:], ident[:]).then_inc(const_ready, 1)

        def root(src, dst, i, n, scale, eps, done_sem):
            nc.gpsimd.tensor_scalar(mean_sq[0:n, i:i + 1], src, scale, eps, ALU.mult, ALU.add).then_inc(pool_step, 1)
            own_step(pool, pool_step)
            nc.gpsimd.tensor_tensor(dst, mean_sq[0:n, i:i + 1], neg_half[0:n], ALU.pow).then_inc(done_sem, 1)

        for s in range(STEPS):
            r = rows(s)
            pool.wait_ge(ssq_ready, s + 1)
            root(ssq[0:r, s:s + 1], rstd[0:r, s:s + 1], s, r, 1.0 / D, EPS, rstd_ready)
        pool.wait_ge(gate_loaded, 16 * (4 + NB))
        for b in range(NB):
            nc.gpsimd.tensor_copy(bs_smp[:, :, b, :], bs[:, :, 0:DS]).then_inc(bs_ready, 1)
        for i, w in enumerate((wsT, wbT)):
            pool.wait_ge(ws_taken, i + 1)
            n = P if i == 0 else NS
            nc.gpsimd.affine_select(out=w[:], in_=w[:], compare_op=ALU.is_ge, fill=0.0, base=0,
                                    pattern=[[0, AG], [1, n]], channel_multiplier=-1).then_inc(ws_cut, 1)
        for s in range(STEPS):
            r = rows(s)
            pool.wait_ge(mv_ready, s + 1)
            root(ln_mv[0:r, s, 1:2], ln_rstd[0:r, s:s + 1], s, r, 1.0, EPS, ln_rstd_ready)
            pool.wait_ge(vc_ready, s + 1)
            nc.gpsimd.tensor_tensor(va[0:r, s, :], va[0:r, s, :], ln_g[0:r, :], ALU.mult).then_inc(pool_step, 1)
            own_step(pool, pool_step)
            nc.gpsimd.tensor_tensor(va[0:r, s, :], va[0:r, s, :], ln_b[0:r, :], ALU.add).then_inc(vn_ready, 1)
        pool.wait_ge(vn_ready, STEPS)
        pool.dma_start(sgu_v_sample[0].rearrange("b t c -> (b t) c"), va[0:NS, STEPS - 1, :]).then_inc(sgu_stored, 16)
        pool.wait_ge(sgu_stored, 16)
        for i in range(NSTEP):
            c = slice(i % 4, i % 4 + 1)
            pool.wait_ge(osq_ready, i + 1)
            nc.gpsimd.tensor_scalar(o_mean[:, c], o_ssq[:, c], 1.0 / DV, SUBLN_EPS, ALU.mult, ALU.add).then_inc(pool_step, 1)
            own_step(pool, pool_step)
            nc.gpsimd.tensor_tensor(o_rstd[:, c], o_mean[:, c], neg_half, ALU.pow).then_inc(pool_step, 1)
            own_step(pool, pool_step)
            nc.gpsimd.tensor_tensor(o_fac[:, c], o_rstd[:, c], precip[:, i % 4, 0:1], ALU.mult).then_inc(ofac_ready, 1)
        pool.wait_ge(smean_ready, 1)
        nc.gpsimd.tensor_tensor(s_rstd, s_mean, neg_half.to_broadcast([P, 2]), ALU.pow).then_inc(srstd_ready, 1)
        def root2(src, mean, dst, t, src_sem, n, done_sem):
            r, c = rows(t), slice(t, t + 1)
            pool.wait_ge(src_sem, n)
            nc.gpsimd.tensor_scalar(mean[0:r, c], src[0:r, c], 1.0 / D, EPS, ALU.mult, ALU.add).then_inc(pool_step, 1)
            own_step(pool, pool_step)
            nc.gpsimd.tensor_tensor(dst[0:r, c], mean[0:r, c], neg_half[0:r], ALU.pow).then_inc(done_sem, 1)
        for t in range(STEPS):
            root2(ssq2, mean_sq2, rstd2, t, yssq_ready, t + 1, yrstd_ready)
            root2(ssq3, mean_sq3, rstd3, t, ssq_ready, STEPS + t + 1, rstd_ready)
        pool.wait_ge(xt_lo_ready, 2 * STEPS + 2 * STEPS)
        for i in range(2):
            pool.wait_ge(xmid_stored[i], 16 * ((STEPS + 1 - i) // 2))
        nc.gpsimd.memset(y_acc[:], 0.0).then_inc(yacc_zero, 1)
        pool.wait_ge(st_taken, 2)
        pool.wait_ge(cw_taken, 1)

        def ffn_pool(i, first, last):
            if not first:
                pool.wait_ge(tap_ready, 4 * i)
                pool.wait_ge(hs_ready, 4 * i)
                keep_states(i - 1)
            nc.gpsimd.tensor_copy(cwi[:], cw[:, :, :, bass.ds(2 * i, 2)]).then_inc(cwi_ready, 1)
            for half in range(2):
                nc.gpsimd.tensor_copy(hsw[:, half, :, :, 0:2], stT[:, bass.ds(JF * half + 2 * i, 2)]).then_inc(hsp_ready, 1)

        def keep_states(i):
            for half in range(2):
                nc.gpsimd.tensor_copy(stT[:, bass.ds(JF * half + 2 * i, 2)], hsw[:, half, :, :, DS:]).then_inc(cs_kept, 1)
                nc.gpsimd.tensor_copy(cpT[:, bass.ds(JF * half + 2 * i, 2)], cpw[:, half]).then_inc(cs_kept, 1)
            pool.wait_ge(cs_kept, 4 * i + 4)
        iterations(pool, ffn_pool)
        pool.wait_ge(tap_ready, 4 * NIT)
        pool.wait_ge(hs_ready, 4 * NIT)
        keep_states(NIT - 1)
        def final_add(t):
            r = rows(t)
            pool.wait_ge(ynrm_ready, STEPS + t + 1)
            pool.wait_ge(x_loaded[t % 3], 16 * (STEPS // 3) + 16 * (t // 3 + 1))
            nc.gpsimd.tensor_tensor(y_acc[0:r, t, :], y_acc[0:r, t, :], x_back[0:r, t % 3, :], ALU.add).then_inc(fout_ready, 1)
        for t in range(STEPS):
            r = rows(t)
            pool.wait_ge(ssq_ready, 2 * STEPS + t + 1)
            c = slice(t, t + 1)
            nc.gpsimd.tensor_scalar(mean_sq[0:r, c], ssq[0:r, c], 1.0 / D, EPS, ALU.mult, ALU.add).then_inc(pool_step, 1)
            own_step(pool, pool_step)
            nc.gpsimd.tensor_tensor(rstd[0:r, c], mean_sq[0:r, c], neg_half[0:r], ALU.pow).then_inc(rstd_ready, 1)
            if 1 <= t < STEPS - 1:
                final_add(t - 1)

    @block.vector
    def _(dve):
        dve.wait_ge(gain_loaded, 16)

        def bias_tables():
            nc.vector.memset(rel_rep[:], 1.0).then_inc(rep_ready, 1)
            dve.wait_ge(setup_loaded, 16 * 7)
            dve.wait_ge(rep_ready, 1)
            for h in range(H):
                nc.vector.tensor_copy(rel_rep[0:BUCKETS, h, :], rel_sb[:, h:h + 1].to_broadcast([BUCKETS, P])).then_inc(rep_ready, 1)
            nc.vector.tensor_tensor(lam_prod[:], lam_in[:, 0:2, :], lam_in[:, 2:4, :], ALU.mult).then_inc(lam_step, 1)
            nc.vector.tensor_scalar(sub_gain[:], sub_gain[:], 1.0 - LAM_INIT, None, ALU.mult).then_inc(lam_step, 1)
            dve.wait_ge(lam_step, 2)
            dve.wait_ge(const_ready, 3)
            nc.vector.tensor_reduce(lam_sum, lam_prod[:], AX.X, ALU.add).then_inc(lam_step, 1)

        def take_lines():
            for h in range(H):
                dve.wait_ge(line_ready, h + 1)
                nc.vector.tensor_copy(line_out[:, h, :], PS[:, 4 + h, 0:LINE]).then_inc(line_taken, 1)

        def xt_lo(s):
            for h in range(2):
                src = PS[:, (2 * s + h) % 4, :].rearrange("p (k t) -> p k t", k=4)[:, :, 0:rows(s)]
                dve.wait_ge(xt_hi_ready, 2 * s + h + 1)
                nc.vector.tensor_tensor(act_lo[:, 4 * h:4 * h + 4, cols(s)], src,
                                        act_hi[:, 4 * h:4 * h + 4, cols(s)].bitcast(F32),
                                        ALU.subtract).then_inc(xt_lo_ready, 1)
        for s in range(STEPS):
            r = rows(s)
            dve.wait_ge(rstd_ready, s + 1)
            if s >= 2:
                dve.wait_ge(xt_ready, 2 * (s - 1))
            nc.vector.scalar_tensor_tensor(x_nrm[0:r, s % 2, :], x_in[0:r, s % 3, :], rstd[0:r, s:s + 1],
                                           gain[0:r, :], ALU.mult, ALU.mult).then_inc(nrm_ready, 1)
            if s >= 1:
                xt_lo(s - 1)
            if s == 0:
                bias_tables()
                dve_split_w(dve, 0)
            if s == 1:
                take_lines()
            if s == 8:
                dve_split_w(dve, 1)
        xt_lo(STEPS - 1)
        dve.wait_ge(lam_exp_ready, 1)
        nc.vector.tensor_scalar(lam_dif, lam_exp[:, 1:2], LAM_INIT, None, ALU.subtract).then_inc(lam_step, 1)
        dve.wait_ge(lam_step, 4)
        nc.vector.tensor_tensor(neg_lam, lam_dif, lam_exp[:, 0:1], ALU.subtract).then_inc(lam_ready, 1)
        split = 1

        def layer_stats(s):
            r = rows(s)
            dve.wait_ge(act_took, STEPS + s + 1)
            nc.vector.bn_stats(scratch[0:r, 8 * s:8 * s + 6], va[0:r, s, :]).then_inc(dve_step, 1)
            own_step(dve, dve_step)
            nc.vector.bn_aggr(ln_mv[0:r, s, :], scratch[0:r, 8 * s:8 * s + 6]).then_inc(mv_ready, 1)

        def center(s):
            r = rows(s)
            dve.wait_ge(ln_rstd_ready, s + 1)
            nc.vector.tensor_scalar(va[0:r, s, :], va[0:r, s, :], ln_mv[0:r, s, 0:1], ln_rstd[0:r, s:s + 1],
                                    ALU.subtract, ALU.mult).then_inc(vc_ready, 1)

        for n, (kind, g, half, f, c) in enumerate(jobs):
            if g > split - 1 and g + 1 < len(GROUPS) and g + 1 > split:
                split = g + 1
                dve_split_w(dve, split)
                if g == 2:
                    for s in range(STEPS):
                        layer_stats(s)
                        if s >= 1:
                            center(s - 1)
                    center(STEPS - 1)
            if kind in ON_ACT:
                continue
            dve.wait_ge(job_ready, n + 1)
            if kind in ("q", "k"):
                w = KEPT[c].stop - KEPT[c].start
                dst = (qT if kind == "q" else kT)[:, 2 * half + f, KEPT[c]]
                if kind == "q":
                    nc.vector.tensor_scalar(dst, PS[:, bank_of[n], 0:w], DH ** -0.5, None, ALU.mult).then_inc(dve_took, 1)
                else:
                    nc.vector.tensor_copy(dst, PS[:, bank_of[n], 0:w]).then_inc(dve_took, 1)
            elif kind == "gate":
                s, w = c, rows(c)
                b_of = bs[:] if s < STEPS - 1 else bs_smp[:].rearrange("p g b t -> p g (b t)")
                if s == 0:
                    dve.wait_ge(act_took, n_u_done)
                    dve.wait_ge(gate_loaded, 16 * (4 + NB))
                    dve.wait_ge(bs_ready, NB)
                if s >= 2:
                    dve.wait_ge(gate_mul, s - 1)
                ps = PS[:, bank_of[n], :].rearrange("p (g t) -> p g t", g=AG)[:, :, 0:w]
                nc.vector.tensor_tensor(g_sum[:, s % 2, :, 0:w], ps, b_of, ALU.add).then_inc(dve_took, 1)
                dve.wait_ge(dve_took, took[n][1])
                nc.vector.tensor_tensor(uT[:, :, cols(s)], g_sum[:, s % 2, :, 0:w], uT[:, :, cols(s)],
                                        ALU.mult).then_inc(gate_mul, 1)
            else:
                r = rows(c)
                vh = slice(GC * half, GC * half + GC)
                if c == 0 and half == 1:
                    dve.wait_ge(bias_hi_ready, 1)
                    nc.vector.tensor_tensor(bias_lo[:], bias_raw[:], bias_hi[:].bitcast(F32),
                                            ALU.subtract).then_inc(bias_lo_ready, 1)
                if c == 0 and half == 0:
                    dve.wait_ge(job_ready, last_gate + 1)
                    dve.wait_ge(sgu_stored, 16)
                nc.vector.tensor_copy(v_all[0:r, c, vh], PS[0:r, bank_of[n], 0:GC]).then_inc(dve_took, 1)
                if c == STEPS - 1:
                    dve.wait_ge(dve_took, took[n][1])
                    nc.vector.tensor_copy(v_smp[0:NS, vh], v_all[0:NS, c, vh]).then_inc(v_kept, 1)
        def gated_lo(g):
            dve.wait_ge(gate_hi_ready, g + 1)
            nc.vector.tensor_tensor(act_lo[:, 4 + g, 0:NTOK], uT[:, g, :], act_hi[:, 4 + g, 0:NTOK].bitcast(F32),
                                    ALU.subtract).then_inc(gate_lo_ready, 1)

        def row_max(i, m):
            dve.wait_ge(score_ready, 2 * i + m + 1)
            src = PS[:, 2 * m:2 * m + 2, :].rearrange("p a b -> p (a b)")[:, 0:P * (i % QB + 1)]
            nc.vector.tensor_reduce(nmax[:, i % 4, m:m + 1], src, AX.X, ALU.max, negate=True).then_inc(nmax_ready, 1)

        def mix(i):
            w = P * (i % QB + 1)
            dve.wait_ge(prob_ready, 2 * i + 2)
            if i >= 4:
                dve.wait_ge(ofac_ready, i - 3)
            nc.vector.reciprocal(precip[:, i % 4, :], prob_sum[:, i % 4, :]).then_inc(dve_step, 1)
            own_step(dve, dve_step)
            nc.vector.scalar_tensor_tensor(pcoef[:, i % 4:i % 4 + 1], precip[:, i % 4, 1:2], neg_lam,
                                           prob_sum[:, i % 4, 0:1], ALU.mult, ALU.mult).then_inc(dve_step, 1)
            own_step(dve, dve_step)
            nc.vector.scalar_tensor_tensor(prob[:, i % 2, 0, 0:w], prob[:, i % 2, 1, 0:w], pcoef[:, i % 4:i % 4 + 1],
                                           prob[:, i % 2, 0, 0:w], ALU.mult, ALU.add).then_inc(mix_ready, 1)

        def out_norm(i):
            dve.wait_ge(ofac_ready, i + 1)
            if i >= QB:
                dve.wait_ge(ot_ready, (i - QB) // OB + 1)
            nc.vector.scalar_tensor_tensor(o_nrm[:, i % QB, :], PS[:, 6, 0:DV], o_fac[:, i % 4:i % 4 + 1], sub_gain[:],
                                           ALU.mult, ALU.mult).then_inc(onrm_ready, 1)

        def out_lo(g):
            dve.wait_ge(ot_hi_ready, g + 1)
            c0 = NS + P * OB * (g % (QB // OB))
            dst = slice(c0, c0 + P * OB)
            nc.vector.tensor_tensor(act_lo[:, g * OB // QB, dst], PS[:, 7, :], act_hi[:, g * OB // QB, dst].bitcast(F32),
                                    ALU.subtract).then_inc(ot_lo_ready, 1)

        dve.wait_ge(lam_ready, 1)
        for i in range(NSTEP + 4):
            if i < NSTEP:
                row_max(i, 0)
            if 0 <= i - 1 < NSTEP:
                mix(i - 1)
            if i < NSTEP:
                row_max(i, 1)
            if 0 <= i - 2 < NSTEP:
                out_norm(i - 2)
            if 1 <= i <= AG:
                gated_lo(i - 1)
            if i >= OB + 3 and (i - OB - 3) % OB == 0:
                out_lo((i - OB - 3) // OB)
        dve.wait_ge(sel_loaded, 32)
        nc.vector.scalar_tensor_tensor(row_coef, select_sb[:, 65:66], neg_lam, select_sb[:, 64:65], ALU.mult, ALU.add).then_inc(rowcoef_step, 1)
        nc.vector.tensor_scalar(gain_col, gain_col, 1.0 - LAM_INIT, None, ALU.mult).then_inc(rowcoef_step, 1)
        dve.wait_ge(ot_lo_ready, NSTEP // OB)
        nc.vector.memset(qp[:], 0.0).then_inc(qp_zero, 1)
        nc.vector.memset(ones[:], 1.0).then_inc(qp_zero, 1)
        dve.wait_ge(qp_zero, 2)

        def take_keys(n):
            u, p = n // 4, n % 4
            dve.wait_ge(kturn_ready, n + 1)
            if u >= 2:
                dve.wait_ge(sscore_ready, u - 1)
            src = PS[:, 3 + n % 2, :].rearrange("p (h t) -> p h t", h=H)
            nc.vector.tensor_copy(kt[:, u % 2, :, P * p:P * p + P], src).then_inc(kt_ready[0], 1)

        def take_rows(b):
            dve.wait_ge(pv_ready, b + 1)
            if b >= 1:
                dve.wait_ge(osel_ready, b)
            nc.vector.tensor_copy(o_rows[:], PS[0:DS * H, 6, :]).then_inc(orows_ready, 1)

        def q_pad(pr):
            if pr >= 1:
                dve.wait_ge(sscore_ready, 4 * pr)
            for m in range(2):
                d = slice(DH * m, DH * m + DH)
                dst = qp[d, :].rearrange("p (b h c) -> p b h c", b=2, h=H)[:, :, :, DS * m:DS * m + DS]
                src = sq[d, :, 16 * pr:16 * pr + 16].rearrange("p h (b q) -> p b h q", b=2)
                nc.vector.tensor_copy(dst, src).then_inc(qp_ready, 1)

        def smp_softmax(pr):
            c = slice(pr, pr + 1)
            dve.wait_ge(sscore_ready, 4 * pr + 4)
            dve.wait_ge(sbias_loaded, 16 * 32)
            last_page = PS[:, 1, 384:512]
            nc.vector.tensor_tensor(last_page, last_page, smp_bias[:, 0:P], ALU.add)
            own = P + DS * (6 - 2 * pr)
            nc.vector.tensor_tensor(PS[:, 2, 0:NS], PS[:, 2, 0:NS], smp_bias[:, own:own + NS], ALU.add).then_inc(dve_step, 1)
            own_step(dve, dve_step)
            nc.vector.tensor_reduce(smp_max[:, c], PS[:, 0:3, :].rearrange("p a b -> p (a b)")[:, 0:SEQ + NS],
                                    AX.X, ALU.max, negate=True).then_inc(smax_ready, 1)

        def smp_factors(pr):
            c = slice(pr, pr + 1)
            dve.wait_ge(sprob_ready, pr + 1)
            nc.vector.reciprocal(smp_recip[:, c], smp_sum[:, c]).then_inc(dve_step, 1)
            own_step(dve, dve_step)
            dve.wait_ge(rowcoef_step, 2)
            nc.vector.tensor_tensor(smp_coef[:, c], smp_recip[:, c], row_coef, ALU.mult).then_inc(dve_step, 1)
            own_step(dve, dve_step)
            if pr >= 1:
                dve.wait_ge(sat_ready, 2 * pr)
            nc.vector.tensor_scalar(c_mat[:], select_sb[:, 0:NS], smp_coef[:, c], None, ALU.mult).then_inc(cmat_ready, 1)

        dve.wait_ge(sqk_ready, 2)
        for u in range(2 * NB + 1):
            if u < 2 * NB:
                take_keys(4 * u)
                take_keys(4 * u + 2)
            if u % 4 == 3 and u >= 7:
                take_rows(2 * (u // 4 - 1))
            if u % 4 == 0 and u < 2 * NB:
                q_pad(u // 4)
            if u % 4 == 0 and u >= 4:
                smp_softmax(u // 4 - 1)
            if u % 4 == 1 and u >= 5:
                smp_factors(u // 4 - 1)
                if u >= 9:
                    take_rows(2 * (u // 4 - 1) - 1)
        smp_factors(NB // 2 - 1)
        take_rows(NB - 3)
        take_rows(NB - 2)
        take_rows(NB - 1)
        dve.wait_ge(ssum_ready, 1)
        dve.wait_ge(sat_ready, NB)
        nc.vector.tensor_scalar(s_mean, PS[:, 6, 0:2], 1.0 / DV, SUBLN_EPS, ALU.mult, ALU.add).then_inc(smean_ready, 1)
        dve.wait_ge(srstd_ready, 1)
        for j in range(2):
            nc.vector.tensor_scalar(s_rs[:, j, :], ident[:], s_rstd[:, j:j + 1], None, ALU.mult).then_inc(sdiag_ready, 1)
        dve.wait_ge(sfac_ready, 1)
        nc.vector.tensor_copy(s_fac[:], PS[:, 5, 0:H * NS]).then_inc(dve_step, 1)
        own_step(dve, dve_step)
        nc.vector.scalar_tensor_tensor(s_out[:], PS[:, 7, 0:H * NS], gain_col, s_fac[:], ALU.mult, ALU.mult).then_inc(sout_ready, 1)
        dve.wait_ge(sout_hi_ready, 1)
        nc.vector.tensor_tensor(act_lo[:, 0:H, 0:NS], s_out[:].rearrange("p (h c) -> p h c", h=H),
                                act_hi[:, 0:H, 0:NS].bitcast(F32), ALU.subtract).then_inc(sout_lo_ready, 1)
        for k in range(KD):
            dve.wait_ge(wo_hi_ready, k + 1)
            nc.vector.tensor_tensor(wo_lo[:, k, :], wo_raw[:, k, :], wo_hi[:, k, :].bitcast(F32), ALU.subtract).then_inc(wo_lo_ready, 1)
        dve.wait_ge(gain_loaded, 48)

        def x2_lo(t):
            for h in range(2):
                dve.wait_ge(xt_hi_ready, 2 * STEPS + 2 * t + h + 1)
                src = PS[:, TURN_BANK[(2 * t + h) % 4], :].rearrange("p (k t) -> p k t", k=4)[:, :, 0:rows(t)]
                dst = cols(t)
                nc.vector.tensor_tensor(act_lo[:, 4 * h:4 * h + 4, dst], src, act_hi[:, 4 * h:4 * h + 4, dst].bitcast(F32),
                                        ALU.subtract).then_inc(xt_lo_ready, 1)
        def wu_lo_first(half):
            dve.wait_ge(wu_hi_ready, half + 1)
            nc.vector.tensor_tensor(wu_lo[:, half], wu_raw[:, half], wu_hi[:, half].bitcast(F32), ALU.subtract).then_inc(wu_lo_ready, 1)

        for t in range(STEPS):
            r, j = rows(t), Y_BANK[t % 2]
            if t == STEPS - 1:
                x2_lo(t - 2)
                x2_lo(t - 1)
                wu_lo_first(0)
            dve.wait_ge(yrstd_ready, t + 1)
            nc.vector.scalar_tensor_tensor(y_nrm[0:r, t % 2, :], PS[0:r, j:j + 2, :].rearrange("p a b -> p (a b)"),
                                           rstd2[0:r, t:t + 1], gain[0:r, :], ALU.mult, ALU.mult).then_inc(ynrm_ready, 1)
            dve.wait_ge(ynrm_ready, t + 1)
            dve.wait_ge(xres_loaded[t % 2], 16 * (t // 2 + 1))
            if t >= 2:
                dve.wait_ge(xmid_stored[t % 2], 16 * (t // 2))
                dve.wait_ge(nrm_ready, STEPS + t - 1)
            nc.vector.tensor_tensor(x_mid[0:r, t % 2, :], y_nrm[0:r, t % 2, :], x_res[0:r, t % 2, :], ALU.add).then_inc(xmid_ready, 1)
            dve.wait_ge(rstd_ready, STEPS + t + 1)
            if t >= 2:
                dve.wait_ge(xt_ready, 2 * STEPS + 2 * (t - 1))
            nc.vector.scalar_tensor_tensor(x2_nrm[0:r, t % 2, :], x_mid[0:r, t % 2, :], rstd3[0:r, t:t + 1], gain2[0:r, :],
                                           ALU.mult, ALU.mult).then_inc(nrm_ready, 1)
            if 2 <= t < STEPS - 1:
                x2_lo(t - 2)
        wu_lo_first(1)
        x2_lo(STEPS - 1)
        dve.wait_ge(cw_turned, 1)
        for b in range(2):
            dve.wait_ge(st_turned, b + 1)
            n = min(32, 2 * JF - 32 * b)
            nc.vector.tensor_copy(stT[:, 32 * b:32 * b + n], PS[:, 6 + b, 0:16 * n].rearrange("p (j b r) -> p j b r", b=NB, r=2)).then_inc(st_taken, 1)
        dve.wait_ge(cw_turned, 1)
        nc.vector.tensor_copy(cw[:], PS[:, 7, CW_AT:CW_AT + 8 * JF].rearrange("p (w a j) -> p w a j", w=4, a=2)).then_inc(cw_taken, 1)

        def add_down(base, n, bank=None):
            t, half = n // 2, n % 2
            bank = 6 + half if bank is None else bank
            r = rows(t)
            dve.wait_ge(down_ready, base + n + 1)
            dst = y_acc[0:r, t, 512 * half:512 * half + 512]
            nc.vector.tensor_tensor(dst, dst, PS[0:r, bank, :], ALU.add).then_inc(ybank_free, 1)

        def ffn_dve(i, first, last):
            adds = iter(range(0 if first else YJ))

            def some_adds(t, most):
                if t == 1:
                    for _, n in zip(range(most), adds):
                        add_down(YJ * i - YJ, n)

            def split(t, ahead):
                dve.wait_ge(wu_hi_ready, 4 * i + t + ahead + 1)
                q = (t + ahead) % 2
                nc.vector.tensor_tensor(wu_lo[:, q], wu_raw[:, q], wu_hi[:, q].bitcast(F32), ALU.subtract).then_inc(wu_lo_ready, 1)

            for t in range(4):
                e, half = t // 2, t % 2
                u = 4 * i + t
                h = h_sb[half]
                w1, w0 = cwi[:, 1, half, e:e + 1], cwi[:, 0, half, e:e + 1]
                some_adds(t, 2)
                dve.wait_ge(conv_ready, u + 1)
                nc.vector.scalar_tensor_tensor(conv[:, half, NS + 1:], h[:, NS:NTOK - 1], w1, conv[:, half, NS + 1:],
                                               ALU.mult, ALU.add).then_inc(tap1_ready, 1)
                some_adds(t, 2)
                nc.vector.tensor_copy(cpw[:, half, e, :], h[:, NTOK - 2:NTOK]).then_inc(tap1_ready, 1)
                dve.wait_ge(hs_ready, u + 1)
                smp_c = conv[:, half, 0:NS].rearrange("p (b q) -> p b q", b=NB)
                nc.vector.scalar_tensor_tensor(smp_c, hsw[:, half, e, :, 1:DS + 1], w1, smp_c, ALU.mult, ALU.add).then_inc(tap1_ready, 1)
                dve.wait_ge(tap1_ready, 3 * u + 3)
                nc.vector.scalar_tensor_tensor(smp_c, hsw[:, half, e, :, 0:DS], w0, smp_c, ALU.mult, ALU.add).then_inc(stap_ready, 1)
                some_adds(t, 1)
                dve.wait_ge(stap_ready, u + 1)
                nc.vector.scalar_tensor_tensor(conv[:, half, NS + 2:], h[:, NS:NTOK - 2], w0, conv[:, half, NS + 2:],
                                               ALU.mult, ALU.add).then_inc(tap_ready, 1)
                some_adds(t, 2)
                if not (last and t >= 2):
                    split(t, 2)
                some_adds(t, 2)
                if half == 1:
                    dve.wait_ge(silu_ready, 2 * i + e + 1)
                    dve.wait_ge(tap_ready, u + 1)
                    nc.vector.tensor_tensor(conv[:, 1, :], conv[:, 0, :], conv[:, 1, :], ALU.mult).then_inc(prod_ready, 1)
                    some_adds(t, YJ)
                    dve.wait_ge(g_hi_ready, 2 * i + e + 1)
                    nc.vector.tensor_tensor(g_lo[:, e, :], conv[:, 1, :], g_hi[:, e, :].bitcast(F32), ALU.subtract).then_inc(g_lo_ready, 1)
                    if t == 1:
                        for k in range(2):
                            dve.wait_ge(wd_hi_ready, 2 * i + k + 1)
                            nc.vector.tensor_tensor(wd_lo[:, k, :], wd_raw[:, k, :], wd_hi[:, k, :].bitcast(F32), ALU.subtract).then_inc(wd_lo_ready, 1)
        dve.wait_ge(xt_lo_ready, 2 * STEPS + 2 * STEPS)
        dve.wait_ge(st_taken, 2)
        dve.wait_ge(cw_taken, 1)
        for bank in (6, 7):
            nc.vector.memset(PS[:, bank, :], 0.0).then_inc(ybank_free, 1)
        dve.wait_ge(yacc_zero, 1)
        iterations(dve, ffn_dve)
        dve.wait_ge(gain_loaded, 64)

        def final_norm(t):
            r = rows(t)
            dve.wait_ge(rstd_ready, 2 * STEPS + t + 1)
            nc.vector.scalar_tensor_tensor(y_acc[0:r, t, :], y_acc[0:r, t, :], rstd[0:r, t:t + 1], gain[0:r, :],
                                           ALU.mult, ALU.mult).then_inc(ynrm_ready, 1)

        def final_add(t):
            r = rows(t)
            dve.wait_ge(ynrm_ready, STEPS + t + 1)
            dve.wait_ge(x_loaded[t % 3], 16 * (STEPS // 3) + 16 * (t // 3 + 1))
            if t == STEPS - 2:
                dve.wait_ge(fout_ready, t)
            nc.vector.tensor_tensor(y_acc[0:r, t, :], y_acc[0:r, t, :], x_back[0:r, t % 3, :], ALU.add).then_inc(fout_ready, 1)

        def take_states(q):
            dve.wait_ge(st_turned, 2 + 7)
            if q < 6:
                n = min(8, 2 * JF - 8 * q)
                nc.vector.tensor_copy(st_nat[0:16 * n, q, :], PS[0:16 * n, q // 4, P * (q % 4):P * (q % 4) + P]).then_inc(st_taken, 1)
            else:
                nc.vector.tensor_copy(cw_nat[:, 0:2, :], PS[0:2 * JF, 1, 2 * P:4 * P].rearrange("p (r c) -> p r c", r=2)).then_inc(st_taken, 1)
        for t in range(STEPS + 2):
            if t < STEPS:
                for n in (2 * t, 2 * t + 1):
                    add_down(YJ * (NIT - 1), n, LAST_BANK[n % 6])
            if t >= 2:
                final_norm(t - 2)
            if t >= STEPS:
                final_add(t - 2)
            if 1 <= t < 8:
                take_states(t - 1)

    @block.tensor
    def _(pe):
        pe.wait_ge(const_ready, 4)

        def bias_lines():
            for h in range(H):
                pe.wait_ge(rep_ready, h + 2)
                nc.tensor.matmul(PS[:, 4 + h, 0:LINE], rel_rep[:, h, :], lines_sb[:], start=True, stop=True).then_inc(line_ready, 1)

        def project(n):
            kind, g, half, f, c = jobs[n]
            if n == first_of[g]:
                pe.wait_ge(w_lo_ready, 2 * g + 2)
            before = [m for m in range(n) if bank_of[m] == bank_of[n]]
            if before:
                pe.wait_ge(*took[before[-1]])
            if kind == "krow":
                if c == 0:
                    pe.wait_ge(dve_took, last_k_took)
                for h in range(H):
                    mm = nc.tensor.transpose(PS[0:rows(c), bank_of[n], P * h:P * h + P], kT[:, h, cols(c)], ident[:])
            elif kind == "gate":
                if c == 0:
                    pe.wait_ge(ws_cut, 2)
                pe.wait_ge(vn_ready, c + 1)
                r, w = rows(c), wsT if c < STEPS - 1 else wbT
                for a in range(AG):
                    mm = nc.tensor.matmul(PS[:, bank_of[n], P * a:P * a + r], va[0:r, c, P * a:P * a + P], w[:, a, :],
                                          start=True, stop=True)
            else:
                if kind in ("va", "v"):
                    out, stat, mov = PS[:, bank_of[n], 0:GC], wide(c), slice(0, GC)
                    pairs = [(a[:, k, stat], w[:, g % 2, k, :]) for k in range(KD)
                             for a, w in ((act_hi, w_hi), (act_hi, w_lo), (act_lo, w_hi))]
                else:
                    out = PS[:, bank_of[n], 0:CW]
                    pairs = [(w[:, g % 2, k, P * f:P * f + P], a[:, k, CHUNKS[c]]) for k in range(KD)
                             for w, a in ((w_hi, act_hi), (w_hi, act_lo), (w_lo, act_hi))]
                for i, (lhs, rhs) in enumerate(pairs):
                    mm = nc.tensor.matmul(out, lhs, rhs, start=(i == 0), stop=(i == len(pairs) - 1))
            mm.then_inc(job_ready, 1)

        pe.wait_ge(pad_zero, 2)
        for s in range(STEPS):
            pe.wait_ge(nrm_ready, s + 1)
            for h in range(2):
                j = 2 * s + h
                if j >= 4:
                    pe.wait_ge(xt_lo_ready, j - 3)
                for k in range(4):
                    mm = nc.tensor.transpose(PS[:, j % 4, P * k:P * k + rows(s)],
                                             x_nrm[0:rows(s), s % 2, P * (4 * h + k):P * (4 * h + k + 1)],
                                             ident[0:rows(s), 0:rows(s)])
                mm.then_inc(xt_ready, 1)
            if s == 0:
                bias_lines()
            if s == 1:
                pe.wait_ge(line_taken, H)
            if s >= 1:
                pe.wait_ge(xt_lo_ready, 2 * s)
                project(s - 1)
        pe.wait_ge(gate_loaded, 16 * (4 + NB))
        pe.wait_ge(xt_lo_ready, 2 * STEPS - 2)
        for i, (w, n) in enumerate(((ws_nat, P), (ws_bd, NS))):
            for g in range(AG):
                mm = nc.tensor.transpose(PS[0:n, 2 + i, n * g:n * g + n], w[:, g, :], ident[0:n, 0:n])
            mm.then_inc(ws_turned, 1)
        pe.wait_ge(xt_lo_ready, 2 * STEPS)
        project(STEPS - 1)
        for n in range(STEPS, len(jobs)):
            if n == STEPS + 1:
                pe.wait_ge(ws_taken, 2)
            project(n)
        for q in took[-8:]:
            pe.wait_ge(*q)
        def scores(i, m):
            h, n = i // QB, i % QB + 1
            w = P * n
            if i == 0:
                pe.wait_ge(bias_lo_ready, 1)
            if i >= 1:
                pe.wait_ge(prob_ready, 2 * (i - 1) + m + 1)
            d = slice(DH * m, DH * m + DH)
            qs = slice(NS + P * (n - 1), NS + P * n)
            for c in range(0, w, 512):
                e = min(c + 512, w)
                out = PS[:, 2 * m + c // 512, :]
                b0 = max(c, w - 2 * P)
                mm = nc.tensor.matmul(out[:, 0:e - c], qT[d, h, qs], kT[d, h, NS + c:NS + e], start=True, stop=b0 >= e)
                if b0 < e:
                    t = slice(b0 - (w - 2 * P), e - (w - 2 * P))
                    for j, b in enumerate((bias_hi, bias_lo)):
                        mm = nc.tensor.matmul(out[:, b0 - c:e - c], identr[:], b[:, h, t], start=False, stop=(j == 1))
            mm.then_inc(score_ready, 1)

        def turn(i):
            n = i % QB + 1
            pe.wait_ge(mix_ready, i + 1)
            for t in range(turns(i)):
                at_turn = turns_before(i) + t
                if at_turn >= 2:
                    pe.wait_ge(at_taken, at_turn - 1)
                for k in range(4 * t, min(4 * t + 4, n)):
                    mm = nc.tensor.transpose(PS[:, 4 + at_turn % 2, P * (k % 4):P * (k % 4) + P],
                                             prob[:, i % 2, 0, P * k:P * k + P], ident[:])
                mm.then_inc(turn_ready, 1)

        def weigh(i):
            h, n = i // QB, i % QB + 1
            pe.wait_ge(at_taken, turns_before(i + 1))
            if i >= 1:
                pe.wait_ge(onrm_ready, i)
            for k in range(n):
                mm = nc.tensor.matmul(PS[:, 6, 0:DV], at_sb[:, i % 2, P * k:P * k + P], v_all[:, k, DV * h:DV * h + DV],
                                      start=(k == 0), stop=(k == n - 1))
            mm.then_inc(o_ready, 1)

        def turn_out(g):
            pe.wait_ge(onrm_ready, OB * (g + 1))
            if g >= 1:
                pe.wait_ge(ot_lo_ready, g)
            for j in range(OB):
                mm = nc.tensor.transpose(PS[:, 7, P * j:P * j + P], o_nrm[:, (OB * g + j) % QB, :], ident[:])
            mm.then_inc(ot_ready, 1)

        for i in range(NSTEP + 4):
            if i < NSTEP:
                scores(i, 0)
            if 0 <= i - 2 < NSTEP:
                weigh(i - 2)
            if i < NSTEP:
                scores(i, 1)
            if 0 <= i - 1 < NSTEP:
                turn(i - 1)
            if i >= OB + 3 and (i - OB - 3) % OB == 0:
                turn_out((i - OB - 3) // OB)
        def turn_keys(u, pages):
            if u >= 2 * NB:
                return
            pe.wait_ge(kp_loaded[u % 2], 64 * (u // 2 + 1))
            for p in pages:
                n = 4 * u + p
                if n >= 2:
                    pe.wait_ge(kt_ready[n % 2], n // 2)
                for h in range(H):
                    mm = nc.tensor.transpose(PS[:, 3 + n % 2, P * h:P * h + P], kpage[:, n % 8, P * h:P * h + P], ident[:])
                mm.then_inc(kturn_ready, 1)

        def smp_scores(u):
            pr, b2, c = u // 4, u // 2 % 2, u % 2
            for i in range(2):
                pe.wait_ge(kt_ready[i], 2 * u + 2)
            pe.wait_ge(qp_ready, 2 * pr + 2)
            if pr >= 1:
                pe.wait_ge(sprob_ready, pr)
            for h in range(H):
                n = 4 * b2 + h
                w = slice(P * n, P * n + P)
                mm = nc.tensor.matmul(PS[:, c, :], qp[:, w], kt[:, u % 2, h, :], start=(n == 0), stop=(n == 7))
                if c == 1:
                    mm = nc.tensor.matmul(PS[:, 2, 0:NS], qp[:, w], sk[:, h, :], start=(n == 0), stop=(n == 7))
            mm.then_inc(sscore_ready, 1)

        def smp_turn(pr):
            pe.wait_ge(cmat_ready, pr + 1)
            if pr >= 1:
                pe.wait_ge(sat_taken, 2 * pr)
            for p in range(NPAGE):
                mm = nc.tensor.matmul(PS[:, 5, NS * p:NS * p + NS], s_prob[:, P * p:P * p + P], c_mat[:], start=True, stop=True)
            mm.then_inc(sat_ready, 1)

        def smp_turn_own(pr):
            pe.wait_ge(sat_taken, 2 * pr + 1)
            nc.tensor.matmul(PS[0:NS, 5, 0:NS], s_prob[:, SEQ:SEQ + NS], c_mat[:], start=True, stop=True).then_inc(sat_ready, 1)

        def smp_weigh(b, first_page, last_page):
            pr, q = b // 2, slice(DS * H * (b % 2), DS * H * (b % 2) + DS * H)
            out = PS[0:DS * H, 6, :]
            if first_page == 0:
                pe.wait_ge(sat_taken, 2 * pr + 1)
                pe.wait_ge(vp_loaded[b % VR], 16 * NPAGE * (b // VR + 1))
                if b >= 1:
                    pe.wait_ge(orows_ready, b)
            for p in range(first_page, last_page):
                nc.tensor.matmul(out, s_at[:, p, q], vpage[b % VR][:, p, :], start=(p == 0), stop=False)
            if last_page == NPAGE:
                pe.wait_ge(sat_taken, 2 * pr + 2)
                nc.tensor.matmul(out, s_own[:, q], v_smp[0:NS, :], start=False, stop=True).then_inc(pv_ready, 1)

        def smp_select(b):
            pe.wait_ge(orows_ready, b + 1)
            for h in range(H):
                mm = nc.tensor.matmul(PS[:, 7, NS * h + DS * b:NS * h + DS * b + DS], o_rows[:, P * h:P * h + P],
                                      ident[0:DS * H, DS * h:DS * h + DS], start=True, stop=True)
            mm.then_inc(osel_ready, 1)

        pe.wait_ge(sqk_ready, 2)
        pe.wait_ge(v_kept, 2)
        pe.wait_ge(at_taken, turns_before(NSTEP))
        pe.wait_ge(ot_lo_ready, NSTEP // OB)
        turn_keys(0, range(4))
        for u in range(2 * NB):
            pr, step = u // 4 - 1, u % 4
            turn_keys(u + 1, (0, 1))
            if step == 0 and pr >= 1:
                smp_weigh(2 * pr - 1, NPAGE // 2, NPAGE)
            if step == 1 and pr >= 0:
                smp_turn(pr)
            smp_scores(u)
            turn_keys(u + 1, (2, 3))
            if pr < 0:
                continue
            if step == 1:
                if pr >= 1:
                    smp_select(2 * pr - 1)
                smp_weigh(2 * pr, 0, NPAGE // 2)
            if step == 2:
                smp_turn_own(pr)
                smp_weigh(2 * pr, NPAGE // 2, NPAGE)
            if step == 3:
                smp_select(2 * pr)
                smp_weigh(2 * pr + 1, 0, NPAGE // 2)
        smp_weigh(NB - 3, NPAGE // 2, NPAGE)
        smp_turn(NB // 2 - 1)
        smp_select(NB - 3)
        smp_turn_own(NB // 2 - 1)
        smp_weigh(NB - 2, 0, NPAGE)
        smp_select(NB - 2)
        smp_weigh(NB - 1, 0, NPAGE)
        smp_select(NB - 1)
        pe.wait_ge(ssq_s_ready, 1)
        pe.wait_ge(qp_zero, 2)
        for j in range(2):
            mm = nc.tensor.matmul(PS[:, 6, j:j + 1], s_sq[:, P * j:P * j + P], ones[:, 0:1], start=True, stop=True)
        mm.then_inc(ssum_ready, 1)
        pe.wait_ge(sdiag_ready, 2)
        for j in range(2):
            mm = nc.tensor.matmul(PS[:, 5, P * j:P * j + P], ones[:], s_rs[:, j, :], start=True, stop=True)
        mm.then_inc(sfac_ready, 1)
        def turn_x2(t):
            pe.wait_ge(nrm_ready, STEPS + t + 1)
            for h in range(2):
                j = 2 * t + h
                if j >= 4:
                    pe.wait_ge(xt_lo_ready, 2 * STEPS + j - 3)
                for k in range(4):
                    mm = nc.tensor.transpose(PS[:, TURN_BANK[j % 4], P * k:P * k + rows(t)],
                                             x2_nrm[0:rows(t), t % 2, P * (4 * h + k):P * (4 * h + k + 1)],
                                             ident[0:rows(t), 0:rows(t)])
                mm.then_inc(xt_ready, 1)

        pe.wait_ge(sout_lo_ready, 1)
        for t in range(STEPS):
            if t >= 2:
                pe.wait_ge(ynrm_ready, t - 1)
            if t == STEPS - 1:
                pe.wait_ge(xt_lo_ready, 2 * STEPS + 2)
            for half in range(2):
                parts = [(a, w, k) for k in range(KD) for a, w in ((act_hi, wo_hi), (act_hi, wo_lo), (act_lo, wo_hi))]
                for j, (a, w, k) in enumerate(parts):
                    if t == 0 and half == 0 and j % 3 == 0:
                        pe.wait_ge(wo_lo_ready, k + 1)
                    mm = nc.tensor.matmul(PS[:, Y_BANK[t % 2] + half, :], a[:, k, wide(t)], w[:, k, 512 * half:512 * half + 512],
                                          start=(j == 0), stop=(j == len(parts) - 1))
            mm.then_inc(y_ready, 1)
            if t >= 2:
                turn_x2(t - 2)
        turn_x2(STEPS - 2)
        pe.wait_ge(ynrm_ready, STEPS - 1)
        pe.wait_ge(st_loaded, 16 * 6)
        for q in range(6):
            n = min(8, 2 * JF - 8 * q)
            mm = nc.tensor.transpose(PS[:, 6 + q // 4, P * (q % 4):P * (q % 4) + 16 * n], st_nat[0:16 * n, q, :], ident[0:16 * n, 0:16 * n])
            if q in (3, 5):
                mm.then_inc(st_turned, 1)
        pe.wait_ge(cw_loaded, 16 * 4)
        for w in range(4):
            mm = nc.tensor.transpose(PS[:, 7, CW_AT + 2 * JF * w:CW_AT + 2 * JF * (w + 1)], cw_nat[:, w, :], ident[0:2 * JF, 0:2 * JF])
        mm.then_inc(cw_turned, 1)

        def up_chunk(half, c):
            parts = [(a, b, k) for k in range(KD) for a, b in ((wu_hi, act_hi), (wu_hi, act_lo), (wu_lo, act_hi))]
            for j, (a, b, k) in enumerate(parts):
                mm = nc.tensor.matmul(PS[:, 3 * half + c, 0:CW], a[:, half, k, :], b[:, k, CHUNKS[c]],
                                      start=(j == 0), stop=(j == len(parts) - 1))
            return mm

        pe.wait_ge(wu_lo_ready, 1)
        pe.wait_ge(xt_lo_ready, 2 * STEPS + 2 * (STEPS - 1))
        for c in (1, 2):
            up_chunk(0, c)
        turn_x2(STEPS - 1)
        pe.wait_ge(xt_lo_ready, 2 * STEPS + 2 * STEPS)

        def ffn_pe(i, first, last):
            for t in range(4):
                half = t % 2
                if t == 2 and not first:
                    down_share(i - 1)
                if first and t == 1:
                    pe.wait_ge(st_taken, 2)
                    pe.wait_ge(cw_taken, 1)
                pe.wait_ge(wu_lo_ready, 4 * i + t + 1)
                if not first or t >= 2:
                    pe.wait_ge(h_ready, 4 * i + t - 1)
                    pe.wait_ge(hs_ready, 4 * i + t - 1)
                for c in range(1 if first and t == 0 else 3):
                    mm = up_chunk(half, c)
                mm.then_inc(up_ready, 1)

        def down_share(i):
            pe.wait_ge(g_lo_ready, 2 * i + 2)
            pe.wait_ge(wd_lo_ready, 2 * i + 2)
            for n in range(YJ):
                t, half = n // 2, n % 2
                pe.wait_ge(ybank_free, YJ * i + n + 1)
                parts = [(g, w, e) for e in range(2) for g, w in ((g_hi, wd_hi), (g_hi, wd_lo), (g_lo, wd_hi))]
                for j, (g, w, e) in enumerate(parts):
                    mm = nc.tensor.matmul(PS[:, 6 + half, :], g[:, e, wide(t)], w[:, e, 512 * half:512 * half + 512],
                                          start=(j == 0), stop=(j == len(parts) - 1))
                mm.then_inc(down_ready, 1)
        iterations(pe, ffn_pe)
        def last_products(n, tiles):
            t, half = n // 2, n % 2
            for e in tiles:
                for j, (g, w) in enumerate(((g_hi, wd_hi), (g_hi, wd_lo), (g_lo, wd_hi))):
                    mm = nc.tensor.matmul(PS[:, LAST_BANK[n % 6], :], g[:, e, wide(t)], w[:, e, 512 * half:512 * half + 512],
                                          start=(e == 0 and j == 0), stop=(e == 1 and j == 2))
            return mm

        pe.wait_ge(wd_lo_ready, 2 * NIT)
        pe.wait_ge(g_lo_ready, 2 * NIT - 1)
        pe.wait_ge(ybank_free, YJ * (NIT - 1) + 2)
        for n in range(6):
            if n == 2:
                pe.wait_ge(h_ready, 4 * NIT)
                pe.wait_ge(hs_ready, 4 * NIT)
            last_products(n, (0,))
        pe.wait_ge(cs_kept, 4 * NIT)
        for q in range(6):
            n = min(8, 2 * JF - 8 * q)
            nc.tensor.transpose(PS[0:16 * n, q // 4, P * (q % 4):P * (q % 4) + P],
                                stT[:, 8 * q:8 * q + n].rearrange("p j b r -> p (j b r)"), ident[:]).then_inc(st_turned, 1)
        for r in range(2):
            mm = nc.tensor.transpose(PS[0:2 * JF, 1, P * (r + 2):P * (r + 3)], cpT[:, :, r], ident[:])
        mm.then_inc(st_turned, 1)
        pe.wait_ge(g_lo_ready, 2 * NIT)
        for n in range(YJ):
            if n >= 6:
                pe.wait_ge(ybank_free, YJ * (NIT - 1) + 2 + n - 5)
            last_products(n, (1,) if n < 6 else (0, 1)).then_inc(down_ready, 1)


_INS = ["x_prompt", "x_sample", "cache_k", "cache_v", "state_conv", "page_table", "rel_bias",
        "norm_mix_pre", "norm_mix_post", "norm_ffn_pre", "norm_ffn_post", "w_in",
        "lambda_q1", "lambda_k1", "lambda_q2", "lambda_k2", "subln_gain", "sgu_ln_gain", "sgu_ln_bias",
        "w_spatial", "b_spatial", "w_out", "w_up", "conv_w", "conv_b", "w_down"]
_OUTS = [(1, SEQ, D), (NB, DS, D), (1, 1, SEQ, H, 2 * DH), (1, 1, SEQ, H, DV), (1, 1, 2, 2 * FF),
         (1, NB, DS, H, 2 * DH), (1, NB, DS, H, DV), (1, NB, 2, 2 * FF), (1, NB, DS, AW)]


def kernel(**inputs):
    import numpy as _np
    import concourse.bacc as _bacc
    from concourse import mybir as _mybir
    from concourse.bass_utils import run_bass_kernel_spmd as _run

    nc = _bacc.Bacc("TRN2", target_bir_lowering=False, num_devices=1)
    arrays, args = {}, []
    given = {name: _np.ascontiguousarray(inputs[name]) for name in _INS}
    given["lines"] = bucket_lines()
    given["select"] = sample_select()
    for name, a in given.items():
        arrays[f"in_{name}_dram"] = a
        args.append(nc.dram_tensor(f"in_{name}_dram", a.shape, _mybir.dt.from_np(a.dtype), kind="ExternalInput").ap())
    for i, shape in enumerate(_OUTS):
        args.append(nc.dram_tensor(f"out_{i}_dram", shape, _mybir.dt.float32, kind="ExternalOutput").ap())
    build(nc, *args)
    r = _run(nc, [arrays], core_ids=[0])
    return tuple(r.results[0][f"out_{i}_dram"] for i in range(len(_OUTS)))
```
